# Optimizing a Trainium2 kernel written in Bass

```python
import jax, jax.numpy as jnp
from jax import lax
import numpy as np

D_MODEL = 1024
BATCH = 1
SEQ = 256
DEPTH = 2

EXPAND = 2
WIDTH = EXPAND * D_MODEL
HEAD_DIM = 128
A_HEADS = WIDTH // HEAD_DIM
B_HEADS = WIDTH // HEAD_DIM
N_A = DEPTH // 2
N_B = DEPTH - N_A
CHUNK = 64
Q_BLOCK = 128
EPS = 1e-6


def _rms(x, g):
    xf = x.astype(jnp.float32)
    y = xf * lax.rsqrt(jnp.mean(xf * xf, axis=-1, keepdims=True) + EPS)
    return (y * g.astype(jnp.float32)).astype(x.dtype)

def _ada(c, w, b):
    return jax.nn.silu(c) @ w + b

def _hgrn2(h, w_in, lb, onorm_g, w_out):
    bsz, s, _ = h.shape
    f32 = jnp.float32
    q, fz, i, g = jnp.split(h @ w_in, 4, axis=-1)
    fz = fz.astype(f32)
    logf = jnp.log(lb + (1.0 - lb) * jax.nn.sigmoid(fz))
    k = (1.0 - lb) * jax.nn.sigmoid(-fz)

    def hc(t):
        return t.reshape(bsz, s // CHUNK, CHUNK, A_HEADS, HEAD_DIM).transpose(0, 3, 1, 2, 4)

    q, k, v, logf = hc(q.astype(f32)), hc(k), hc(i.astype(f32)), hc(logf)
    b = jnp.cumsum(logf, axis=3)
    b_last = b[:, :, :, -1:, :]
    q_dec = q * jnp.exp(b)
    k_in = k * jnp.exp(-b)
    k_st = k * jnp.exp(b_last - b)
    causal = jnp.tril(jnp.ones((CHUNK, CHUNK), dtype=bool))
    att = jnp.where(causal, jnp.einsum('bhnck,bhnsk->bhncs', q_dec, k_in), 0.0)
    o_intra = jnp.einsum('bhncs,bhnsv->bhncv', att, v)

    def step(state, xs):
        qd, ks, vv, dl = xs
        o = jnp.einsum('bhck,bhkv->bhcv', qd, state)
        state = dl[..., None] * state + jnp.einsum('bhck,bhcv->bhkv', ks, vv)
        return state, o

    xs = (jnp.moveaxis(q_dec, 2, 0), jnp.moveaxis(k_st, 2, 0), jnp.moveaxis(v, 2, 0),
          jnp.moveaxis(jnp.exp(b_last[:, :, :, 0, :]), 2, 0))
    s0 = jnp.zeros((bsz, A_HEADS, HEAD_DIM, HEAD_DIM), f32)
    _, o_inter = lax.scan(step, s0, xs)
    o = o_intra + jnp.moveaxis(o_inter, 0, 2)
    o = o.transpose(0, 2, 3, 1, 4).reshape(bsz, s, A_HEADS, HEAD_DIM)
    o = _rms(o, onorm_g.reshape(A_HEADS, HEAD_DIM)).reshape(bsz, s, WIDTH).astype(h.dtype)
    return (o * jax.nn.silu(g)) @ w_out

def _shared_kv(x, c, kv_mod_w, kv_mod_b, kv_norm_g, kv_w, kv_fb, k_norm_g):
    bsz, s, _ = x.shape
    shift, scale = jnp.split(_ada(c, kv_mod_w, kv_mod_b), 2, axis=-1)
    h = _rms(x, kv_norm_g) * (1.0 + scale[:, None]) + shift[:, None]
    proj = h @ kv_w
    k = proj[..., :WIDTH].reshape(bsz, s, B_HEADS, HEAD_DIM)
    v = proj[..., WIDTH:2 * WIDTH].reshape(bsz, s, B_HEADS, HEAD_DIM)
    fl = proj[..., 2 * WIDTH:] + kv_fb
    k = _rms(k, k_norm_g).transpose(0, 2, 1, 3)
    v = v.transpose(0, 2, 1, 3)
    F = jnp.cumsum(jax.nn.log_sigmoid(fl.astype(jnp.float32)), axis=1).transpose(0, 2, 1)
    return k, v, F

def _fox(h, w_in, q_norm_g, w_out, k, v, F):
    bsz, s, _ = h.shape
    q, g = jnp.split(h @ w_in, 2, axis=-1)
    q = _rms(q.reshape(bsz, s, B_HEADS, HEAD_DIM), q_norm_g).transpose(0, 2, 1, 3)
    scale = HEAD_DIM ** -0.5
    outs = []
    for blk in range(s // Q_BLOCK):
        lo, hi = blk * Q_BLOCK, (blk + 1) * Q_BLOCK
        logits = (jnp.einsum('bhqd,bhkd->bhqk', q[:, :, lo:hi], k[:, :, :hi]).astype(jnp.float32) * scale
                  + (F[:, :, lo:hi, None] - F[:, :, None, :hi]))
        mask = (lo + jnp.arange(Q_BLOCK))[:, None] >= jnp.arange(hi)[None, :]
        p = jax.nn.softmax(jnp.where(mask, logits, -jnp.inf), axis=-1)
        outs.append(jnp.einsum('bhqk,bhkd->bhqd', p.astype(v.dtype), v[:, :, :hi]))
    o = jnp.concatenate(outs, axis=2).transpose(0, 2, 1, 3).reshape(bsz, s, WIDTH)
    return (o * jax.nn.silu(g)) @ w_out

def first_inputs(seed: int = 0) -> dict:
    key = jax.random.key(seed)
    ks = jax.random.split(key, 20)
    n = jax.random.normal
    D, W = D_MODEL, WIDTH
    return {
        "x": n(ks[0], (BATCH, SEQ, D), jnp.float32),
        "c": n(ks[1], (BATCH, D), jnp.float32),
        "mod_w": n(ks[2], (DEPTH, D, 3 * D), jnp.float32) * (0.3 * D ** -0.5),
        "mod_b": n(ks[3], (DEPTH, 3 * D), jnp.float32) * 0.02,
        "norm_g": 1.0 + 0.02 * n(ks[4], (DEPTH, D), jnp.float32),
        "a_w_in": n(ks[5], (N_A, D, 4 * W), jnp.float32) * D ** -0.5,
        "a_lb_logits": 0.5 * n(ks[6], (N_A + 1, W), jnp.float32),
        "a_onorm_g": 1.0 + 0.02 * n(ks[7], (N_A, W), jnp.float32),
        "a_w_out": n(ks[8], (N_A, W, D), jnp.float32) * W ** -0.5,
        "kv_mod_w": n(ks[9], (D, 2 * D), jnp.float32) * (0.3 * D ** -0.5),
        "kv_mod_b": n(ks[10], (2 * D,), jnp.float32) * 0.02,
        "kv_norm_g": 1.0 + 0.02 * n(ks[11], (D,), jnp.float32),
        "kv_w": n(ks[12], (D, 2 * W + B_HEADS), jnp.float32) * D ** -0.5,
        "kv_fb": 2.0 + 0.5 * n(ks[13], (B_HEADS,), jnp.float32),
        "k_norm_g": 1.0 + 0.02 * n(ks[14], (HEAD_DIM,), jnp.float32),
        "b_w_in": n(ks[15], (N_B, D, 2 * W), jnp.float32) * D ** -0.5,
        "b_q_norm_g": 1.0 + 0.02 * n(ks[16], (N_B, HEAD_DIM), jnp.float32),
        "b_w_out": n(ks[17], (N_B, W, D), jnp.float32) * W ** -0.5,
    }

def first_block(x, c, mod_w, mod_b, norm_g, a_w_in, a_lb_logits, a_onorm_g, a_w_out,
              kv_mod_w, kv_mod_b, kv_norm_g, kv_w, kv_fb, k_norm_g,
              b_w_in, b_q_norm_g, b_w_out):
    lb_all = jnp.cumsum(jax.nn.softmax(a_lb_logits.astype(jnp.float32), axis=0), axis=0)
    kv = None
    for l in range(DEPTH):
        shift, scale, gate = jnp.split(_ada(c, mod_w[l], mod_b[l]), 3, axis=-1)
        h = _rms(x, norm_g[l]) * (1.0 + scale[:, None]) + shift[:, None]
        if l < N_A:
            y = _hgrn2(h, a_w_in[l], lb_all[l], a_onorm_g[l], a_w_out[l])
        else:
            if l == N_A:
                kv = _shared_kv(x, c, kv_mod_w, kv_mod_b, kv_norm_g, kv_w, kv_fb, k_norm_g)
            j = l - N_A
            y = _fox(h, b_w_in[j], b_q_norm_g[j], b_w_out[j], *kv)
        x = x + gate[:, None] * y
    return x


HEAD_DIM_2 = 64
A_HEADS_2 = 8
A_KV_HEADS = 2
A_WIDTH = A_HEADS_2 * HEAD_DIM_2
A_KV_WIDTH = A_KV_HEADS * HEAD_DIM_2
IDX_HEADS = 4
IDX_DIM = 64
IDX_SCALE = (IDX_HEADS * IDX_DIM) ** -0.5
TOPK_MAX = 256
POOL_WINDOWS = (2, 4, 8, 16)
POOL_GROUP = 128
POOL_WIDTH = POOL_GROUP * len(POOL_WINDOWS)
EVEN_MIX_WIDTH = A_WIDTH + POOL_WIDTH
EVEN_IN_COLS = A_WIDTH + 2 * A_KV_WIDTH + IDX_HEADS * IDX_DIM + IDX_DIM + IDX_HEADS + POOL_WIDTH
C_HEADS = 16
C_WIDTH = C_HEADS * HEAD_DIM_2
D_FF = -(-8 * D_MODEL // (3 * 256)) * 256
N_EVEN = (DEPTH + 1) // 2
N_ODD = DEPTH // 2


def rms_norm(x, g):
    x32 = x.astype(jnp.float32)
    y = x32 * lax.rsqrt(jnp.mean(x32 * x32, axis=-1, keepdims=True) + EPS)
    return (y * g.astype(jnp.float32)).astype(x.dtype)

def to_blocks(a):
    b, t = a.shape[:2]
    a = a.reshape((b, t // Q_BLOCK, Q_BLOCK) + a.shape[2:])
    return jnp.moveaxis(a, 1, 0)

def from_blocks(a):
    a = jnp.moveaxis(a, 0, 1)
    return a.reshape((a.shape[0], a.shape[1] * a.shape[2]) + a.shape[3:])

def dsa_attention(q, k, v, q_idx, k_idx, w_idx):
    b, t = q.shape[:2]
    n_sel = min(TOPK_MAX, t // 4)
    rep = A_HEADS_2 // A_KV_HEADS
    key_pos = jnp.arange(t)
    gather = jax.vmap(lambda kv, ids: kv[ids])

    def block(args):
        qb, qib, wb, start = args
        q_pos = start + jnp.arange(Q_BLOCK)
        causal = key_pos[None, :] <= q_pos[:, None]
        rel = jax.nn.relu(jnp.einsum('bthd,bsd->bths', qib, k_idx).astype(jnp.float32))
        score = jnp.einsum('bths,bth->bts', rel, wb.astype(jnp.float32)) * IDX_SCALE
        score = jnp.where(causal[None], score, -jnp.inf)
        _, sel = lax.top_k(score, n_sel)
        k_sel = gather(k, sel)
        v_sel = gather(v, sel)
        valid = sel <= q_pos[None, :, None]
        qg = qb.reshape(b, Q_BLOCK, A_KV_HEADS, rep, HEAD_DIM_2)
        logits = jnp.einsum('btgrd,btkgd->btgrk', qg, k_sel).astype(jnp.float32) * (HEAD_DIM_2 ** -0.5)
        logits = jnp.where(valid[:, :, None, None, :], logits, -jnp.inf)
        p = jax.nn.softmax(logits, axis=-1).astype(v.dtype)
        o = jnp.einsum('btgrk,btkgd->btgrd', p, v_sel)
        return o.reshape(b, Q_BLOCK, A_WIDTH)

    starts = jnp.arange(t // Q_BLOCK) * Q_BLOCK
    out = lax.map(block, (to_blocks(q), to_blocks(q_idx), to_blocks(w_idx), starts))
    return from_blocks(out)

def multiscale_pool(u, pool_w, pool_scale):
    b, t, _ = u.shape
    groups = u.astype(jnp.float32).reshape(b, t, len(POOL_WINDOWS), POOL_GROUP)
    c0 = jnp.pad(jnp.cumsum(groups, axis=1), ((0, 0), (1, 0), (0, 0), (0, 0)))
    pos = jnp.arange(1, t + 1, dtype=jnp.float32)
    outs = []
    for g, w in enumerate(POOL_WINDOWS):
        cg = c0[:, :, g]
        hi = cg[:, 1:]
        lo = jnp.pad(cg[:, :t + 1 - w], ((0, 0), (w - 1, 0), (0, 0)))
        count = jnp.minimum(pos, float(w))[None, :, None]
        outs.append((hi - lo) / count - groups[:, :, g])
    mixed = jnp.stack(outs, axis=2)
    y = jnp.einsum('btgc,gcd->btgd', mixed, pool_w.astype(jnp.float32))
    return (y.reshape(b, t, POOL_WIDTH) * pool_scale.astype(jnp.float32)).astype(u.dtype)

def stick_breaking_attention(q, k, v):
    b, t = q.shape[:2]
    key_pos = jnp.arange(t)

    def block(args):
        qb, start = args
        q_pos = start + jnp.arange(Q_BLOCK)
        strict = key_pos[None, :] < q_pos[:, None]
        z = jnp.einsum('bthd,bshd->bhts', qb, k).astype(jnp.float32) * (HEAD_DIM_2 ** -0.5)
        brk = jnp.where(strict, jax.nn.softplus(z), 0.0)
        later = jnp.pad(brk[..., 1:], ((0, 0), (0, 0), (0, 0), (0, 1)))
        remain = lax.cumsum(later, axis=3, reverse=True)
        log_a = jax.nn.log_sigmoid(z) - remain
        a = jnp.where(strict, jnp.exp(log_a), 0.0).astype(v.dtype)
        o = jnp.einsum('bhts,bshd->bthd', a, v)
        return o.reshape(b, Q_BLOCK, C_WIDTH)

    starts = jnp.arange(t // Q_BLOCK) * Q_BLOCK
    out = lax.map(block, (to_blocks(q), starts))
    return from_blocks(out)

def even_mixer(h, w_in, w_out, q_g, k_g, pool_w, pool_scale):
    b, t, _ = h.shape
    proj = h @ w_in
    sizes = [A_WIDTH, A_KV_WIDTH, A_KV_WIDTH, IDX_HEADS * IDX_DIM, IDX_DIM, IDX_HEADS]
    offsets = np.cumsum(sizes).tolist()
    q, k, v, qi, ki, wi, u = jnp.split(proj, offsets, axis=-1)
    q = rms_norm(q.reshape(b, t, A_HEADS_2, HEAD_DIM_2), q_g)
    k = rms_norm(k.reshape(b, t, A_KV_HEADS, HEAD_DIM_2), k_g)
    v = v.reshape(b, t, A_KV_HEADS, HEAD_DIM_2)
    attn = dsa_attention(q, k, v, qi.reshape(b, t, IDX_HEADS, IDX_DIM), ki, wi)
    pooled = multiscale_pool(u, pool_w, pool_scale)
    return jnp.concatenate([attn, pooled], axis=-1) @ w_out

def odd_mixer(h, w_qkv, w_out):
    b, t, _ = h.shape
    q, k, v = jnp.split((h @ w_qkv).reshape(b, t, 3, C_HEADS, HEAD_DIM_2), 3, axis=2)
    o = stick_breaking_attention(q[:, :, 0], k[:, :, 0], v[:, :, 0])
    return o @ w_out

def swiglu(h, w1, w3, w2):
    return (jax.nn.silu(h @ w1) * (h @ w3)) @ w2

def second_inputs(seed: int = 0) -> dict:
    key = jax.random.key(seed)
    ks = jax.random.split(key, 16)
    f32 = jnp.float32

    def dense(k, shape):
        return jax.random.normal(k, shape, f32) * (shape[-2] ** -0.5)

    def gain(k, shape, s):
        return 1.0 + s * jax.random.normal(k, shape, f32)

    return {
        'x': jax.random.normal(ks[0], (BATCH, SEQ, D_MODEL), f32),
        'norm_mix_g': gain(ks[1], (DEPTH, D_MODEL), 0.05),
        'norm_ffn_g': gain(ks[2], (DEPTH, D_MODEL), 0.05),
        'ev_w_in': dense(ks[3], (N_EVEN, D_MODEL, EVEN_IN_COLS)),
        'ev_w_out': dense(ks[4], (N_EVEN, EVEN_MIX_WIDTH, D_MODEL)),
        'ev_q_norm_g': gain(ks[5], (N_EVEN, HEAD_DIM_2), 0.05),
        'ev_k_norm_g': gain(ks[6], (N_EVEN, HEAD_DIM_2), 0.05),
        'ev_pool_w': dense(ks[7], (N_EVEN, len(POOL_WINDOWS), POOL_GROUP, POOL_GROUP)),
        'ev_pool_scale': gain(ks[8], (N_EVEN, POOL_WIDTH), 0.1),
        'od_w_qkv': dense(ks[9], (N_ODD, D_MODEL, 3 * C_WIDTH)),
        'od_w_out': dense(ks[10], (N_ODD, C_WIDTH, D_MODEL)),
        'ffn_w1': dense(ks[11], (DEPTH, D_MODEL, D_FF)),
        'ffn_w3': dense(ks[12], (DEPTH, D_MODEL, D_FF)),
        'ffn_w2': dense(ks[13], (DEPTH, D_FF, D_MODEL)),
    }

def second_block(x, norm_mix_g, norm_ffn_g, ev_w_in, ev_w_out, ev_q_norm_g, ev_k_norm_g,
              ev_pool_w, ev_pool_scale, od_w_qkv, od_w_out, ffn_w1, ffn_w3, ffn_w2):
    for layer in range(DEPTH):
        i = layer // 2
        h = rms_norm(x, norm_mix_g[layer])
        if layer % 2 == 0:
            x = x + even_mixer(h, ev_w_in[i], ev_w_out[i], ev_q_norm_g[i], ev_k_norm_g[i],
                               ev_pool_w[i], ev_pool_scale[i])
        else:
            x = x + odd_mixer(h, od_w_qkv[i], od_w_out[i])
        h = rms_norm(x, norm_ffn_g[layer])
        x = x + swiglu(h, ffn_w1[layer], ffn_w3[layer], ffn_w2[layer])
    return x


def setup_inputs(seed=0):
    out = dict(first_inputs(seed))
    for name, value in second_inputs(seed + 1).items():
        if name != "x":
            out[name + "_2"] = value
    return out


def reference(
    x, c, mod_w, mod_b, norm_g, a_w_in, a_lb_logits, a_onorm_g, a_w_out, kv_mod_w, kv_mod_b,
    kv_norm_g, kv_w, kv_fb, k_norm_g, b_w_in, b_q_norm_g, b_w_out, norm_mix_g_2, norm_ffn_g_2,
    ev_w_in_2, ev_w_out_2, ev_q_norm_g_2, ev_k_norm_g_2, ev_pool_w_2, ev_pool_scale_2,
    od_w_qkv_2, od_w_out_2, ffn_w1_2, ffn_w3_2, ffn_w2_2,
):
    x = first_block(
        x, c, mod_w, mod_b, norm_g, a_w_in, a_lb_logits, a_onorm_g, a_w_out, kv_mod_w, kv_mod_b,
        kv_norm_g, kv_w, kv_fb, k_norm_g, b_w_in, b_q_norm_g, b_w_out,
    )
    return second_block(
        x, norm_mix_g_2, norm_ffn_g_2, ev_w_in_2, ev_w_out_2, ev_q_norm_g_2, ev_k_norm_g_2,
        ev_pool_w_2, ev_pool_scale_2, od_w_qkv_2, od_w_out_2, ffn_w1_2, ffn_w3_2, ffn_w2_2,
    )


_drawn_inputs = setup_inputs


def setup_inputs(seed=0):
    import zlib

    import numpy as np

    out = dict(_drawn_inputs(seed))
    spreads = {}
    factors = {'norm_g': 4.352,
     'a_onorm_g': 6.526,
     'kv_mod_b': 7.15,
     'kv_norm_g': 8.0,
     'kv_fb': 3.01,
     'k_norm_g': 8.0,
     'b_q_norm_g': 8.0,
     'ev_q_norm_g_2': 5.831,
     'ev_k_norm_g_2': 8.0,
     'norm_ffn_g_2': 5.614,
     'ev_pool_scale_2': 5.528}
    for name, (base, spread) in spreads.items():
        noise = np.random.default_rng([zlib.crc32(name.encode()), seed]).standard_normal(out[name].shape)
        drawn = base * np.exp(spread * noise) if base else spread * noise
        out[name] = __import__('jax').numpy.asarray(drawn.astype(out[name].dtype))
    for name, factor in factors.items():
        out[name] = (out[name] * factor).astype(out[name].dtype)
    return out
```

```python
from contextlib import ExitStack

import numpy as np

import concourse.bass as bass
from concourse import mybir
from concourse.alu_op_type import AluOpType as ALU

ACT = mybir.ActivationFunctionType
F32 = mybir.dt.float32
I32 = mybir.dt.int32
X = mybir.AxisListType.X

P = 128
D = 1024
T = 256
NT = T // P
KD = D // P
W = 2048
HA = W // P
CHUNK = 64
NC = T // CHUNK
HALF = 512
FF = 2816
FC = FF // P
HD2 = 64
HE = 8
HIDX = 4
HO = 16
EV_COLS = 1604
TOPK = min(256, T // 4)
EPS = 1e-6
FAR = -1e30
LOW = -3e38
NSLOT = 4
SLOT = 4096
S3 = P + T
Q0, Q1 = slice(0, P), slice(P, S3)

VEC_A = [("c", 8), ("norm_g", 16), ("mod_b", 48), ("kv_norm_g", 8), ("kv_mod_b", 16),
         ("norm_mix_g_2", 16), ("norm_ffn_g_2", 16)]
VEC_B = [("a_lb_logits", 32), ("a_onorm_g", 16), ("ev_pool_scale_2", 4), ("k_norm_g", 1), ("b_q_norm_g", 1)]


def weight_tiles():
    tiles = [("mod", m) for m in range(4)]
    for n in range(16):
        tiles.append(("a_in", n))
        if 2 <= n < 12:
            tiles.append(("mod", n + 2))
    tiles += [("a_out", n) for n in range(4)]
    tiles += [("kv", n) for n in range(8)] + [("forget", 0)]
    for n in range(8):
        tiles.append(("b_in", n))
        if n < 2:
            tiles.append(("mod", 14 + n))
    tiles += [("b_out", n) for n in range(4)]
    tiles += [("ev_kvi", 0), ("ev_small", 0), ("ev_q", 0), ("ev_u", 0), ("pool_w", 0)]
    tiles += [("ev_out", n) for n in range(2)]

    def ffn(layer):
        order = [("up", layer, 0), ("up", layer, 1), ("up", layer, 2), ("down", layer, 0)]
        for i in range(1, 5):
            order += [("up", layer, 2 * i + 1), ("up", layer, 2 * i + 2), ("down", layer, i)]
        return order + [("down", layer, 5)]

    tiles += ffn(0)
    tiles += [("od_in", n) for n in range(6)] + [("od_out", n) for n in range(2)]
    tiles += ffn(1)
    return tiles


def units():
    out = []

    def add(stage, engines):
        out.extend((stage, e) for e in engines)

    add("norm0", "avvv")
    add("a_f", "a" * 8)
    add("a_i", "a" * 8)
    add("a_q", "v" * 8)
    add("a_g", "a" * 8)
    add("norm1", "avvv")
    add("k", "v" * 8)
    add("v", "a" * 8)
    add("forget", "v")
    add("q", "v" * 8)
    add("g", "a" * 8)
    add("norm2", "avvv")
    add("ev_i", "aaa")
    add("ev_k", "v")
    add("ev_q", "vv")
    add("ev_u", "aa")
    add("ev_pool", "vv")
    add("norm3", "avvv")
    add("up0", "v" * FC)
    add("norm4", "avvv")
    add("od_q", "aaaa")
    add("od_k", "vvvv")
    add("od_v", "avav")
    add("norm5", "avvv")
    add("up1", "v" * FC)
    return out


def build(nc, a, const, mask, out):
    TILES = weight_tiles()
    AT = {t: n for n, t in enumerate(TILES)}
    UNITS = units()
    FIRST = {}
    for n, (s, _) in enumerate(UNITS):
        FIRST.setdefault(s, n)

    with ExitStack() as ctx:
        def sb(name, shape, dt=F32):
            return ctx.enter_context(nc.sbuf_tensor(name, shape, dt))

        def sem(name):
            return ctx.enter_context(nc.semaphore(name))

        slots = sb("slots", [P, NSLOT, SLOT])
        big = sb("big", [P, 6, SLOT])
        x = sb("x", [P, NT, D])
        hT = sb("hT", [P, KD, T])
        gate = sb("gate", [P, D])
        acc = sb("acc", [P, 2, HALF])
        cst = sb("cst", [P, const.shape[1]])
        att_mask = sb("att_mask", [P, 2, P], I32)
        cols = sb("cols", [P, 256])
        small = sb("small", [P, 256])
        work = sb("work", [P, 3328])

        ident, ones, ones64 = cst[:, 0:128], cst[:, 128:256], cst[:, 256:384]
        neg_after, neg_ones = cst[:, 384:512], cst[:, 512:640]
        causal = cst[:, 640:1024]
        chunk_go = cst[:, 1024:1280]
        inv_count = cst[:, 1280:1344].rearrange("p (g t) -> p g t", g=4)

        def grid(n, heads=HA):
            return big[:, n, 0:heads * T].rearrange("p (h t) -> p h t", h=heads)

        xn = big[:, 5, 0:NT * D].rearrange("p (t n) -> p t n", t=NT)
        hkT = big[:, 5, NT * D:].rearrange("p (k t) -> p k t", k=KD)

        at = 0
        col = {}
        for vecs, base in ((VEC_A, 0), (VEC_B, 128)):
            at = base
            for name, n in vecs:
                col[name] = cols[:, at:at + n]
                at += n
        ev_gain = cols[:, at:at + 2]

        silu_c = small[:, 0:8]
        one_m_lb, lb = small[:, 8:24], small[:, 24:40]
        lb_tmp = small[:, 40:56]
        scale0, shift0 = small[:, 56:64], small[:, 64:72]
        scale1, shift1 = small[:, 72:80], small[:, 80:88]
        scale_kv, shift_kv = small[:, 88:96], small[:, 96:104]
        ssum, rstd = small[:, 104:106], small[:, 106:108]
        q_gain = small[:, 108:109]
        ev_q_gain = small[:, 109:110]
        eps_t = small[:, 110:111]
        row_max, row_neg = small[:, 112:116], small[:, 116:120]
        row_sum, row_inv = small[:, 120:124], small[:, 124:128]
        dl = small[:, 128:192].rearrange("p (h n) -> p h n", h=HA)
        w_idx = small[:, 192:200]
        top8 = small[:, 200:208]
        cnt, rest = small[:, 208:209], small[:, 209:210]
        mod_tmp = small[:, 210:214]
        forget_b = small[0:HA, 214:215]

        ps = ctx.enter_context(nc.psum_tensor("ps", [P, 8, HALF], F32))

        def unit_bank(u):
            return ps[:, u % 4, :]

        def y_bank(t, n):
            return ps[:, 4 + 2 * t + n, :]

        loaded = [sem(f"slot{s}_loaded") for s in range(NSLOT)]
        pe_used, mod_summed = sem("tile_used_by_pe"), sem("mod_summed")
        consts_in, rows_in, x_in, gate_b_in, out_stored = (sem(n) for n in (
            "consts_in", "rows_in", "x_in", "gate_bias_in", "out_stored"))
        fb_in = sem("forget_bias_in")
        rows_turned, cols_ready = sem("rows_turned"), sem("cols_ready")
        silu_c_ready = sem("silu_c_ready")
        unit_ready = sem("unit_ready")
        unit_free = {"a": sem("unit_read_by_act"), "v": sem("unit_read_by_dve")}
        mod_cols, mod_read = sem("mod_cols_ready"), sem("mod_cols_read")
        x_done, sq_done, rstd_done, xn_done = sem("x_done"), sem("x_squares_done"), sem("x_rstd_done"), sem("xn_done")
        y_ready = sem("y_ready")
        act_chain, dve_chain, pool_chain = sem("act_step"), sem("dve_step"), sem("pool_step")

        def before(engine, u):
            return sum(1 for _, e in UNITS[:u + 1] if e == engine)

        def wait_read(eng, stage, i):
            u = FIRST[stage] + i
            eng.wait_ge(unit_free[UNITS[u][1]], before(UNITS[u][1], u))

        last_use = {AT[("mod", m)]: (mod_summed, m + 1) for m in range(16)}

        def dmas_of(n):
            return 2 if TILES[n][0] == "up" else 1

        def wait_loaded(eng, n):
            eng.wait_ge(loaded[n % NSLOT], 16 * sum(dmas_of(i) for i in range(n % NSLOT, n + 1, NSLOT)))

        def slot(n):
            return slots[:, n % NSLOT, :]

        chain = {"act": 0, "dve": 0, "pool": 0}

        def then(eng_name, eng, ins):
            s = {"act": act_chain, "dve": dve_chain, "pool": pool_chain}[eng_name]
            chain[eng_name] += 1
            ins.then_inc(s, 1)
            eng.wait_ge(s, chain[eng_name])

        S = {}

        def st(name):
            if name not in S:
                S[name] = sem(name)
            return S[name]

        for name in ("gate_sig_in sig_ready ln_ready scan_ready exp_ready spread_ready spread_exp kin_ready "
                     "kst_turned kst_copied att_ready att_masked state_ready state_saved o_ready "
                     "osq_ready ossq_ready orstd_ready o_used ot_ready "
                     "hsq_ready hssq_ready hrstd_ready "
                     "f_min f_ln nf_ready "
                     "fx_logits fx_max fx_exp fx_prob fx_turned fx_tcopied fx_o fx_out "
                     "ev_rel ev_relu ev_score_used "
                     "ev_mixed "
                     "ds_logits ds_max ds_exp ds_prob ds_turned ds_tcopied ds_o ds_out "
                     "up_silu sb_z sb_ln sb_soft sb_masked sb_log sb_exp sb_sel sb_o sb_out"
                     ).split():
            st(name)

        a_in_at = [2048 + 512 * n for n in range(4)] + [4096 + 512 * n for n in range(4)] + \
                  [512 * n for n in range(4)] + [6144 + 512 * n for n in range(4)]

        def col_tile(w, c0, n):
            return w.rearrange("(k p) n -> p k n", p=P)[:, :, c0:c0 + n]

        def row_tile(w, k0, nk):
            return w[k0 * P:(k0 + nk) * P, :].rearrange("(k p) n -> p k n", p=P)

        def tile_dmas(n):
            kind, i = TILES[n][0], TILES[n][-1]
            s = slot(n)
            wide = s.rearrange("p (k n) -> p k n", k=KD)
            rows = s.rearrange("p (k n) -> p k n", k=4)
            if kind == "mod":
                w, j = (a["mod_w"][0], i) if i < 6 else (a["mod_w"][1], i - 6) if i < 10 else \
                       (a["kv_mod_w"], i - 10) if i < 14 else (a["mod_w"][1], i - 10)
                return [(wide, col_tile(w, HALF * j, HALF))]
            if kind == "a_in":
                return [(wide, col_tile(a["a_w_in"][0], a_in_at[i], HALF))]
            if kind == "kv":
                return [(wide, col_tile(a["kv_w"], HALF * i, HALF))]
            if kind == "forget":
                return [(s[:, 0:KD * HA].rearrange("p (k n) -> p k n", k=KD), col_tile(a["kv_w"], 2 * W, HA))]
            if kind == "b_in":
                return [(wide, col_tile(a["b_w_in"][0], HALF * i, HALF))]
            if kind == "ev_kvi":
                return [(wide, col_tile(a["ev_w_in_2"][0], 512, HALF))]
            if kind == "ev_small":
                return [(s[:, 0:KD * 68].rearrange("p (k n) -> p k n", k=KD), col_tile(a["ev_w_in_2"][0], 1024, 68))]
            if kind == "ev_q":
                return [(wide, col_tile(a["ev_w_in_2"][0], 0, HALF))]
            if kind == "ev_u":
                return [(wide, col_tile(a["ev_w_in_2"][0], 1092, HALF))]
            if kind == "pool_w":
                return [(s[:, 0:4 * P].rearrange("p (g d) -> p g d", g=4), a["ev_pool_w_2"][0].rearrange("g c d -> c g d"))]
            if kind == "od_in":
                return [(wide, col_tile(a["od_w_qkv_2"][0], HALF * i, HALF))]
            if kind in ("a_out", "b_out", "ev_out", "od_out"):
                w = {"a_out": "a_w_out", "b_out": "b_w_out", "ev_out": "ev_w_out_2", "od_out": "od_w_out_2"}[kind]
                return [(rows, row_tile(a[w][0], 4 * i, 4))]
            layer = TILES[n][1]
            if kind == "up":
                return [(s[:, 2048 * j:2048 * (j + 1)].rearrange("p (k n) -> p k n", k=KD),
                         col_tile(a[w][layer], T * i, T)) for j, w in enumerate(("ffn_w1_2", "ffn_w3_2"))]
            nk = min(4, FC - 4 * i)
            return [(rows[:, 0:nk, :], row_tile(a["ffn_w2_2"][layer], 4 * i, nk))]

        fz_b, k_in0, q_dec, k_in, k_st, v_tok = (grid(n) for n in (0, 1, 2, 3, 4, 5))
        silu_g, oT = grid(0), grid(1)
        v_rows = big[:, 5, :].rearrange("p (t n) -> p t n", t=NT)
        kst_sb = work[:, 0:512].rearrange("p (b t k) -> p b t k", b=2, t=2)
        att_sb = work[:, 512:1024].rearrange("p (b t c) -> p b t c", b=2, t=2)
        state = work[:, 1024:1792].rearrange("p (b n v) -> p b n v", b=2, n=3)
        o_sq = work[:, 1792:2304].rearrange("p (b t) -> p b t", b=2)
        o_r = work[:, 2304:2816].rearrange("p (b t) -> p b t", b=2)
        o_tmp = work[:, 2816:3072]

        kN, v2_rows, qN, silu_g2, oT2 = grid(0), big[:, 1, :].rearrange("p (t n) -> p t n", t=NT), grid(2), grid(3), grid(4)
        h_sq = work[:, 0:1024].rearrange("p (b n) -> p b n", b=2)
        h_r = work[:, 1024:2048].rearrange("p (b n) -> p b n", b=2)
        f_a, f_b = work[0:HA, 2048:2048 + T], work[0:HA, 2304:2304 + T]
        neg_f = work[0:HA, 3072:3072 + T]
        lg = work[:, 0:2 * S3].rearrange("p (b n) -> p b n", b=2)
        prob = work[:, 768:768 + 3 * S3].rearrange("p (b n) -> p b n", b=3)
        probT = work[:, 1920:1920 + 2 * S3].rearrange("p (b n) -> p b n", b=2)

        evq = big[:, 0, 0:1024].rearrange("p (c t) -> p c t", c=4)
        evk = big[:, 0, 1024:1536].rearrange("p (g t) -> p g t", g=2)
        evqi = big[:, 0, 1536:2048].rearrange("p (c t) -> p c t", c=2)
        evki = big[:, 0, 2048:2304]
        evv = big[:, 0, 2304:2560].rearrange("p (t d) -> p t d", t=2)
        PAD = 16
        u_pad = big[:, 1, 0:4 * (PAD + T)].rearrange("p (g t) -> p g t", g=4)
        run_a = big[:, 1, 1088:1088 + PAD + T]
        run_b = big[:, 1, 1360:1360 + PAD + T]
        mixed = big[:, 1, 1632:1632 + 4 * T].rearrange("p (g t) -> p g t", g=4)
        ev_oT = big[:, 2, 0:8 * T].rearrange("p (c t) -> p c t", c=8)
        score = big[:, 3, 0:S3]
        relu_s = big[:, 3, 384:384 + 2 * S3].rearrange("p (b n) -> p b n", b=2)
        cut = big[:, 3, 1152:1152 + T]
        sel_gt = big[:, 3, 1536:1536 + T]
        sel_eq = big[:, 3, 1792:1792 + T]
        sel_pre = big[:, 3, 2048:2048 + T]
        ev_bias_t = big[:, 3, 2304:2304 + S3]

        gated = big[:, 3, 0:8 * T].rearrange("p (c t) -> p c t", c=8)
        silu_a = work[:, 0:512].rearrange("p (b t) -> p b t", b=2)

        odq, odk = grid(0, 8), big[:, 0, 2048:4096].rearrange("p (h t) -> p h t", h=8)
        odv = big[:, 1, 0:2048].rearrange("p (t n) -> p t n", t=NT)
        od_oT = big[:, 2, 0:8 * T].rearrange("p (c t) -> p c t", c=8)

        def sb_ln_t(i):
            return work[:, (i % 2) * S3:(i % 2) * S3 + S3]

        def sb_brk(i):
            return work[:, (2 + i % 3) * S3:(2 + i % 3) * S3 + S3]

        def sb_prob(i):
            return work[:, (5 + i % 3) * S3:(5 + i % 3) * S3 + S3]

        block = ctx.enter_context(nc.Block())

        vec_rows = [work[:, 0:P], work[:, P:2 * P]]

        @block.gpsimd
        def _(pool):
            pool.memset(vec_rows[1], 0.0).then_inc(pool_chain, 1)
            pool.wait_ge(pool_chain, 1)
            for vecs, rows in ((VEC_A, vec_rows[0]), (VEC_B, vec_rows[1])):
                r = 0
                for name, n in vecs:
                    src = a[name]
                    if len(src.shape) == 2:
                        src = src.rearrange("a b -> (a b)")
                    pool.dma_start(rows[r:r + n, :], src.rearrange("(r c) -> r c", c=P)).then_inc(rows_in, 16)
                    r += n
            for i, name in enumerate(("ev_q_norm_g_2", "ev_k_norm_g_2")):
                for half in range(2):
                    pool.dma_start(vec_rows[1][r + i:r + i + 1, HD2 * half:HD2 * (half + 1)], a[name]).then_inc(rows_in, 16)
            pool.dma_start(x[:, :, :], a["x"][0].rearrange("(t p) n -> p t n", p=P)).then_inc(x_in, 16)
            pool.dma_start(forget_b, a["kv_fb"].rearrange("(h a) -> h a", a=1)).then_inc(fb_in, 16)
            pool.dma_start(gate[:, :], a["mod_b"][0:1, 2 * D:3 * D].to_broadcast([P, D])).then_inc(gate_b_in, 16)
            pool.wait_ge(x_done, 4)
            pool.dma_start(gate[:, :], a["mod_b"][1:2, 2 * D:3 * D].to_broadcast([P, D])).then_inc(gate_b_in, 16)

            for i in range(HO + 1):
                if i < HO:
                    pool.wait_ge(st("sb_soft"), i + 1)
                    part = sb_brk(i).rearrange("p (b t) -> p b t", b=3)[:, 0:3:2, :]
                    pool.affine_select(out=part, in_=part, compare_op=ALU.is_gt, fill=0.0, base=0,
                                       pattern=[[0, 2], [1, P]], channel_multiplier=-1).then_inc(st("sb_masked"), 1)
                if i >= 1:
                    pool.wait_ge(st("sb_exp"), i)
                    part = sb_prob(i - 1).rearrange("p (b t) -> p b t", b=3)[:, 0:3:2, :]
                    pool.affine_select(out=part, in_=part, compare_op=ALU.is_gt, fill=0.0, base=0,
                                       pattern=[[0, 2], [1, P]], channel_multiplier=-1).then_inc(st("sb_sel"), 1)

        NVEC = len(VEC_A) + len(VEC_B) + 4

        downs = {}

        @block.tensor
        def _(pe):
            unit = [0]

            def open_unit(stage):
                u = unit[0]
                assert UNITS[u][0] == stage, (u, UNITS[u], stage)
                if u >= 4:
                    pe.wait_ge(unit_free[UNITS[u - 4][1]], before(UNITS[u - 4][1], u - 4))
                unit[0] += 1
                return unit_bank(u)

            def feature_major(dst, w, h):
                for k in range(KD):
                    ins = pe.matmul(dst, w(k), h[:, k, :], start=(k == 0), stop=(k == KD - 1))
                return ins

            def token_major(dst, h, t, w):
                for k in range(KD):
                    ins = pe.matmul(dst, h[:, k, t * P:(t + 1) * P], w(k), start=(k == 0), stop=(k == KD - 1))
                return ins

            def project_features(stage, n, h):
                wait_loaded(pe, n)
                w = slot(n).rearrange("p (k n) -> p k n", k=KD)
                for pair in range(2):
                    bank = open_unit(stage)
                    for j in range(2):
                        c = (2 * pair + j) * P
                        ins = feature_major(bank[:, j * T:(j + 1) * T], lambda k: w[:, k, c:c + P], h)
                    ins.then_inc(unit_ready, 1)
                    if pair == 1:
                        used(n)
                    yield pair

            tiles_used, y_count = [0], [0]

            def used(n, ins=None):
                if ins is None:
                    last_use[n] = (unit_ready, unit[0])
                else:
                    tiles_used[0] += 1
                    ins.then_inc(pe_used, 1)
                    last_use[n] = (pe_used, tiles_used[0])

            def project_tokens(stage, n, h):
                wait_loaded(pe, n)
                w = slot(n).rearrange("p (k n) -> p k n", k=KD)
                for t in range(NT):
                    bank = open_unit(stage)
                    token_major(bank, h, t, lambda k: w[:, k, :]).then_inc(unit_ready, 1)
                used(n)

            def out_project(tiles, oT_, ready, per_tile):
                total = 4 * len(tiles)
                for i, n in enumerate(tiles):
                    wait_loaded(pe, n)
                    w = slot(n).rearrange("p (k n) -> p k n", k=4)
                    for kk in range(4):
                        k = 4 * i + kk
                        per_tile(k)
                        for t in range(NT):
                            for half in range(2):
                                ins = pe.matmul(y_bank(t, half), oT_[:, k, t * P:(t + 1) * P],
                                                w[:, kk, half * HALF:(half + 1) * HALF],
                                                start=(k == 0), stop=(k == total - 1))
                                if k == total - 1:
                                    ins.then_inc(y_ready, 1)
                    if i < len(tiles) - 1:
                        used(n, ins)
                    else:
                        y_count[0] += 4
                        last_use[n] = (y_ready, y_count[0])

            def norm(j):
                for u in range(4):
                    bank = open_unit(f"norm{j}")
                    pe.wait_ge(xn_done, 2 * (j + 1))
                    for kk in range(2):
                        for t in range(NT):
                            k = 2 * u + kk
                            ins = pe.transpose(bank[:, kk * T + t * P:kk * T + (t + 1) * P],
                                               xn[:, t, k * P:(k + 1) * P], ident)
                    ins.then_inc(unit_ready, 1)

            def wait_h(j):
                wait_read(pe, f"norm{j}", 0)
                wait_read(pe, f"norm{j}", 3)

            def mod_columns(m):
                pe.wait_ge(mod_summed, m + 1)
                if m >= 2:
                    pe.wait_ge(mod_read, m - 1)
                bank = ps[:, 6 + m % 2, :]
                if m in (4, 5, 14, 15):
                    ins = pe.matmul(bank, ones, acc[:, m % 2, :], start=True, stop=True)
                else:
                    for c in range(4):
                        ins = pe.matmul(bank[:, c:c + 1], acc[:, m % 2, c * P:(c + 1) * P], ones[:, 0:1],
                                        start=True, stop=True)
                ins.then_inc(mod_cols, 1)

            pe.wait_ge(consts_in, 32)
            pe.wait_ge(rows_in, 16 * NVEC)
            for i in range(2):
                ins = pe.transpose(ps[:, 4, i * P:(i + 1) * P], vec_rows[i], ident)
            ins.then_inc(rows_turned, 1)
            for m in range(4):
                mod_columns(m)
            norm(0)
            wait_h(0)

            for n in range(16):
                tile = AT[("a_in", n)]
                stage = ("a_f", "a_i", "a_q", "a_g")[n // 4]
                if stage == "a_i":
                    project_tokens(stage, tile, hT)
                else:
                    for _ in project_features(stage, tile, hT):
                        pass
                if 4 <= n < 14:
                    mod_columns(n)

            def keys_turned(h):
                pe.wait_ge(st("kin_ready"), 2 * (h + 1))
                if h >= 2:
                    pe.wait_ge(st("kst_copied"), h - 1)
                for t in range(NT):
                    ins = pe.transpose(ps[:, 6 + h % 2, t * P:(t + 1) * P],
                                       k_st[:, h, t * P:(t + 1) * P], ident)
                ins.then_inc(st("kst_turned"), 1)

            def scores(h):
                wait_read(pe, "a_q", h // 2)
                if h >= 2:
                    pe.wait_ge(st("att_masked"), h - 1)
                for t in range(NT):
                    sl = slice(t * P, (t + 1) * P)
                    ins = pe.matmul(ps[:, 4 + h % 2, sl], k_in[:, h, sl], q_dec[:, h, sl], start=True, stop=True)
                ins.then_inc(st("att_ready"), 1)

            def states(h):
                pe.wait_ge(st("kst_copied"), h + 1)
                if h >= 1:
                    pe.wait_ge(st("state_saved"), h)
                for n in range(NC - 1):
                    rows = slice(CHUNK * (n % 2), CHUNK * (n % 2) + CHUNK)
                    ins = pe.matmul(ps[:, n % 2, n * P:(n + 1) * P], kst_sb[rows, h % 2, n // 2, :],
                                    v_rows[rows, n // 2, h * P:(h + 1) * P], start=True, stop=True)
                ins.then_inc(st("state_ready"), 1)

            def outputs(h):
                pe.wait_ge(st("att_masked"), h + 1)
                pe.wait_ge(st("state_saved"), h + 1)
                if h >= 2:
                    pe.wait_ge(st("o_used"), h - 1)
                bank = ps[:, 2 + h % 2, :]
                for t in range(NT):
                    pe.matmul(bank[:, t * P:(t + 1) * P], v_rows[:, t, h * P:(h + 1) * P], att_sb[:, h % 2, t, :],
                              start=True, stop=False)
                    for n in range(max(1, 2 * t), 2 * t + 2):
                        sl = slice(n * CHUNK, (n + 1) * CHUNK)
                        ins = pe.matmul(bank[:, sl], state[:, h % 2, n - 1, :], q_dec[:, h, sl],
                                        start=False, stop=(n == 2 * t + 1))
                ins.then_inc(st("o_ready"), 1)

            def square_sums(h):
                pe.wait_ge(st("osq_ready"), h + 1)
                pe.matmul(ps[:, 2 + h % 2, T:2 * T], ones, o_sq[:, h % 2, :], start=True, stop=True)\
                    .then_inc(st("ossq_ready"), 1)

            pe.wait_ge(unit_free["a"], before("a", unit[0] - 1))
            pe.wait_ge(unit_free["v"], before("v", unit[0] - 1))
            pe.wait_ge(mod_read, 14)
            for i in range(HA + 3):
                if i < HA:
                    keys_turned(i)
                    scores(i)
                if 1 <= i <= HA:
                    states(i - 1)
                if 2 <= i <= HA + 1:
                    outputs(i - 2)
                if i >= 3:
                    square_sums(i - 3)
            pe.wait_ge(st("ot_ready"), HA)
            out_project([AT[("a_out", n)] for n in range(4)], oT, None, lambda k: None)

            norm(1)
            wait_h(1)

            def head_square_sums(j, mat, count):
                pe.wait_ge(st("hsq_ready"), count + 1)
                if count >= 2:
                    pe.wait_ge(st("hrstd_ready"), count - 1)
                pe.matmul(ps[:, 4 + count % 2, :], mat, h_sq[:, count % 2, :], start=True, stop=True)\
                    .then_inc(st("hssq_ready"), 1)

            count = 0
            pe.wait_ge(x_done, 4)
            for n in range(4):
                for pair in project_features("k", AT[("kv", n)], hkT):
                    if 2 * n + pair >= 1:
                        head_square_sums(0, ones, count)
                        count += 1
            for n in range(4, 8):
                project_tokens("v", AT[("kv", n)], hkT)
                if n == 4:
                    head_square_sums(0, ones, count)
                    count += 1
            n = AT[("forget", 0)]
            wait_loaded(pe, n)
            bank = open_unit("forget")
            w = slot(n)[:, 0:KD * HA].rearrange("p (k n) -> p k n", k=KD)
            feature_major(bank[0:HA, 0:T], lambda k: w[:, k, :], hkT).then_inc(unit_ready, 1)
            used(n)
            for n in range(8):
                stage = "q" if n < 4 else "g"
                for pair in project_features(stage, AT[("b_in", n)], hT):
                    if n < 4 and 2 * n + pair >= 1 or n == 4 and pair == 0:
                        head_square_sums(0, ones, count)
                        count += 1
                if n in (2, 3):
                    mod_columns(12 + n)

            def softmax_heads(pre, heads, logits, pv):
                for i in range(heads + 3):
                    if i < heads:
                        if i >= 2:
                            pe.wait_ge(st(pre + "_max"), i - 1)
                        logits(i, ps[:, 4 + i % 2, :]).then_inc(st(pre + "_logits"), 1)
                    if 2 <= i < heads + 2:
                        h = i - 2
                        pe.wait_ge(st(pre + "_prob"), h + 1)
                        if h >= 2:
                            pe.wait_ge(st(pre + "_tcopied"), h - 1)
                        for b in range(3):
                            ins = pe.transpose(ps[:, 6 + h % 2, b * P:(b + 1) * P], prob[:, h % 3, b * P:(b + 1) * P], ident)
                        ins.then_inc(st(pre + "_turned"), 1)
                    if i >= 3:
                        h = i - 3
                        pe.wait_ge(st(pre + "_tcopied"), h + 1)
                        pv(h)

            def fox_logits(h, bank):
                if h % 2 == 0:
                    wait_read(pe, "q", h // 2)
                if h == 0:
                    pe.wait_ge(st("nf_ready"), 1)
                one = ident[0:HA, h:h + 1].to_broadcast([HA, P])
                for t in range(NT):
                    o = bank[:, P * t:P * t + P * (t + 1)]
                    pe.matmul(o, qN[:, h, t * P:(t + 1) * P], kN[:, h, 0:P * (t + 1)], start=True, stop=False)
                    ins = pe.matmul(o, one, neg_f[:, 0:P * (t + 1)], start=False, stop=True)
                return ins

            def fox_pv(h):
                if h >= 2:
                    pe.wait_ge(st("fx_out"), h - 1)
                bank = ps[:, h % 2, :]
                vh = lambda s: v2_rows[:, s, h * P:(h + 1) * P]
                pe.matmul(bank[:, 0:P], vh(0), probT[:, h % 2, 0:P], start=True, stop=True)
                pe.matmul(bank[:, P:T], vh(0), probT[:, h % 2, P:2 * P], start=True, stop=False)
                pe.matmul(bank[:, P:T], vh(1), probT[:, h % 2, 2 * P:3 * P], start=False, stop=True)\
                    .then_inc(st("fx_o"), 1)

            pe.wait_ge(unit_free["a"], before("a", unit[0] - 1))
            pe.wait_ge(unit_free["v"], before("v", unit[0] - 1))
            pe.wait_ge(mod_read, 16)
            pe.wait_ge(st("hrstd_ready"), 16)
            softmax_heads("fx", HA, fox_logits, fox_pv)
            pe.wait_ge(st("fx_out"), HA)
            out_project([AT[("b_out", n)] for n in range(4)], oT2, None, lambda k: None)

            norm(2)
            wait_h(2)
            n = AT[("ev_kvi", 0)]
            wait_loaded(pe, n)
            wk = slot(n).rearrange("p (k n) -> p k n", k=KD)
            bank = open_unit("ev_i")
            for c in range(2):
                ins = feature_major(bank[:, c * T:(c + 1) * T], lambda k: wk[:, k, 256 + c * P:256 + (c + 1) * P], hT)
            ins.then_inc(unit_ready, 1)
            n2 = AT[("ev_small", 0)]
            wait_loaded(pe, n2)
            ws = slot(n2)[:, 0:KD * 68].rearrange("p (k n) -> p k n", k=KD)
            bank = open_unit("ev_i")
            for half in range(2):
                for k in range(KD):
                    pe.matmul(bank[HD2 * half:HD2 * (half + 1), 0:T], ws[:, k, 0:HD2], hT[:, k, :],
                              start=(k == 0), stop=(k == KD - 1))
            for t in range(NT):
                ins = token_major(bank[:, T + 4 * t:T + 4 * t + 4], hT, t, lambda k: ws[:, k, 64:68])
            ins.then_inc(unit_ready, 1)
            bank = open_unit("ev_i")
            for t in range(NT):
                ins = token_major(bank[:, t * P:(t + 1) * P], hT, t, lambda k: wk[:, k, P:2 * P])
            ins.then_inc(unit_ready, 1)
            pe.wait_ge(x_done, 8)
            wait_read(pe, "ev_i", 1)
            for h in range(HIDX):
                rows = slice(HD2 * (h % 2), HD2 * (h % 2) + HD2)
                for t in range(NT):
                    ins = pe.matmul(ps[:, 4 + h, P * t:P * t + P * (t + 1)], evqi[rows, h // 2, t * P:(t + 1) * P],
                                    evki[rows, 0:P * (t + 1)], start=True, stop=True)
                ins.then_inc(st("ev_rel"), 1)
            bank = open_unit("ev_k")
            for g in range(2):
                for half in range(2):
                    for k in range(KD):
                        ins = pe.matmul(bank[HD2 * half:HD2 * (half + 1), g * T:(g + 1) * T],
                                        wk[:, k, HD2 * g:HD2 * (g + 1)], hT[:, k, :],
                                        start=(k == 0), stop=(k == KD - 1))
            ins.then_inc(unit_ready, 1)
            used(AT[("ev_kvi", 0)])
            used(AT[("ev_small", 0)])
            for pair in project_features("ev_q", AT[("ev_q", 0)], hT):
                if pair == 0:
                    pe.wait_ge(st("ev_relu"), HIDX)
                head_square_sums(0, ones64, count)
                count += 1
            for pair in project_features("ev_u", AT[("ev_u", 0)], hT):
                if pair == 0:
                    head_square_sums(0, ones64, count)
                    count += 1
            n = AT[("pool_w", 0)]
            wait_loaded(pe, n)
            wp = slot(n)[:, 0:4 * P].rearrange("p (g d) -> p g d", g=4)
            for pair in range(2):
                bank = open_unit("ev_pool")
                for j in range(2):
                    g = 2 * pair + j
                    pe.wait_ge(st("ev_mixed"), g + 1)
                    ins = pe.matmul(bank[:, j * T:(j + 1) * T], wp[:, g, :], mixed[:, g, :], start=True, stop=True)
                ins.then_inc(unit_ready, 1)
            used(n)

            def ds_logits(h, bank):
                if h == 0:
                    wait_read(pe, "ev_q", 1)
                rows = slice(HD2 * (h % 2), HD2 * (h % 2) + HD2)
                for t in range(NT):
                    ins = pe.matmul(bank[:, P * t:P * t + P * (t + 1)], evq[rows, h // 2, t * P:(t + 1) * P],
                                    evk[rows, h // 4, 0:P * (t + 1)], start=True, stop=True)
                return ins

            def ds_pv(h):
                if h % 2 == 0 and h >= 4:
                    pe.wait_ge(st("ds_out"), h // 2 - 1)
                rows = slice(HD2 * (h % 2), HD2 * (h % 2) + HD2)
                bank = ps[rows, (h // 2) % 2, :]
                vh = lambda s: evv[:, s, HD2 * (h // 4):HD2 * (h // 4) + HD2]
                pe.matmul(bank[:, 0:P], vh(0), probT[:, h % 2, 0:P], start=True, stop=True)
                pe.matmul(bank[:, P:T], vh(0), probT[:, h % 2, P:2 * P], start=True, stop=False)
                pe.matmul(bank[:, P:T], vh(1), probT[:, h % 2, 2 * P:3 * P], start=False, stop=True)\
                    .then_inc(st("ds_o"), 1)

            pe.wait_ge(unit_free["a"], before("a", unit[0] - 1))
            pe.wait_ge(unit_free["v"], before("v", unit[0] - 1))
            softmax_heads("ds", HE, ds_logits, ds_pv)
            pe.wait_ge(st("ds_out"), HE // 2)
            wait_read(pe, "ev_pool", 1)
            out_project([AT[("ev_out", n)] for n in range(2)], ev_oT, None, lambda k: None)

            def feed_forward(layer, xs):
                stage = f"up{layer}"

                def up(i):
                    n = AT[("up", layer, i)]
                    wait_loaded(pe, n)
                    for j in range(2):
                        bank = open_unit(stage)
                        for part in range(2):
                            w = slot(n)[:, 2048 * part:2048 * (part + 1)].rearrange("p (k n) -> p k n", k=KD)
                            ins = feature_major(bank[:, part * T:(part + 1) * T],
                                                lambda k: w[:, k, j * P:(j + 1) * P], hT)
                        ins.then_inc(unit_ready, 1)
                    used(n)

                def down(i):
                    n = AT[("down", layer, i)]
                    wait_loaded(pe, n)
                    if i == 0:
                        pe.wait_ge(x_done, xs)
                    w = slot(n).rearrange("p (k n) -> p k n", k=4)
                    for c in range(4 * i, min(4 * i + 4, FC)):
                        wait_read(pe, f"up{layer}", c)
                        for t in range(NT):
                            for half in range(2):
                                ins = pe.matmul(y_bank(t, half), gated[:, c % 8, t * P:(t + 1) * P],
                                                w[:, c - 4 * i, half * HALF:(half + 1) * HALF],
                                                start=(c == 0), stop=(c == FC - 1))
                                if c == FC - 1:
                                    ins.then_inc(y_ready, 1)
                    if i < 5:
                        used(n, ins)
                        downs[layer, i] = tiles_used[0]
                    else:
                        y_count[0] += 4
                        last_use[n] = (y_ready, y_count[0])

                up(0)
                up(1)
                up(2)
                down(0)
                for i in range(1, 5):
                    up(2 * i + 1)
                    up(2 * i + 2)
                    down(i)
                down(5)

            norm(3)
            wait_h(3)
            feed_forward(0, 12)

            norm(4)
            wait_h(4)
            for n in range(4):
                for _ in project_features("od_q" if n < 2 else "od_k", AT[("od_in", n)], hT):
                    pass
            for n in range(4, 6):
                project_tokens("od_v", AT[("od_in", n)], hT)

            def z_scores(h):
                if h >= 3:
                    pe.wait_ge(st("sb_exp"), h - 2)
                rows = slice(HD2 * (h % 2), HD2 * (h % 2) + HD2)
                bank = ps[:, 4 + h % 3, :]
                pe.matmul(bank[:, 0:T], odk[rows, h // 2, 0:P], odq[rows, h // 2, :], start=True, stop=True)
                pe.matmul(bank[:, T:S3], odk[rows, h // 2, P:T], odq[rows, h // 2, P:T], start=True, stop=True)\
                    .then_inc(st("sb_z"), 1)

            def minus_breaks(h):
                pe.wait_ge(st("sb_masked"), h + 1)
                bank, b = ps[:, 4 + h % 3, :], sb_brk(h)
                rows = slice(HD2 * (h % 2), HD2 * (h % 2) + HD2)
                pe.matmul(bank[:, 0:T], odk[rows, h // 2, 0:P], odq[rows, h // 2, :], start=True, stop=False)
                pe.matmul(bank[:, 0:T], neg_after, b[:, 0:T], start=False, stop=False)
                pe.matmul(bank[:, P:T], neg_ones, b[:, T:S3], start=False, stop=True)
                pe.matmul(bank[:, T:S3], odk[rows, h // 2, P:T], odq[rows, h // 2, P:T], start=True, stop=False)
                pe.matmul(bank[:, T:S3], neg_after, b[:, T:S3], start=False, stop=True).then_inc(st("sb_log"), 1)

            def weighted_values(h):
                pe.wait_ge(st("sb_sel"), h + 1)
                if h % 2 == 0 and h >= 4:
                    pe.wait_ge(st("sb_out"), h // 2 - 1)
                rows = slice(HD2 * (h % 2), HD2 * (h % 2) + HD2)
                bank, pr = ps[rows, (h // 2) % 2, :], sb_prob(h)
                vh = lambda s: odv[:, s, h * HD2:(h + 1) * HD2]
                pe.matmul(bank[:, 0:T], vh(0), pr[:, 0:T], start=True, stop=False)
                pe.matmul(bank[:, P:T], vh(1), pr[:, T:S3], start=False, stop=True).then_inc(st("sb_o"), 1)

            pe.wait_ge(unit_free["a"], before("a", unit[0] - 1))
            pe.wait_ge(unit_free["v"], before("v", unit[0] - 1))
            pe.wait_ge(x_done, 16)
            for i in range(HO + 3):
                if i < HO:
                    z_scores(i)
                if 1 <= i < HO + 1:
                    minus_breaks(i - 1)
                if i >= 3:
                    weighted_values(i - 3)
            pe.wait_ge(st("sb_out"), HO // 2)
            out_project([AT[("od_out", n)] for n in range(2)], od_oT, None, lambda k: None)
            norm(5)
            wait_h(5)
            feed_forward(1, 20)

        @block.sync
        def _(sp):
            sp.dma_start(cst[:, :], const).then_inc(consts_in, 16)
            sp.dma_start(att_mask[:, :, :], mask.rearrange("p (t c) -> p t c", t=2)).then_inc(consts_in, 16)
            for n in range(len(TILES)):
                if n >= NSLOT:
                    sp.wait_ge(*last_use[n - NSLOT])
                for dst, src in tile_dmas(n):
                    sp.dma_start(dst, src).then_inc(loaded[n % NSLOT], 16)
            for t in range(NT):
                sp.wait_ge(x_done, 4 * 5 + 2 * (t + 1))
                sp.dma_start(out[0, t * P:(t + 1) * P, :], x[:, t, :]).then_inc(out_stored, 16)
            sp.wait_ge(out_stored, 16 * NT)

        @block.scalar
        def _(act):
            def link(ins):
                then("act", act, ins)

            def unit_of(stage, i):
                u = FIRST[stage] + i
                act.wait_ge(unit_ready, u + 1)
                return unit_bank(u)

            def norm(j, outs):
                for t in range(NT):
                    if j == 0:
                        if t == 0:
                            act.wait_ge(x_in, 16)
                    else:
                        act.wait_ge(x_done, 4 * (j - 1) + 2 * (t + 1))
                    ins = act.activation(xn[:, t, :], x[:, t, :], ACT.Square, accum_out=ssum[:, t:t + 1])
                link(ins)
                link(act.activation(rstd, ssum, ACT.Ln, scale=1.0 / D, bias=eps_t))
                act.activation(rstd, rstd, ACT.Exp, scale=-0.5).then_inc(rstd_done, 1)
                bank = unit_of(f"norm{j}", 0)
                for dst, scale, shift in outs:
                    for kk in range(2):
                        ins = act.activation(dst[:, kk, :], bank[:, kk * T:(kk + 1) * T], ACT.Identity,
                                             scale=scale[:, kk:kk + 1],
                                             bias=0.0 if shift is None else shift[:, kk:kk + 1])
                ins.then_inc(unit_free["a"], 1)

            act.wait_ge(cols_ready, 2)
            act.activation(silu_c, col["c"], ACT.Silu).then_inc(silu_c_ready, 1)
            link(act.activation(lb, lb_tmp, ACT.Sigmoid))
            act.activation(one_m_lb, lb_tmp, ACT.Sigmoid, scale=-1.0).then_inc(st("gate_sig_in"), 1)
            act.wait_ge(mod_read, 4)
            norm(0, [(hT, scale0, shift0)])

            for u in range(8):
                bank = unit_of("a_f", u)
                sl = slice(2 * u, 2 * u + 2)
                act.activation(fz_b[:, sl, :], bank.rearrange("p (h t) -> p h t", h=2), ACT.Sigmoid)\
                    .then_inc(st("sig_ready"), 1)
                act.activation(k_in0[:, sl, :], bank.rearrange("p (h t) -> p h t", h=2), ACT.Sigmoid, scale=-1.0)\
                    .then_inc(unit_free["a"], 1)
            act.wait_ge(st("sig_ready"), 8)
            for h in range(HA):
                act.activation(fz_b[:, h, :], fz_b[:, h, :], ACT.Ln, scale=one_m_lb[:, h:h + 1],
                               bias=lb[:, h:h + 1]).then_inc(st("ln_ready"), 1)

            def copy_v(u):
                bank = unit_of("a_i", u)
                act.activation(v_rows[:, u % 2, (u // 2) * HALF:(u // 2 + 1) * HALF], bank, ACT.Copy)\
                    .then_inc(unit_free["a"], 1)

            def exps(g):
                sl = slice(4 * g, 4 * g + 4)
                act.wait_ge(st("scan_ready"), g + 1)
                act.activation(q_dec[:, sl, :], fz_b[:, sl, :], ACT.Exp).then_inc(st("exp_ready"), 1)
                act.activation(k_in[:, sl, :], fz_b[:, sl, :], ACT.Exp, scale=-1.0).then_inc(st("exp_ready"), 1)
                act.wait_ge(st("spread_ready"), g + 1)
                act.activation(k_st[:, sl, :], k_st[:, sl, :], ACT.Exp).then_inc(st("spread_exp"), 1)

            copy_v(0)
            exps(0)
            copy_v(1)
            exps(1)
            copy_v(2)
            exps(2)
            copy_v(3)
            exps(3)
            for u in range(4, 8):
                copy_v(u)
            for u in range(8):
                bank = unit_of("a_g", u)
                act.activation(silu_g[:, 2 * u:2 * u + 2, :], bank.rearrange("p (h t) -> p h t", h=2), ACT.Silu)\
                    .then_inc(unit_free["a"], 1)

            def o_scale(h):
                act.wait_ge(st("ossq_ready"), h + 1)
                if h >= 2:
                    act.wait_ge(st("o_used"), h - 1)
                link(act.activation(o_r[:, h % 2, :], ps[:, 2 + h % 2, T:2 * T], ACT.Ln,
                                    scale=1.0 / P, bias=eps_t))
                act.activation(o_r[:, h % 2, :], o_r[:, h % 2, :], ACT.Exp, scale=-0.5).then_inc(st("orstd_ready"), 1)

            for i in range(HA + 4):
                if i < HA:
                    act.wait_ge(st("kst_turned"), i + 1)
                    if i >= 2:
                        act.wait_ge(st("state_ready"), i - 1)
                    act.activation(kst_sb[:, i % 2, :, :], ps[:, 6 + i % 2, 0:T].rearrange(
                        "p (t k) -> p t k", t=2), ACT.Copy).then_inc(st("kst_copied"), 1)
                if 2 <= i < HA + 2:
                    h = i - 2
                    act.wait_ge(st("o_ready"), h + 1)
                    if h >= 2:
                        act.wait_ge(st("ossq_ready"), h - 1)
                    act.activation(o_sq[:, h % 2, :], ps[:, 2 + h % 2, 0:T], ACT.Square).then_inc(st("osq_ready"), 1)
                if 3 <= i < HA + 3:
                    o_scale(i - 3)

            norm(1, [(hkT, scale_kv, shift_kv), (hT, scale1, shift1)])
            count = [0]

            normed_units = [("k", i) for i in range(8)] + [("q", i) for i in range(8)] + [
                ("ev_k", 0), ("ev_q", 0), ("ev_q", 1)]

            def square_unit(stage, i):
                n = count[0]
                bank = unit_of(stage, i)
                if n >= 2:
                    act.wait_ge(st("hssq_ready"), n - 1)
                act.activation(h_sq[:, n % 2, :], bank, ACT.Square).then_inc(st("hsq_ready"), 1)
                count[0] += 1

            def scale_unit(n, size):
                act.wait_ge(st("hssq_ready"), n + 1)
                if n >= 2:
                    wait_read(act, *normed_units[n - 2])
                link(act.activation(h_r[:, n % 2, :], ps[:, 4 + n % 2, :], ACT.Ln, scale=1.0 / size, bias=eps_t))
                act.activation(h_r[:, n % 2, :], h_r[:, n % 2, :], ACT.Exp, scale=-0.5).then_inc(st("hrstd_ready"), 1)

            for i in range(8):
                square_unit("k", i)
                if i >= 1:
                    scale_unit(i - 1, P)
            for u in range(8):
                bank = unit_of("v", u)
                act.activation(v2_rows[:, u % 2, (u // 2) * HALF:(u // 2 + 1) * HALF], bank, ACT.Copy)\
                    .then_inc(unit_free["a"], 1)
                if u == 1:
                    scale_unit(7, P)
            bank = unit_of("forget", 0)
            act.wait_ge(fb_in, 16)
            act.wait_ge(st("f_min"), 1)
            link(act.activation(f_a, bank[0:HA, 0:T], ACT.Abs, bias=forget_b))
            link(act.activation(f_a, f_a, ACT.Exp, scale=-1.0))
            act.activation(f_a, f_a, ACT.Ln, bias=1.0).then_inc(st("f_ln"), 1)
            for i in range(8):
                square_unit("q", i)
                if i >= 1:
                    scale_unit(8 + i - 1, P)
            scale_unit(15, P)
            for u in range(8):
                bank = unit_of("g", u)
                act.activation(silu_g2[:, 2 * u:2 * u + 2, :], bank.rearrange("p (h t) -> p h t", h=2), ACT.Silu)\
                    .then_inc(unit_free["a"], 1)

            def softmax_heads(pre, heads):
                for i in range(heads + 2):
                    if i < heads:
                        act.wait_ge(st(pre + "_max"), i + 1)
                        if i >= 3:
                            act.wait_ge(st(pre + "_turned"), i - 2)
                        for t, q in enumerate((Q0, Q1)):
                            c = 2 * (i % 2) + t
                            ins = act.activation(prob[:, i % 3, q], lg[:, i % 2, q], ACT.Exp,
                                                 bias=row_neg[:, c:c + 1], accum_out=row_sum[:, c:c + 1])
                            if t == 1:
                                ins.then_inc(st(pre + "_exp"), 1)
                    if i >= 2:
                        h = i - 2
                        act.wait_ge(st(pre + "_turned"), h + 1)
                        if h >= 2:
                            act.wait_ge(st(pre + "_o"), h - 1)
                        act.activation(probT[:, h % 2, :], ps[:, 6 + h % 2, 0:S3], ACT.Copy)\
                            .then_inc(st(pre + "_tcopied"), 1)

            softmax_heads("fx", HA)

            norm(2, [(hT, col["norm_mix_g_2"][:, 0:8], None)])
            bank = unit_of("ev_i", 0)
            act.activation(evqi, bank.rearrange("p (c t) -> p c t", c=2), ACT.Copy).then_inc(unit_free["a"], 1)
            bank = unit_of("ev_i", 1)
            act.activation(evki, bank[:, 0:T], ACT.Copy)
            act.activation(w_idx, bank[:, T:T + 8], ACT.Copy, scale=float((HIDX * HD2) ** -0.5))\
                .then_inc(unit_free["a"], 1)
            bank = unit_of("ev_i", 2)
            act.activation(evv, bank[:, 0:T].rearrange("p (t d) -> p t d", t=2), ACT.Copy).then_inc(unit_free["a"], 1)
            for h in range(HIDX):
                act.wait_ge(st("ev_rel"), h + 1)
                if h >= 2:
                    act.wait_ge(st("ev_score_used"), h - 1)
                act.activation(relu_s[:, h % 2, :], ps[:, 4 + h, 0:S3], ACT.Relu).then_inc(st("ev_relu"), 1)
            square_unit("ev_k", 0)
            square_unit("ev_q", 0)
            scale_unit(16, HD2)
            square_unit("ev_q", 1)
            scale_unit(17, HD2)
            for u in range(2):
                bank = unit_of("ev_u", u)
                act.activation(u_pad[:, 2 * u:2 * u + 2, PAD:], bank.rearrange("p (g t) -> p g t", g=2), ACT.Copy)\
                    .then_inc(unit_free["a"], 1)
                if u == 0:
                    scale_unit(18, HD2)
            softmax_heads("ds", HE)

            def feed_forward(layer):
                for c in range(FC):
                    bank = unit_of(f"up{layer}", c)
                    if c >= 2:
                        wait_read(act, f"up{layer}", c - 2)
                    act.activation(silu_a[:, c % 2, :], bank[:, 0:T], ACT.Silu).then_inc(st("up_silu"), 1)

            norm(3, [(hT, col["norm_ffn_g_2"][:, 0:8], None)])
            feed_forward(0)

            norm(4, [(hT, col["norm_mix_g_2"][:, 8:16], None)])
            for u in range(4):
                bank = unit_of("od_q", u)
                act.activation(odq[:, 2 * u:2 * u + 2, :], bank.rearrange("p (h t) -> p h t", h=2), ACT.Copy,
                               scale=float(HD2 ** -0.5)).then_inc(unit_free["a"], 1)
            for u in (0, 2):
                bank = unit_of("od_v", u)
                act.activation(odv[:, 0, (u // 2) * HALF:(u // 2 + 1) * HALF], bank, ACT.Copy)\
                    .then_inc(unit_free["a"], 1)
            for i in range(HO + 1):
                if i < HO:
                    act.wait_ge(st("sb_z"), i + 1)
                    if i >= 2:
                        act.wait_ge(st("sb_soft"), i - 1)
                    link(act.activation(sb_ln_t(i), ps[:, 4 + i % 3, 0:S3], ACT.Abs))
                    link(act.activation(sb_ln_t(i), sb_ln_t(i), ACT.Exp, scale=-1.0))
                    act.activation(sb_ln_t(i), sb_ln_t(i), ACT.Ln, bias=1.0).then_inc(st("sb_ln"), 1)
                if i >= 1:
                    h = i - 1
                    act.wait_ge(st("sb_log"), h + 1)
                    if h >= 3:
                        act.wait_ge(st("sb_o"), h - 2)
                    act.activation(sb_prob(h), ps[:, 4 + h % 3, 0:S3], ACT.Exp).then_inc(st("sb_exp"), 1)
            norm(5, [(hT, col["norm_ffn_g_2"][:, 8:16], None)])
            feed_forward(1)

        @block.vector
        def _(dve):
            def link(ins):
                then("dve", dve, ins)

            def unit_of(stage, i):
                u = FIRST[stage] + i
                dve.wait_ge(unit_ready, u + 1)
                return unit_bank(u)

            def norm(j, outs):
                dve.wait_ge(rstd_done, j + 1)
                for t in range(NT):
                    dve.tensor_scalar(xn[:, t, :], x[:, t, :], rstd[:, t:t + 1], None, ALU.mult).then_inc(xn_done, 1)
                for u in range(1, 4):
                    bank = unit_of(f"norm{j}", u)
                    for dst, scale, shift in outs:
                        for kk in range(2):
                            k = 2 * u + kk
                            if shift is None:
                                ins = dve.tensor_scalar(dst[:, k, :], bank[:, kk * T:(kk + 1) * T], scale[:, k:k + 1],
                                                        None, ALU.mult)
                            else:
                                ins = dve.tensor_scalar(dst[:, k, :], bank[:, kk * T:(kk + 1) * T], scale[:, k:k + 1],
                                                        shift[:, k:k + 1], ALU.mult, ALU.add)
                    ins.then_inc(unit_free["v"], 1)

            def add_y(j, gated_):
                for t in range(NT):
                    for n in range(2):
                        sl = slice(n * HALF, (n + 1) * HALF)
                        dve.wait_ge(y_ready, 4 * j + 2 * t + n + 1)
                        src = y_bank(t, n)
                        if gated_:
                            link(dve.tensor_tensor(acc[:, n, :], src, gate[:, sl], ALU.mult))
                            src = acc[:, n, :]
                        dve.tensor_tensor(x[:, t, sl], x[:, t, sl], src, ALU.add).then_inc(x_done, 1)

            mb = col["mod_b"]
            dest = {0: (shift0, 0, mb, 0, None), 1: (shift0, 4, mb, 4, None),
                    2: (scale0, 0, mb, 8, col["norm_g"][:, 0:4]), 3: (scale0, 4, mb, 12, col["norm_g"][:, 4:8]),
                    6: (shift1, 0, mb, 24, None), 7: (shift1, 4, mb, 28, None),
                    8: (scale1, 0, mb, 32, col["norm_g"][:, 8:12]), 9: (scale1, 4, mb, 36, col["norm_g"][:, 12:16]),
                    10: (shift_kv, 0, col["kv_mod_b"], 0, None), 11: (shift_kv, 4, col["kv_mod_b"], 4, None),
                    12: (scale_kv, 0, col["kv_mod_b"], 8, col["kv_norm_g"][:, 0:4]),
                    13: (scale_kv, 4, col["kv_mod_b"], 12, col["kv_norm_g"][:, 4:8])}

            def mod_sum(m):
                n = AT[("mod", m)]
                wait_loaded(dve, n)
                if m >= 2:
                    dve.wait_ge(mod_cols, m - 1)
                w = slot(n).rearrange("p (k n) -> p k n", k=KD)
                link(dve.tensor_scalar(acc[:, m % 2, :], w[:, 0, :], silu_c[:, 0:1], None, ALU.mult))
                for k in range(1, KD):
                    ins = dve.scalar_tensor_tensor(out=acc[:, m % 2, :], in0=w[:, k, :], scalar=silu_c[:, k:k + 1],
                                                   in1=acc[:, m % 2, :], op0=ALU.mult, op1=ALU.add)
                    if k < KD - 1:
                        link(ins)
                ins.then_inc(mod_summed, 1)

            def mod_take(m):
                dve.wait_ge(mod_cols, m + 1)
                bank = ps[:, 6 + m % 2, :]
                if m in (4, 5, 14, 15):
                    dve.wait_ge(gate_b_in, 16 if m < 14 else 32)
                    sl = slice((m % 2) * HALF, (m % 2 + 1) * HALF)
                    dve.tensor_tensor(gate[:, sl], gate[:, sl], bank, ALU.add).then_inc(mod_read, 1)
                    return
                dst, c, bias, b, gain = dest[m]
                if gain is None:
                    dve.tensor_tensor(dst[:, c:c + 4], bank[:, 0:4], bias[:, b:b + 4], ALU.add).then_inc(mod_read, 1)
                else:
                    link(dve.scalar_tensor_tensor(out=mod_tmp, in0=bank[:, 0:4], scalar=1.0, in1=bias[:, b:b + 4],
                                                  op0=ALU.add, op1=ALU.add))
                    dve.tensor_tensor(dst[:, c:c + 4], mod_tmp, gain, ALU.mult).then_inc(mod_read, 1)
                dve.wait_ge(mod_read, m + 1)

            dve.memset(eps_t, EPS)
            dve.wait_ge(rows_turned, 1)
            dve.tensor_copy(cols[:, :], ps[:, 4, 0:256]).then_inc(cols_ready, 1)
            dve.wait_ge(cols_ready, 1)
            link(dve.tensor_tensor(lb_tmp, col["a_lb_logits"][:, 0:16], col["a_lb_logits"][:, 16:32], ALU.subtract))
            dve.tensor_scalar(q_gain, col["b_q_norm_g"], float(P ** -0.5), None, ALU.mult)
            dve.tensor_scalar(ev_q_gain, ev_gain[:, 0:1], float(HD2 ** -0.5), None, ALU.mult).then_inc(cols_ready, 1)
            dve.wait_ge(cols_ready, 2)
            dve.wait_ge(silu_c_ready, 1)
            for m in range(4):
                mod_sum(m)
                if m >= 1:
                    mod_take(m - 1)
            mod_take(3)
            norm(0, [(hT, scale0, shift0)])
            dve.wait_ge(st("gate_sig_in"), 1)

            link(dve.memset(att_sb, 0.0))
            mod_sum(4)
            mod_sum(5)
            for g in range(4):
                sl = slice(4 * g, 4 * g + 4)
                for h in range(4 * g, 4 * g + 4):
                    dve.wait_ge(st("ln_ready"), h + 1)
                    ins = dve.tensor_tensor_scan(fz_b[:, h, :], chunk_go, fz_b[:, h, :], 0.0, ALU.mult, ALU.add)
                ins.then_inc(st("scan_ready"), 1)
                dve.wait_ge(st("scan_ready"), g + 1)
                part = fz_b[:, sl, :].rearrange("p h (n c) -> p (h n) c", c=CHUNK)
                dst = k_st[:, sl, :].rearrange("p h (n c) -> p (h n) c", c=CHUNK)
                dve.tensor_tensor(dst, part[:, :, CHUNK - 1:CHUNK].to_broadcast([P, 4 * NC, CHUNK]), part,
                                  ALU.subtract).then_inc(st("spread_ready"), 1)
                mod_take(4 + g)
                mod_sum(6 + g)
                dve.wait_ge(st("exp_ready"), 2 * (g + 1))
                dve.tensor_copy(dl[:, sl, :], q_dec[:, sl, CHUNK - 1::CHUNK])
                for h in range(4 * g, 4 * g + 4):
                    dve.scalar_tensor_tensor(out=k_in[:, h, :], in0=k_in0[:, h, :], scalar=one_m_lb[:, h:h + 1],
                                             in1=k_in[:, h, :], op0=ALU.mult, op1=ALU.mult)\
                        .then_inc(st("kin_ready"), 1)
                    dve.wait_ge(st("spread_exp"), g + 1)
                    dve.scalar_tensor_tensor(out=k_st[:, h, :], in0=k_in0[:, h, :], scalar=one_m_lb[:, h:h + 1],
                                             in1=k_st[:, h, :], op0=ALU.mult, op1=ALU.mult)\
                        .then_inc(st("kin_ready"), 1)
            for u in range(8):
                bank = unit_of("a_q", u)
                sl = slice(2 * u, 2 * u + 2)
                dve.tensor_tensor(q_dec[:, sl, :], bank.rearrange("p (h t) -> p h t", h=2), q_dec[:, sl, :], ALU.mult)\
                    .then_inc(unit_free["v"], 1)
                if u % 2 == 1:
                    m = 8 + u // 2
                    mod_take(m)
                    mod_sum(m + 2)
            mod_take(12)
            mod_take(13)
            dve.wait_ge(unit_free["a"], before("a", FIRST["a_g"] + 7))

            def o_out(h):
                dve.wait_ge(st("orstd_ready"), h + 1)
                if h >= 1:
                    dve.wait_ge(st("ot_ready"), h)
                dve.scalar_tensor_tensor(out=o_tmp, in0=ps[:, 2 + h % 2, 0:T], scalar=col["a_onorm_g"][:, h:h + 1],
                                         in1=o_r[:, h % 2, :], op0=ALU.mult, op1=ALU.mult).then_inc(st("o_used"), 1)
                dve.wait_ge(st("o_used"), h + 1)
                dve.tensor_tensor(oT[:, h, :], o_tmp, silu_g[:, h, :], ALU.mult).then_inc(st("ot_ready"), 1)

            for i in range(HA + 4):
                if i >= 4:
                    o_out(i - 4)
                if i < HA:
                    dve.wait_ge(st("att_ready"), i + 1)
                    if i >= 2:
                        dve.wait_ge(st("o_ready"), i - 1)
                    dve.copy_predicated(att_sb[:, i % 2, :, :], att_mask[:, :, :],
                                        ps[:, 4 + i % 2, 0:T].rearrange("p (t c) -> p t c", t=2))\
                        .then_inc(st("att_masked"), 1)
                if 1 <= i < HA + 1:
                    h = i - 1
                    dve.wait_ge(st("state_ready"), h + 1)
                    if h >= 2:
                        dve.wait_ge(st("o_ready"), h - 1)
                    link(dve.tensor_copy(state[:, h % 2, 0, :], ps[:, 0, 0:P]))
                    for n in range(1, NC - 1):
                        ins = dve.scalar_tensor_tensor(out=state[:, h % 2, n, :], in0=state[:, h % 2, n - 1, :],
                                                       scalar=dl[:, h, n:n + 1], in1=ps[:, n % 2, n * P:(n + 1) * P],
                                                       op0=ALU.mult, op1=ALU.add)
                        if n < NC - 2:
                            link(ins)
                    ins.then_inc(st("state_saved"), 1)
            add_y(0, True)

            norm(1, [(hkT, scale_kv, shift_kv), (hT, scale1, shift1)])

            def normed(stage, i, n, dst, gain):
                bank = unit_of(stage, i)
                dve.wait_ge(st("hrstd_ready"), n + 1)
                dve.scalar_tensor_tensor(out=dst, in0=bank.rearrange("p (h t) -> p h t", h=2), scalar=gain,
                                         in1=h_r[:, n % 2, :].rearrange("p (h t) -> p h t", h=2),
                                         op0=ALU.mult, op1=ALU.mult).then_inc(unit_free["v"], 1)

            for i in range(8):
                normed("k", i, i, kN[:, 2 * i:2 * i + 2, :], col["k_norm_g"])
            bank = unit_of("forget", 0)
            dve.wait_ge(fb_in, 16)
            dve.tensor_scalar(f_b, bank[0:HA, 0:T], forget_b, 0.0, ALU.add, ALU.min).then_inc(st("f_min"), 1)
            dve.wait_ge(st("f_ln"), 1)
            link(dve.tensor_tensor(f_b, f_a, f_b, ALU.subtract))
            dve.nop().then_inc(unit_free["v"], 1)
            dve.tensor_tensor_scan(neg_f, f_b, f_b, 0.0, ALU.add, ALU.max).then_inc(st("nf_ready"), 1)
            for i in range(8):
                normed("q", i, 8 + i, qN[:, 2 * i:2 * i + 2, :], q_gain)
                if i == 1:
                    mod_sum(14)
                if i == 3:
                    mod_sum(15)
                if i == 6:
                    mod_take(14)
            mod_take(15)
            dve.wait_ge(unit_free["a"], before("a", FIRST["g"] + 7))

            def softmax_heads(pre, heads, bias, output):
                for i in range(heads + 4):
                    if i < heads:
                        dve.wait_ge(st(pre + "_logits"), i + 1)
                        if i >= 2:
                            dve.wait_ge(st(pre + "_exp"), i - 1)
                        c = 2 * (i % 2)
                        for t, q in enumerate((Q0, Q1)):
                            ins = dve.tensor_tensor_reduce(out=lg[:, i % 2, q], in0=ps[:, 4 + i % 2, q], in1=bias[:, q],
                                                           scale=1.0, scalar=LOW, op0=ALU.add, op1=ALU.max,
                                                           accum_out=row_max[:, c + t:c + t + 1])
                        link(ins)
                        dve.tensor_scalar(row_neg[:, c:c + 2], row_max[:, c:c + 2], -1.0, None, ALU.mult)\
                            .then_inc(st(pre + "_max"), 1)
                    if 1 <= i < heads + 1:
                        h = i - 1
                        c = 2 * (h % 2)
                        dve.wait_ge(st(pre + "_exp"), h + 1)
                        link(dve.reciprocal(row_inv[:, c:c + 2], row_sum[:, c:c + 2]))
                        for t, q in enumerate((Q0, Q1)):
                            ins = dve.tensor_scalar(prob[:, h % 3, q], prob[:, h % 3, q], row_inv[:, c + t:c + t + 1],
                                                    None, ALU.mult)
                        ins.then_inc(st(pre + "_prob"), 1)
                    if i >= 4:
                        output(i - 4)

            def fox_out(h):
                dve.wait_ge(st("fx_o"), h + 1)
                dve.tensor_tensor(oT2[:, h, :], ps[:, h % 2, 0:T], silu_g2[:, h, :], ALU.mult).then_inc(st("fx_out"), 1)

            softmax_heads("fx", HA, causal, fox_out)
            add_y(1, True)

            norm(2, [(hT, col["norm_mix_g_2"][:, 0:8], None)])
            dve.memset(u_pad[:, :, 0:PAD], 0.0)
            dve.memset(run_a[:, 0:PAD], 0.0)
            dve.memset(run_b[:, 0:PAD], 0.0)
            wait_read(dve, "ev_i", 1)
            for h in range(HIDX):
                dve.wait_ge(st("ev_relu"), h + 1)
                for t, q in enumerate((Q0, Q1)):
                    wcol = w_idx[:, 4 * t + h:4 * t + h + 1]
                    if h == 0:
                        ins = dve.tensor_scalar(score[:, q], relu_s[:, h % 2, q], wcol, None, ALU.mult)
                    else:
                        ins = dve.scalar_tensor_tensor(out=score[:, q], in0=relu_s[:, h % 2, q], scalar=wcol,
                                                       in1=score[:, q], op0=ALU.mult, op1=ALU.add)
                ins.then_inc(st("ev_score_used"), 1)
                dve.wait_ge(st("ev_score_used"), h + 1)
            link(dve.tensor_tensor(score, score, causal, ALU.add))

            def choose(q, n):
                src = score[:, q]
                for r in range(TOPK // 8):
                    link(dve.max(top8, src))
                    if r < TOPK // 8 - 1:
                        link(dve.match_replace(out=cut[:, 0:n], in_to_replace=top8, in_values=src, imm_value=LOW))
                        src = cut[:, 0:n]
                least = top8[:, 7:8]
                dve.tensor_scalar(sel_eq[:, 0:n], score[:, q], least, None, ALU.is_equal)
                link(dve.tensor_scalar(sel_gt[:, 0:n], score[:, q], least, None, ALU.is_gt, ALU.add, accum_out=cnt))
                link(dve.tensor_scalar(rest, cnt, -1.0, float(TOPK), ALU.mult, ALU.add))
                link(dve.tensor_tensor_scan(sel_pre[:, 0:n], sel_eq[:, 0:n], sel_eq[:, 0:n], 0.0, ALU.add, ALU.max))
                link(dve.scalar_tensor_tensor(out=sel_eq[:, 0:n], in0=sel_pre[:, 0:n], scalar=rest, in1=sel_eq[:, 0:n],
                                              op0=ALU.is_le, op1=ALU.mult))
                link(dve.tensor_tensor(sel_gt[:, 0:n], sel_gt[:, 0:n], sel_eq[:, 0:n], ALU.add))
                link(dve.tensor_scalar(sel_gt[:, 0:n], sel_gt[:, 0:n], -FAR, FAR, ALU.mult, ALU.add))
                link(dve.tensor_tensor(ev_bias_t[:, q], sel_gt[:, 0:n], causal[:, q], ALU.add))

            choose(Q1, T)
            normed("ev_k", 0, 16, evk, ev_gain[:, 1:2])
            normed("ev_q", 0, 17, evq[:, 0:2, :], ev_q_gain)
            normed("ev_q", 1, 18, evq[:, 2:4, :], ev_q_gain)
            choose(Q0, P)
            dve.wait_ge(unit_free["a"], before("a", FIRST["ev_u"] + 1))
            for g in range(4):
                u, window = u_pad[:, g, :], 2
                src, dst, spare = u, run_a, run_b
                step = 1
                for _ in range(g + 1):
                    link(dve.tensor_tensor(dst[:, PAD:], src[:, PAD:], src[:, PAD - step:PAD + T - step], ALU.add))
                    src, dst, spare = dst, spare, dst
                    step *= 2
                window = step
                dve.scalar_tensor_tensor(out=mixed[:, g, PAD:], in0=src[:, 2 * PAD:], scalar=1.0 / window,
                                         in1=u[:, 2 * PAD:], op0=ALU.mult, op1=ALU.subtract)
                link(dve.tensor_tensor(mixed[:, g, 0:PAD], src[:, PAD:2 * PAD], inv_count[:, g, :], ALU.mult))
                dve.tensor_tensor(mixed[:, g, 0:PAD], mixed[:, g, 0:PAD], u[:, PAD:2 * PAD], ALU.subtract)\
                    .then_inc(st("ev_mixed"), 1)
            for pair in range(2):
                bank = unit_of("ev_pool", pair)
                for j in range(2):
                    g = 2 * pair + j
                    ins = dve.tensor_scalar(ev_oT[:, 4 + g, :], bank[:, j * T:(j + 1) * T],
                                            col["ev_pool_scale_2"][:, g:g + 1], None, ALU.mult)
                ins.then_inc(unit_free["v"], 1)

            def ds_out(h):
                if h % 2 == 1:
                    dve.wait_ge(st("ds_o"), h + 1)
                    dve.tensor_copy(ev_oT[:, h // 2, :], ps[:, (h // 2) % 2, 0:T]).then_inc(st("ds_out"), 1)

            softmax_heads("ds", HE, ev_bias_t, ds_out)
            add_y(2, False)

            def feed_forward(layer):
                for c in range(FC):
                    bank = unit_of(f"up{layer}", c)
                    dve.wait_ge(st("up_silu"), layer * FC + c + 1)
                    if c >= 8:
                        dve.wait_ge(pe_used, downs[layer, (c - 8) // 4])
                    dve.tensor_tensor(gated[:, c % 8, :], bank[:, T:2 * T], silu_a[:, c % 2, :], ALU.mult)\
                        .then_inc(unit_free["v"], 1)

            norm(3, [(hT, col["norm_ffn_g_2"][:, 0:8], None)])
            feed_forward(0)
            add_y(3, False)

            norm(4, [(hT, col["norm_mix_g_2"][:, 8:16], None)])
            for u in range(4):
                bank = unit_of("od_k", u)
                dve.tensor_copy(odk[:, 2 * u:2 * u + 2, :], bank.rearrange("p (h t) -> p h t", h=2))\
                    .then_inc(unit_free["v"], 1)
            for u in (1, 3):
                bank = unit_of("od_v", u)
                dve.tensor_copy(odv[:, 1, (u // 2) * HALF:(u // 2 + 1) * HALF], bank).then_inc(unit_free["v"], 1)
            for i in range(HO + 4):
                if i < HO:
                    dve.wait_ge(st("sb_ln"), i + 1)
                    if i >= 3:
                        dve.wait_ge(st("sb_log"), i - 2)
                    dve.scalar_tensor_tensor(out=sb_brk(i), in0=ps[:, 4 + i % 3, 0:S3], scalar=0.0, in1=sb_ln_t(i),
                                             op0=ALU.max, op1=ALU.add).then_inc(st("sb_soft"), 1)
                if i >= 4 and i % 2 == 1:
                    h = i - 4
                    dve.wait_ge(st("sb_o"), h + 1)
                    dve.tensor_copy(od_oT[:, h // 2, :], ps[:, (h // 2) % 2, 0:T]).then_inc(st("sb_out"), 1)
            add_y(4, False)
            norm(5, [(hT, col["norm_ffn_g_2"][:, 8:16], None)])
            feed_forward(1)
            add_y(5, False)


def shape_constants():
    p = np.arange(P)
    ident = np.eye(P)
    ones = np.ones((P, P))
    ones64 = (p[:, None] // HD2 == p[None, :] // HD2).astype(float)
    neg_after = -(p[:, None] >= p[None, :]).astype(float)
    t0 = np.where(p[None, :] <= p[:, None], 0.0, FAR)
    causal = np.concatenate([t0, np.zeros((P, P)), t0], axis=1)
    go = np.broadcast_to((np.arange(T) % CHUNK != 0).astype(float), (P, T))
    count = np.concatenate([1.0 / np.minimum(np.arange(1, 17), w) for w in (2, 4, 8, 16)])
    count = np.broadcast_to(count, (P, 64))
    const = np.concatenate([ident, ones, ones64, neg_after, -ones, causal, go, count], axis=1).astype(np.float32)
    m = ((p[:, None] // CHUNK == p[None, :] // CHUNK) & (p[:, None] <= p[None, :])).astype(np.int32)
    return np.ascontiguousarray(const), np.ascontiguousarray(np.concatenate([m, m], axis=1))


_INS = ["x", "c", "mod_w", "mod_b", "norm_g", "a_w_in", "a_lb_logits", "a_onorm_g", "a_w_out", "kv_mod_w", "kv_mod_b",
        "kv_norm_g", "kv_w", "kv_fb", "k_norm_g", "b_w_in", "b_q_norm_g", "b_w_out", "norm_mix_g_2", "norm_ffn_g_2",
        "ev_w_in_2", "ev_w_out_2", "ev_q_norm_g_2", "ev_k_norm_g_2", "ev_pool_w_2", "ev_pool_scale_2",
        "od_w_qkv_2", "od_w_out_2", "ffn_w1_2", "ffn_w3_2", "ffn_w2_2"]


def kernel(**inputs):
    import concourse.bacc as bacc
    from concourse.bass_utils import run_bass_kernel_spmd

    nc = bacc.Bacc("TRN2", target_bir_lowering=False, num_devices=1)
    arrays, views = {}, {}
    for name in _INS:
        v = np.ascontiguousarray(inputs[name])
        arrays[f"in_{name}"] = v
        views[name] = nc.dram_tensor(f"in_{name}", v.shape, mybir.dt.from_np(v.dtype), kind="ExternalInput").ap()
    const, mask = shape_constants()
    arrays["shape_constants"], arrays["shape_mask"] = const, mask
    c = nc.dram_tensor("shape_constants", const.shape, F32, kind="ExternalInput").ap()
    m = nc.dram_tensor("shape_mask", mask.shape, I32, kind="ExternalInput").ap()
    out = nc.dram_tensor("out", (1, T, D), F32, kind="ExternalOutput").ap()
    build(nc, views, c, m, out)
    r = run_bass_kernel_spmd(nc, [arrays], core_ids=[0])
    return r.results[0]["out"]
```

```python
from contextlib import ExitStack

import numpy as np

import concourse.bass as bass
from concourse import mybir
from concourse.alu_op_type import AluOpType as ALU

ACT = mybir.ActivationFunctionType
F32 = mybir.dt.float32
F32R = mybir.dt.float32r
I32 = mybir.dt.int32
X = mybir.AxisListType.X

P = 128
D = 1024
T = 256
NT = T // P
KD = D // P
W = 2048
HA = W // P
CHUNK = 64
NC = T // CHUNK
HALF = 512
FF = 2816
FC = FF // P
HD2 = 64
HE = 8
HIDX = 4
HO = 16
EV_COLS = 1604
TOPK = min(256, T // 4)
EPS = 1e-6
FAR = -1e30
LOW = -3e38
NRAW = 3
PIECE = 2048
NSPLIT = 4
PART = PIECE // 2
ARRAY = 4096
S3 = P + T
Q0, Q1 = slice(0, P), slice(P, S3)

VEC_A = [("c", 8), ("norm_g", 16), ("mod_b", 48), ("kv_norm_g", 8), ("kv_mod_b", 16),
         ("norm_mix_g_2", 16), ("norm_ffn_g_2", 16)]
VEC_B = [("a_lb_logits", 32), ("a_onorm_g", 16), ("ev_pool_scale_2", 4), ("k_norm_g", 1), ("b_q_norm_g", 1)]


def weight_pieces():
    pieces = [("mod", m, q) for m in range(4) for q in range(2)]
    mods = [(m, q) for m in range(4, 14) for q in range(2)]
    for n in range(32):
        pieces.append(("a_in", n))
        if n % 3 and mods:
            pieces.append(("mod", *mods.pop(0)))
    pieces += [("a_out", n) for n in range(8)]
    pieces += [("kv", n) for n in range(16)] + [("forget", 0)]
    mods = [(m, q) for m in (14, 15) for q in range(2)]
    for n in range(16):
        pieces.append(("b_in", n))
        if n % 3 and mods:
            pieces.append(("mod", *mods.pop(0)))
    pieces += [("b_out", n) for n in range(8)]
    pieces += [("ev_qi", 0), ("ev_small", 0), ("ev_kv", 0), ("ev_q", 0), ("ev_q", 1), ("ev_u", 0), ("ev_u", 1),
               ("pool_w", 0)]
    pieces += [("ev_out", n) for n in range(4)]

    def ffn(layer):
        order = []
        for i in range(FC // 2 + 2):
            if i < FC // 2:
                order += [("w1", layer, i), ("w3", layer, i)]
            if i >= 2:
                order.append(("w2", layer, i - 2))
        return order

    pieces += ffn(0)
    pieces += [("od_in", n) for n in range(12)] + [("od_out", n) for n in range(4)]
    pieces += ffn(1)
    return pieces


def units():
    out = []

    def add(stage, engines):
        out.extend((stage, e) for e in engines)

    add("norm0", "vvvv")
    add("a_f", "a" * 8)
    add("a_q", "v" * 8)
    add("a_g", "a" * 8)
    add("a_i", "a" * 8)
    add("norm1", "vvvv")
    add("k", "v" * 8)
    add("v", "a" * 8)
    add("forget", "v")
    add("q", "v" * 8)
    add("g", "a" * 8)
    add("norm2", "vvvv")
    add("ev_i", "aa")
    add("ev_k", "v")
    add("ev_v", "a")
    add("ev_q", "vv")
    add("ev_u", "aa")
    add("ev_pool", "vv")
    add("norm3", "vvvv")
    add("up0", "v" * FC)
    add("norm4", "vvvv")
    add("od_q", "aaaa")
    add("od_k", "vvvv")
    add("od_v", "avav")
    add("norm5", "vvvv")
    add("up1", "v" * FC)
    return out


def build(nc, a, const, mask, out):
    PIECES = weight_pieces()
    AT = {t: n for n, t in enumerate(PIECES)}
    UNITS = units()
    FIRST = {}
    for n, (s, _) in enumerate(UNITS):
        FIRST.setdefault(s, n)

    with ExitStack() as ctx:
        def sb(name, shape, dt=F32):
            return ctx.enter_context(nc.sbuf_tensor(name, shape, dt))

        def sem(name):
            return ctx.enter_context(nc.semaphore(name))

        raw = sb("raw_weights", [P, NRAW, PIECE])
        w_hi = sb("w_hi", [P, NSPLIT * PART], F32R)
        w_lo = sb("w_lo", [P, NSPLIT * PART], F32R)
        act_hi = sb("act_hi", [P, 16, T], F32R)
        act_lo = sb("act_lo", [P, 16, T], F32R)
        big = sb("big", [P, 5, ARRAY])
        x = sb("x", [P, NT, D])
        gate = sb("gate", [P, D])
        acc = sb("acc", [P, 2, HALF])
        cst = sb("cst", [P, const.shape[1]])
        att_mask = sb("att_mask", [P, 2, P], I32)
        cols = sb("cols", [P, 256])
        small = sb("small", [P, 256])
        work = sb("work", [P, 3584])

        ident, ones, ones64 = cst[:, 0:128], cst[:, 128:256], cst[:, 256:384]
        neg_after, neg_ones = cst[:, 384:512], cst[:, 512:640]
        causal = cst[:, 640:1024]
        chunk_go = cst[:, 1024:1280]
        inv_count = cst[:, 1280:1344].rearrange("p (g t) -> p g t", g=4)

        def grid(n, heads=HA):
            return big[:, n, 0:heads * T].rearrange("p (h t) -> p h t", h=heads)

        xn = big[:, 4, 0:NT * D].rearrange("p (t n) -> p t n", t=NT)
        SELF, KV = 0, KD

        at = 0
        col = {}
        for vecs, base in ((VEC_A, 0), (VEC_B, 128)):
            at = base
            for name, n in vecs:
                col[name] = cols[:, at:at + n]
                at += n
        ev_gain = cols[:, at:at + 2]

        silu_c = small[:, 0:8]
        one_m_lb, lb = small[:, 8:24], small[:, 24:40]
        lb_tmp = small[:, 40:56]
        scale0, shift0 = small[:, 56:64], small[:, 64:72]
        scale1, shift1 = small[:, 72:80], small[:, 80:88]
        scale_kv, shift_kv = small[:, 88:96], small[:, 96:104]
        ssum, rstd = small[:, 104:106], small[:, 106:108]
        q_gain = small[:, 108:109]
        ev_q_gain = small[:, 109:110]
        eps_t = small[:, 110:111]
        row_max, row_neg = small[:, 112:116], small[:, 116:120]
        row_sum, row_inv = small[:, 120:124], small[:, 124:128]
        dl = small[:, 128:192].rearrange("p (h n) -> p h n", h=HA)
        w_idx = small[:, 192:200]
        top8 = small[:, 200:208]
        cnt, rest = small[:, 208:209], small[:, 209:210]
        mod_tmp = small[:, 210:214]
        forget_b = small[0:HA, 214:215]

        ps = ctx.enter_context(nc.psum_tensor("ps", [P, 8, HALF], F32))

        def unit_bank(u):
            return ps[:, u % 4, :]

        def y_bank(t, n):
            return ps[:, 4 + 2 * t + n, :]

        loaded = [sem(f"raw{s}_loaded") for s in range(NRAW)]
        hi_done, lo_done = sem("half_hi_written"), sem("half_lo_written")
        pe_used, mod_summed = sem("half_used_by_pe"), sem("mod_piece_summed")
        h_hi, h_lo, h_used = sem("h_hi_written"), sem("h_lo_written"), sem("h_read")
        consts_in, rows_in, x_in, gate_b_in, out_stored = (sem(n) for n in (
            "consts_in", "rows_in", "x_in", "gate_bias_in", "out_stored"))
        fb_in = sem("forget_bias_in")
        rows_turned, cols_ready = sem("rows_turned"), sem("cols_ready")
        silu_c_ready = sem("silu_c_ready")
        unit_ready = sem("unit_ready")
        unit_free = {"a": sem("unit_read_by_act"), "v": sem("unit_read_by_dve")}
        mod_cols, mod_read = sem("mod_cols_ready"), sem("mod_cols_read")
        x_done, sq_done, rstd_done, xn_done = sem("x_done"), sem("x_squares_done"), sem("x_rstd_done"), sem("xn_done")
        y_ready = sem("y_ready")
        act_chain, dve_chain, pool_chain = sem("act_step"), sem("dve_step"), sem("pool_step")

        def before(engine, u):
            return sum(1 for _, e in UNITS[:u + 1] if e == engine)

        def wait_loaded(eng, n):
            eng.wait_ge(loaded[n % NRAW], 16 * (n // NRAW + 1))

        def slot(n):
            return raw[:, n % NRAW, :]

        def by_k(v, k=KD):
            return v.rearrange("p (k n) -> p k n", k=k)

        HALVES, first_half = [], {}

        def add_half(n, src, dst):
            HALVES.append((n, at_slot[0] % NSPLIT, src, dst))
            at_slot[0] += 1

        at_slot = [0]
        for n, piece in enumerate(PIECES):
            kind = piece[0]
            first_half[n] = len(HALVES)
            if kind in ("mod", "pool_w"):
                continue
            if kind in ("a_out", "b_out", "ev_out", "od_out", "w2"):
                for j in range(2):
                    add_half(n, by_k(slot(n), 2)[:, j, :], lambda v: v)
            elif kind == "forget":
                src = by_k(slot(n)[:, 0:KD * HA]).rearrange("p k (a n) -> p k a n", a=1)
                add_half(n, src.to_broadcast([P, KD, 8, HA]), lambda v: v.rearrange("p (k a n) -> p k a n", k=KD, a=8))
            elif kind == "ev_small":
                w = by_k(slot(n)[:, 0:KD * 68])
                src = w[:, :, 0:HD2].rearrange("p k (a n) -> p k a n", a=1)
                add_half(n, src.to_broadcast([P, KD, 2, HD2]), lambda v: v.rearrange("p (k a n) -> p k a n", k=KD, a=2))
                add_half(n, w[:, :, 64:68], lambda v: by_k(v[:, 0:KD * 4]))
            elif kind == "ev_kv":
                w = by_k(slot(n))
                for g in range(2):
                    src = w[:, :, g * HD2:(g + 1) * HD2].rearrange("p k (a n) -> p k a n", a=1)
                    add_half(n, src.to_broadcast([P, KD, 2, HD2]),
                             lambda v: v.rearrange("p (k a n) -> p k a n", k=KD, a=2))
                add_half(n, w[:, :, P:2 * P], by_k)
            elif kind == "a_in" and piece[1] >= 24 or kind == "kv" and piece[1] >= 8 or kind == "od_in" and piece[1] >= 8:
                at_slot[0] += at_slot[0] % 2
                for j in range(2):
                    add_half(n, by_k(slot(n))[:, :, j * P:(j + 1) * P], ("pair", j))
            else:
                for j in range(2):
                    add_half(n, by_k(slot(n))[:, :, j * P:(j + 1) * P], by_k)
        first_half[len(PIECES)] = len(HALVES)

        def half_view(tensor, s):
            place, dst = HALVES[s][1], HALVES[s][3]
            if isinstance(dst, tuple):
                pair = by_k(tensor[:, (place - dst[1]) * PART:(place - dst[1] + 2) * PART])
                return pair[:, :, dst[1] * P:(dst[1] + 1) * P]
            return dst(tensor[:, place * PART:(place + 1) * PART])

        def half_flat(tensor, s):
            place = HALVES[s][1]
            return tensor[:, place * PART:(place + 1) * PART]

        def previous_in(s):
            return next((r for r in range(s - 1, -1, -1) if HALVES[r][1] == HALVES[s][1]), None)

        def wait_read(eng, stage, i):
            u = FIRST[stage] + i
            eng.wait_ge(unit_free[UNITS[u][1]], before(UNITS[u][1], u))

        half_use = {}
        unit_half = {}
        raw_use = {}
        for n, piece in enumerate(PIECES):
            if piece[0] == "mod":
                raw_use[n] = (mod_summed, sum(1 for p in PIECES[:n + 1] if p[0] == "mod"))
            elif piece[0] != "pool_w":
                raw_use[n] = (lo_done, first_half[n + 1])

        chain = {"act": 0, "dve": 0, "pool": 0}

        def then(eng_name, eng, ins):
            s = {"act": act_chain, "dve": dve_chain, "pool": pool_chain}[eng_name]
            chain[eng_name] += 1
            ins.then_inc(s, 1)
            eng.wait_ge(s, chain[eng_name])

        S = {}

        def st(name):
            if name not in S:
                S[name] = sem(name)
            return S[name]

        for name in ("gate_sig_in sig_ready ln_ready scan_ready exp_ready spread_ready spread_exp kin_ready "
                     "out_hi ot_split fx_split ds_split sb_split kst_turned kst_copied att_ready att_masked state_ready state_saved o_ready "
                     "osq_ready ossq_ready orstd_ready o_used ot_ready "
                     "hsq_ready hssq_ready hrstd_ready "
                     "f_min f_ln nf_ready "
                     "fx_logits fx_max fx_exp fx_prob fx_turned fx_tcopied fx_o fx_out "
                     "ev_rel ev_relu ev_score_used "
                     "ev_mixed "
                     "ds_logits ds_max ds_exp ds_prob ds_turned ds_tcopied ds_o ds_out "
                     "up_silu g_full g_hi sb_z sb_ln sb_soft sb_masked sb_log sb_exp sb_sel sb_o sb_out"
                     ).split():
            st(name)

        a_in_at = [2048, 0, 6144, 4096]

        def col_tile(w, c0, n):
            return w.rearrange("(k p) n -> p k n", p=P)[:, :, c0:c0 + n]

        def row_tile(w, k0, nk):
            return w[k0 * P:(k0 + nk) * P, :].rearrange("(k p) n -> p k n", p=P)

        def piece_dma(n):
            kind, i = PIECES[n][0], PIECES[n][-1]
            s = slot(n)
            wide, rows = by_k(s), by_k(s, 2)
            if kind == "mod":
                m = PIECES[n][1]
                w, j = (a["mod_w"][0], m) if m < 6 else (a["mod_w"][1], m - 6) if m < 10 else \
                       (a["kv_mod_w"], m - 10) if m < 14 else (a["mod_w"][1], m - 10)
                return by_k(s, 4), row_tile(w, 4 * i, 4)[:, :, HALF * j:HALF * (j + 1)]
            if kind == "a_in":
                return wide, col_tile(a["a_w_in"][0], a_in_at[i // 8] + T * (i % 8), T)
            if kind == "kv":
                return wide, col_tile(a["kv_w"], T * i, T)
            if kind == "forget":
                return by_k(s[:, 0:KD * HA]), col_tile(a["kv_w"], 2 * W, HA)
            if kind == "b_in":
                return wide, col_tile(a["b_w_in"][0], T * i, T)
            if kind == "ev_small":
                return by_k(s[:, 0:KD * 68]), col_tile(a["ev_w_in_2"][0], 1024, 68)
            if kind in ("ev_qi", "ev_kv", "ev_q", "ev_u"):
                c0 = {"ev_qi": 768, "ev_kv": 512, "ev_q": T * i, "ev_u": 1092 + T * i}[kind]
                return wide, col_tile(a["ev_w_in_2"][0], c0, T)
            if kind == "pool_w":
                return by_k(s[:, 0:4 * P], 4), a["ev_pool_w_2"][0].rearrange("g c d -> c g d")
            if kind == "od_in":
                return wide, col_tile(a["od_w_qkv_2"][0], T * i, T)
            if kind in ("a_out", "b_out", "ev_out", "od_out"):
                w = {"a_out": "a_w_out", "b_out": "b_w_out", "ev_out": "ev_w_out_2", "od_out": "od_w_out_2"}[kind]
                return rows, row_tile(a[w][0], 2 * i, 2)
            layer = PIECES[n][1]
            if kind in ("w1", "w3"):
                return wide, col_tile(a[f"ffn_{kind}_2"][layer], T * i, T)
            return rows, row_tile(a["ffn_w2_2"][layer], 2 * i, 2)

        fz_b, k_in0, q_dec, k_in, k_st = (grid(n) for n in range(5))
        silu_g = grid(0)
        v_rows = big[:, 1, :].rearrange("p (t n) -> p t n", t=NT)
        kst_sb = work[:, 0:512].rearrange("p (b t k) -> p b t k", b=2, t=2)
        att_sb = work[:, 512:1024].rearrange("p (b t c) -> p b t c", b=2, t=2)
        state = work[:, 1024:1792].rearrange("p (b n v) -> p b n v", b=2, n=3)
        o_sq = work[:, 1792:2304].rearrange("p (b t) -> p b t", b=2)
        o_r = work[:, 2304:2816].rearrange("p (b t) -> p b t", b=2)
        o_tmp = work[:, 2816:3072]
        o_full = work[:, 3072:3584].rearrange("p (b t) -> p b t", b=2)
        h_full = work[:, 2560:3584].rearrange("p (b n) -> p b n", b=2)

        kN, v2_rows, qN, silu_g2 = grid(0), big[:, 1, :].rearrange("p (t n) -> p t n", t=NT), grid(2), grid(3)
        h_sq = work[:, 0:1024].rearrange("p (b n) -> p b n", b=2)
        h_r = work[:, 1024:2048].rearrange("p (b n) -> p b n", b=2)
        f_a, f_b = work[0:HA, 2048:2048 + T], work[0:HA, 2304:2304 + T]
        neg_f = work[0:HA, 2688:2688 + T]
        lg = work[:, 0:2 * S3].rearrange("p (b n) -> p b n", b=2)
        prob = work[:, 768:768 + 3 * S3].rearrange("p (b n) -> p b n", b=3)
        probT = work[:, 1920:1920 + 2 * S3].rearrange("p (b n) -> p b n", b=2)

        evq = big[:, 0, 0:1024].rearrange("p (c t) -> p c t", c=4)
        evk = big[:, 0, 1024:1536].rearrange("p (g t) -> p g t", g=2)
        evqi = big[:, 0, 1536:2048].rearrange("p (c t) -> p c t", c=2)
        evki = big[:, 0, 2048:2304]
        evv = big[:, 0, 2304:2560].rearrange("p (t d) -> p t d", t=2)
        PAD = 16
        u_pad = big[:, 1, 0:4 * (PAD + T)].rearrange("p (g t) -> p g t", g=4)
        run_a = big[:, 1, 1088:1088 + PAD + T]
        run_b = big[:, 1, 1360:1360 + PAD + T]
        mixed = big[:, 1, 1632:1632 + 4 * T].rearrange("p (g t) -> p g t", g=4)
        pooled = big[:, 1, 2656:2656 + 4 * T].rearrange("p (g t) -> p g t", g=4)
        score = big[:, 3, 0:S3]
        relu_s = big[:, 3, 384:384 + 2 * S3].rearrange("p (b n) -> p b n", b=2)
        cut = big[:, 3, 1152:1152 + T]
        sel_gt = big[:, 3, 1536:1536 + T]
        sel_eq = big[:, 3, 1792:1792 + T]
        sel_pre = big[:, 3, 2048:2048 + T]
        ev_bias_t = big[:, 3, 2304:2304 + S3]
        OUT2 = 8

        silu_a = work[:, 0:512].rearrange("p (b t) -> p b t", b=2)
        g_full = work[:, 512:1024].rearrange("p (b t) -> p b t", b=2)

        odq, odk = grid(0, 8), big[:, 0, 2048:4096].rearrange("p (h t) -> p h t", h=8)
        odv = big[:, 1, 0:2048].rearrange("p (t n) -> p t n", t=NT)

        def sb_ln_t(i):
            return work[:, (i % 2) * S3:(i % 2) * S3 + S3]

        def sb_brk(i):
            return work[:, (2 + i % 3) * S3:(2 + i % 3) * S3 + S3]

        def sb_prob(i):
            return work[:, (5 + i % 3) * S3:(5 + i % 3) * S3 + S3]

        block = ctx.enter_context(nc.Block())

        vec_rows = [work[:, 0:P], work[:, P:2 * P]]

        @block.gpsimd
        def _(pool):
            pool.memset(vec_rows[1], 0.0).then_inc(pool_chain, 1)
            pool.wait_ge(pool_chain, 1)
            for vecs, rows in ((VEC_A, vec_rows[0]), (VEC_B, vec_rows[1])):
                r = 0
                for name, n in vecs:
                    src = a[name]
                    if len(src.shape) == 2:
                        src = src.rearrange("a b -> (a b)")
                    pool.dma_start(rows[r:r + n, :], src.rearrange("(r c) -> r c", c=P)).then_inc(rows_in, 16)
                    r += n
            for i, name in enumerate(("ev_q_norm_g_2", "ev_k_norm_g_2")):
                for half in range(2):
                    pool.dma_start(vec_rows[1][r + i:r + i + 1, HD2 * half:HD2 * (half + 1)], a[name]).then_inc(rows_in, 16)
            pool.dma_start(x[:, :, :], a["x"][0].rearrange("(t p) n -> p t n", p=P)).then_inc(x_in, 16)
            pool.dma_start(forget_b, a["kv_fb"].rearrange("(h a) -> h a", a=1)).then_inc(fb_in, 16)
            pool.dma_start(gate[:, :], a["mod_b"][0:1, 2 * D:3 * D].to_broadcast([P, D])).then_inc(gate_b_in, 16)

            def split_output(i, full, done, freed, chunk):
                pool.wait_ge(done, i + 1)
                pool.tensor_copy(act_hi[:, chunk, :], full).then_inc(st("out_hi"), 1)
                outs[0] += 1
                pool.wait_ge(st("out_hi"), outs[0])
                pool.tensor_tensor(act_lo[:, chunk, :], full, act_hi[:, chunk, :].bitcast(F32), ALU.subtract)\
                    .then_inc(freed, 1)

            outs = [0]
            for h in range(HA):
                split_output(h, o_full[:, h % 2, :], st("ot_ready"), st("ot_split"), h)
            pool.wait_ge(x_done, 4)
            pool.dma_start(gate[:, :], a["mod_b"][1:2, 2 * D:3 * D].to_broadcast([P, D])).then_inc(gate_b_in, 16)
            for h in range(HA):
                split_output(h, o_full[:, h % 2, :], st("fx_out"), st("fx_split"), h)
            for c in range(HE // 2):
                split_output(c, o_full[:, c % 2, :], st("ds_out"), st("ds_split"), OUT2 + c)

            for i in range(HO + 5):
                if i >= 5 and i % 2 == 1:
                    c = (i - 5) // 2
                    split_output(c, o_full[:, c % 2, :], st("sb_out"), st("sb_split"), OUT2 + c)
                if i < HO:
                    pool.wait_ge(st("sb_soft"), i + 1)
                    part = sb_brk(i).rearrange("p (b t) -> p b t", b=3)[:, 0:3:2, :]
                    pool.affine_select(out=part, in_=part, compare_op=ALU.is_gt, fill=0.0, base=0,
                                       pattern=[[0, 2], [1, P]], channel_multiplier=-1).then_inc(st("sb_masked"), 1)
                if 1 <= i <= HO:
                    pool.wait_ge(st("sb_exp"), i)
                    part = sb_prob(i - 1).rearrange("p (b t) -> p b t", b=3)[:, 0:3:2, :]
                    pool.affine_select(out=part, in_=part, compare_op=ALU.is_gt, fill=0.0, base=0,
                                       pattern=[[0, 2], [1, P]], channel_multiplier=-1).then_inc(st("sb_sel"), 1)

        NVEC = len(VEC_A) + len(VEC_B) + 4

        down_half = {}

        @block.tensor
        def _(pe):
            unit = [0]

            def open_unit(stage):
                u = unit[0]
                assert UNITS[u][0] == stage, (u, UNITS[u], stage)
                if u >= 4:
                    pe.wait_ge(unit_free[UNITS[u - 4][1]], before(UNITS[u - 4][1], u - 4))
                unit[0] += 1
                return unit_bank(u)

            def feature_major(dst, w, h):
                for k in range(KD):
                    ins = pe.matmul(dst, w(k), h[:, k, :], start=(k == 0), stop=(k == KD - 1))
                return ins

            def token_major(dst, h, t, w):
                for k in range(KD):
                    ins = pe.matmul(dst, h[:, k, t * P:(t + 1) * P], w(k), start=(k == 0), stop=(k == KD - 1))
                return ins

            def project_features(stage, n, h):
                wait_loaded(pe, n)
                w = slot(n).rearrange("p (k n) -> p k n", k=KD)
                for pair in range(2):
                    bank = open_unit(stage)
                    for j in range(2):
                        c = (2 * pair + j) * P
                        ins = feature_major(bank[:, j * T:(j + 1) * T], lambda k: w[:, k, c:c + P], h)
                    ins.then_inc(unit_ready, 1)
                    if pair == 1:
                        used(n)
                    yield pair

            halves_used, y_count, half, lo_waits = [0], [0], [0], [0]

            def used(s, ins=None):
                if ins is None:
                    half_use[s] = (unit_ready, unit[0])
                else:
                    halves_used[0] += 1
                    ins.then_inc(pe_used, 1)
                    half_use[s] = (pe_used, halves_used[0])

            def next_half(kind):
                s = half[0]
                assert PIECES[HALVES[s][0]][0] == kind, (PIECES[HALVES[s][0]], kind)
                half[0] += 1
                pe.wait_ge(hi_done, s + 1)
                return s

            def wait_lo(s):
                pe.wait_ge(lo_done, s + 1)

            def close_unit(ins, s):
                ins.then_inc(unit_ready, 1)
                unit_half[unit[0] - 1] = s

            def features(dst, s, base, waits=None):
                wh, wl = by_k(half_flat(w_hi, s)), by_k(half_flat(w_lo, s))
                for k in range(KD):
                    if waits is not None and k % 2 == 0:
                        pe.wait_ge(h_lo, waits + k // 2 + 1)
                    pe.matmul(dst, wh[:, k, :], act_hi[:, base + k, :], start=(k == 0), stop=False)
                    pe.matmul(dst, wh[:, k, :], act_lo[:, base + k, :], start=False, stop=False)
                wait_lo(s)
                for k in range(KD):
                    ins = pe.matmul(dst, wl[:, k, :], act_hi[:, base + k, :], start=False, stop=(k == KD - 1))
                return ins

            def project_features(stage, kind, base, waits=None):
                bank = open_unit(stage)
                s = next_half(kind)
                used(s, features(bank[:, 0:T], s, base, waits))
                s = next_half(kind)
                close_unit(features(bank[:, T:2 * T], s, base), s)
                used(s)

            def project_tokens(stage, kind, base):
                banks = [open_unit(stage) for _ in range(NT)]
                for piece in range(2):
                    s = next_half(kind)
                    s2 = next_half(kind)
                    assert HALVES[s][1] % 2 == 0
                    place = HALVES[s][1]
                    wh = by_k(w_hi[:, place * PART:(place + 2) * PART])
                    wl = by_k(w_lo[:, place * PART:(place + 2) * PART])
                    out_cols = slice(piece * T, (piece + 1) * T)
                    for t in range(NT):
                        dst, tok = banks[t][:, out_cols], slice(t * P, (t + 1) * P)
                        for k in range(KD):
                            pe.matmul(dst, act_hi[:, base + k, tok], wh[:, k, :], start=(k == 0), stop=False)
                            pe.matmul(dst, act_lo[:, base + k, tok], wh[:, k, :], start=False, stop=False)
                        if t == 0:
                            wait_lo(s2)
                        for k in range(KD):
                            ins = pe.matmul(dst, act_hi[:, base + k, tok], wl[:, k, :], start=False, stop=(k == KD - 1))
                        if piece == 1:
                            ins.then_inc(unit_ready, 1)
                            unit_half[unit[0] - 2 + t] = s2
                    if piece == 0:
                        used(s, ins)
                        half_use[s2] = half_use[s]
                    else:
                        used(s)
                        used(s2)

            def out_half(kind, chunk, first, last):
                s = next_half(kind)
                wh, wl = half_flat(w_hi, s), half_flat(w_lo, s)
                parts = [(y_bank(t, n), slice(t * P, (t + 1) * P), slice(n * HALF, (n + 1) * HALF))
                         for t in range(NT) for n in range(2)]
                for dst, tok, cols_ in parts:
                    pe.matmul(dst, act_hi[:, chunk, tok], wh[:, cols_], start=first, stop=False)
                    pe.matmul(dst, act_lo[:, chunk, tok], wh[:, cols_], start=False, stop=False)
                wait_lo(s)
                for dst, tok, cols_ in parts:
                    ins = pe.matmul(dst, act_hi[:, chunk, tok], wl[:, cols_], start=False, stop=last)
                    if last:
                        ins.then_inc(y_ready, 1)
                if last:
                    y_count[0] += 4
                    half_use[s] = (y_ready, y_count[0])
                else:
                    used(s, ins)
                return s

            def out_project(kind, chunks, base, ready=None):
                for k in range(chunks):
                    if ready is not None:
                        ready(k)
                    out_half(kind, base + k, k == 0, k == chunks - 1)

            def norm(j):
                for u in range(4):
                    bank = open_unit(f"norm{j}")
                    pe.wait_ge(xn_done, 2 * (j + 1))
                    for kk in range(2):
                        for t in range(NT):
                            k = 2 * u + kk
                            ins = pe.transpose(bank[:, kk * T + t * P:kk * T + (t + 1) * P],
                                               xn[:, t, k * P:(k + 1) * P], ident)
                    close_unit(ins, half[0] - 1)

            def mod_columns(m):
                pe.wait_ge(mod_summed, 2 * (m + 1))
                if m >= 2:
                    pe.wait_ge(mod_read, m - 1)
                bank = ps[:, 6 + m % 2, :]
                if m in (4, 5, 14, 15):
                    ins = pe.matmul(bank, ones, acc[:, m % 2, :], start=True, stop=True)
                else:
                    for c in range(4):
                        ins = pe.matmul(bank[:, c:c + 1], acc[:, m % 2, c * P:(c + 1) * P], ones[:, 0:1],
                                        start=True, stop=True)
                ins.then_inc(mod_cols, 1)

            pe.wait_ge(consts_in, 32)
            pe.wait_ge(rows_in, 16 * NVEC)
            for i in range(2):
                ins = pe.transpose(ps[:, 4, i * P:(i + 1) * P], vec_rows[i], ident)
            ins.then_inc(rows_turned, 1)
            for m in range(4):
                mod_columns(m)
            norm(0)

            mod_end = {}
            for n, piece in enumerate(PIECES):
                if piece[0] == "mod" and piece[1] >= 4 and piece[2] == 1:
                    k = next(r for r in PIECES[n:] if r[0] in ("a_in", "b_in"))
                    mod_end.setdefault(k, []).append(piece[1])
            for n in range(24):
                project_features(("a_f", "a_q", "a_g")[n // 8], "a_in", SELF, 0 if n == 0 else None)
                for m in mod_end.get(("a_in", n), ()):
                    mod_columns(m)
            for n in range(24, 32, 2):
                project_tokens("a_i", "a_in", SELF)
                for m in mod_end.get(("a_in", n), []) + mod_end.get(("a_in", n + 1), []):
                    mod_columns(m)

            def keys_turned(h):
                pe.wait_ge(st("kin_ready"), 2 * (h + 1))
                if h >= 2:
                    pe.wait_ge(st("kst_copied"), h - 1)
                for t in range(NT):
                    ins = pe.transpose(ps[:, 6 + h % 2, t * P:(t + 1) * P],
                                       k_st[:, h, t * P:(t + 1) * P], ident)
                ins.then_inc(st("kst_turned"), 1)

            def scores(h):
                wait_read(pe, "a_q", h // 2)
                if h >= 2:
                    pe.wait_ge(st("att_masked"), h - 1)
                for t in range(NT):
                    sl = slice(t * P, (t + 1) * P)
                    ins = pe.matmul(ps[:, 4 + h % 2, sl], k_in[:, h, sl], q_dec[:, h, sl], start=True, stop=True)
                ins.then_inc(st("att_ready"), 1)

            def states(h):
                pe.wait_ge(st("kst_copied"), h + 1)
                if h >= 1:
                    pe.wait_ge(st("state_saved"), h)
                for n in range(NC - 1):
                    rows = slice(CHUNK * (n % 2), CHUNK * (n % 2) + CHUNK)
                    ins = pe.matmul(ps[:, n % 2, n * P:(n + 1) * P], kst_sb[rows, h % 2, n // 2, :],
                                    v_rows[rows, n // 2, h * P:(h + 1) * P], start=True, stop=True)
                ins.then_inc(st("state_ready"), 1)

            def outputs(h):
                pe.wait_ge(st("att_masked"), h + 1)
                pe.wait_ge(st("state_saved"), h + 1)
                if h >= 2:
                    pe.wait_ge(st("o_used"), h - 1)
                bank = ps[:, 2 + h % 2, :]
                for t in range(NT):
                    pe.matmul(bank[:, t * P:(t + 1) * P], v_rows[:, t, h * P:(h + 1) * P], att_sb[:, h % 2, t, :],
                              start=True, stop=False)
                    for n in range(max(1, 2 * t), 2 * t + 2):
                        sl = slice(n * CHUNK, (n + 1) * CHUNK)
                        ins = pe.matmul(bank[:, sl], state[:, h % 2, n - 1, :], q_dec[:, h, sl],
                                        start=False, stop=(n == 2 * t + 1))
                ins.then_inc(st("o_ready"), 1)

            def square_sums(h):
                pe.wait_ge(st("osq_ready"), h + 1)
                pe.matmul(ps[:, 2 + h % 2, T:2 * T], ones, o_sq[:, h % 2, :], start=True, stop=True)\
                    .then_inc(st("ossq_ready"), 1)

            pe.wait_ge(unit_free["a"], before("a", unit[0] - 1))
            pe.wait_ge(unit_free["v"], before("v", unit[0] - 1))
            pe.wait_ge(mod_read, 14)
            for i in range(HA + 3):
                if i < HA:
                    keys_turned(i)
                    scores(i)
                if 1 <= i <= HA:
                    states(i - 1)
                if 2 <= i <= HA + 1:
                    outputs(i - 2)
                if i >= 3:
                    square_sums(i - 3)
            pe.wait_ge(st("o_used"), HA)
            out_project("a_out", HA, 0, lambda k: pe.wait_ge(st("ot_split"), k + 1))

            norm(1)

            def head_square_sums(mat, count):
                pe.wait_ge(st("hsq_ready"), count + 1)
                if count >= 2:
                    pe.wait_ge(st("hrstd_ready"), count - 1)
                pe.matmul(ps[:, 4 + count % 2, :], mat, h_sq[:, count % 2, :], start=True, stop=True)\
                    .then_inc(st("hssq_ready"), 1)

            pe.wait_ge(x_done, 4)
            for n in range(8):
                project_features("k", "kv", KV, 4 if n == 0 else None)
                if n >= 1:
                    head_square_sums(ones, n - 1)
            for n in range(4):
                project_tokens("v", "kv", KV)
                if n == 0:
                    head_square_sums(ones, 7)
            bank = open_unit("forget")
            s = next_half("forget")
            close_unit(features(bank[:, 0:T], s, KV), s)
            used(s)
            for n in range(16):
                project_features("q" if n < 8 else "g", "b_in", SELF, 8 if n == 0 else None)
                if 1 <= n <= 8:
                    head_square_sums(ones, 8 + n - 1)
                for m in mod_end.get(("b_in", n), ()):
                    mod_columns(m)

            def softmax_heads(pre, heads, logits, pv):
                for i in range(heads + 3):
                    if i < heads:
                        if i >= 2:
                            pe.wait_ge(st(pre + "_max"), i - 1)
                        logits(i, ps[:, 4 + i % 2, :]).then_inc(st(pre + "_logits"), 1)
                    if 2 <= i < heads + 2:
                        h = i - 2
                        pe.wait_ge(st(pre + "_prob"), h + 1)
                        if h >= 2:
                            pe.wait_ge(st(pre + "_tcopied"), h - 1)
                        for b in range(3):
                            ins = pe.transpose(ps[:, 6 + h % 2, b * P:(b + 1) * P], prob[:, h % 3, b * P:(b + 1) * P], ident)
                        ins.then_inc(st(pre + "_turned"), 1)
                    if i >= 3:
                        h = i - 3
                        pe.wait_ge(st(pre + "_tcopied"), h + 1)
                        pv(h)

            def fox_logits(h, bank):
                if h % 2 == 0:
                    wait_read(pe, "q", h // 2)
                if h == 0:
                    pe.wait_ge(st("nf_ready"), 1)
                one = ident[0:HA, h:h + 1].to_broadcast([HA, P])
                for t in range(NT):
                    o = bank[:, P * t:P * t + P * (t + 1)]
                    pe.matmul(o, qN[:, h, t * P:(t + 1) * P], kN[:, h, 0:P * (t + 1)], start=True, stop=False)
                    ins = pe.matmul(o, one, neg_f[:, 0:P * (t + 1)], start=False, stop=True)
                return ins

            def fox_pv(h):
                if h >= 2:
                    pe.wait_ge(st("fx_out"), h - 1)
                bank = ps[:, h % 2, :]
                vh = lambda s: v2_rows[:, s, h * P:(h + 1) * P]
                pe.matmul(bank[:, 0:P], vh(0), probT[:, h % 2, 0:P], start=True, stop=True)
                pe.matmul(bank[:, P:T], vh(0), probT[:, h % 2, P:2 * P], start=True, stop=False)
                pe.matmul(bank[:, P:T], vh(1), probT[:, h % 2, 2 * P:3 * P], start=False, stop=True)\
                    .then_inc(st("fx_o"), 1)

            pe.wait_ge(unit_free["a"], before("a", unit[0] - 1))
            pe.wait_ge(unit_free["v"], before("v", unit[0] - 1))
            pe.wait_ge(mod_read, 16)
            pe.wait_ge(st("hrstd_ready"), 16)
            softmax_heads("fx", HA, fox_logits, fox_pv)
            out_project("b_out", HA, 0, lambda k: pe.wait_ge(st("fx_split"), k + 1))

            norm(2)
            count = 16
            project_features("ev_i", "ev_qi", SELF, 12)
            bank = open_unit("ev_i")
            s = next_half("ev_small")
            used(s, features(bank[:, 0:T], s, SELF))
            s = next_half("ev_small")
            wh, wl = (by_k(half_flat(w, s)[:, 0:KD * 4]) for w in (w_hi, w_lo))
            wait_lo(s)
            for t in range(NT):
                dst, tok = bank[:, T + 4 * t:T + 4 * t + 4], slice(t * P, (t + 1) * P)
                for k in range(KD):
                    pe.matmul(dst, act_hi[:, k, tok], wh[:, k, :], start=(k == 0), stop=False)
                    pe.matmul(dst, act_lo[:, k, tok], wh[:, k, :], start=False, stop=False)
                    ins = pe.matmul(dst, act_hi[:, k, tok], wl[:, k, :], start=False, stop=(k == KD - 1))
            close_unit(ins, s)
            used(s)
            pe.wait_ge(x_done, 8)
            bank = open_unit("ev_k")
            s = next_half("ev_kv")
            used(s, features(bank[:, 0:T], s, SELF))
            wait_read(pe, "ev_i", 1)
            for h in range(HIDX):
                rows = slice(HD2 * (h % 2), HD2 * (h % 2) + HD2)
                for t in range(NT):
                    ins = pe.matmul(ps[:, 4 + h, P * t:P * t + P * (t + 1)], evqi[rows, h // 2, t * P:(t + 1) * P],
                                    evki[rows, 0:P * (t + 1)], start=True, stop=True)
                ins.then_inc(st("ev_rel"), 1)
            s = next_half("ev_kv")
            close_unit(features(bank[:, T:2 * T], s, SELF), s)
            used(s)
            bank = open_unit("ev_v")
            s = next_half("ev_kv")
            wh, wl = by_k(half_flat(w_hi, s)), by_k(half_flat(w_lo, s))
            wait_lo(s)
            for t in range(NT):
                dst, tok = bank[:, t * P:(t + 1) * P], slice(t * P, (t + 1) * P)
                for k in range(KD):
                    pe.matmul(dst, act_hi[:, k, tok], wh[:, k, :], start=(k == 0), stop=False)
                    pe.matmul(dst, act_lo[:, k, tok], wh[:, k, :], start=False, stop=False)
                    ins = pe.matmul(dst, act_hi[:, k, tok], wl[:, k, :], start=False, stop=(k == KD - 1))
            close_unit(ins, s)
            used(s)
            pe.wait_ge(st("ev_relu"), HIDX)
            head_square_sums(ones64, 16)
            project_features("ev_q", "ev_q", SELF)
            project_features("ev_q", "ev_q", SELF)
            head_square_sums(ones64, 17)
            project_features("ev_u", "ev_u", SELF)
            head_square_sums(ones64, 18)
            project_features("ev_u", "ev_u", SELF)
            n = AT[("pool_w", 0)]
            wait_loaded(pe, n)
            wp = by_k(slot(n)[:, 0:4 * P], 4)
            for pair in range(2):
                bank = open_unit("ev_pool")
                for j in range(2):
                    g = 2 * pair + j
                    pe.wait_ge(st("ev_mixed"), g + 1)
                    ins = pe.matmul(bank[:, j * T:(j + 1) * T], wp[:, g, :], mixed[:, g, :], start=True, stop=True)
                close_unit(ins, half[0] - 1)
            raw_use[n] = (unit_ready, unit[0])

            def ds_logits(h, bank):
                if h == 0:
                    wait_read(pe, "ev_q", 1)
                rows = slice(HD2 * (h % 2), HD2 * (h % 2) + HD2)
                for t in range(NT):
                    ins = pe.matmul(bank[:, P * t:P * t + P * (t + 1)], evq[rows, h // 2, t * P:(t + 1) * P],
                                    evk[rows, h // 4, 0:P * (t + 1)], start=True, stop=True)
                return ins

            def ds_pv(h):
                if h % 2 == 0 and h >= 4:
                    pe.wait_ge(st("ds_out"), h // 2 - 1)
                rows = slice(HD2 * (h % 2), HD2 * (h % 2) + HD2)
                bank = ps[rows, (h // 2) % 2, :]
                vh = lambda s: evv[:, s, HD2 * (h // 4):HD2 * (h // 4) + HD2]
                pe.matmul(bank[:, 0:P], vh(0), probT[:, h % 2, 0:P], start=True, stop=True)
                pe.matmul(bank[:, P:T], vh(0), probT[:, h % 2, P:2 * P], start=True, stop=False)
                pe.matmul(bank[:, P:T], vh(1), probT[:, h % 2, 2 * P:3 * P], start=False, stop=True)\
                    .then_inc(st("ds_o"), 1)

            pe.wait_ge(unit_free["a"], before("a", unit[0] - 1))
            pe.wait_ge(unit_free["v"], before("v", unit[0] - 1))
            softmax_heads("ds", HE, ds_logits, ds_pv)
            wait_read(pe, "ev_pool", 1)
            out_project("ev_out", 8, OUT2, lambda k: pe.wait_ge(st("ds_split"), k + 1) if k < 4 else None)

            def feed_forward(layer, xs, waits):
                def up(i):
                    banks = [open_unit(f"up{layer}") for _ in range(2)]
                    for j in range(2):
                        s = next_half("w1")
                        used(s, features(banks[j][:, 0:T], s, SELF, waits if i == 0 and j == 0 else None))
                    for j in range(2):
                        s = next_half("w3")
                        features(banks[j][:, T:2 * T], s, SELF).then_inc(unit_ready, 1)
                        half_use[s] = (unit_ready, unit[0] - 1 + j)
                        unit_half[unit[0] - 2 + j] = s

                def down(i):
                    if i == 0:
                        pe.wait_ge(x_done, xs)
                    for c in (2 * i, 2 * i + 1):
                        wait_read(pe, f"up{layer}", c)
                        down_half[layer, c] = out_half("w2", 8 + c % 8, c == 0, c == FC - 1)

                for i in range(FC // 2 + 2):
                    if i < FC // 2:
                        up(i)
                    if i >= 2:
                        down(i - 2)

            norm(3)
            feed_forward(0, 12, 16)

            norm(4)
            for n in range(8):
                project_features("od_q" if n < 4 else "od_k", "od_in", SELF, 20 if n == 0 else None)
            for n in range(2):
                project_tokens("od_v", "od_in", SELF)

            def z_scores(h):
                if h >= 3:
                    pe.wait_ge(st("sb_exp"), h - 2)
                rows = slice(HD2 * (h % 2), HD2 * (h % 2) + HD2)
                bank = ps[:, 4 + h % 3, :]
                pe.matmul(bank[:, 0:T], odk[rows, h // 2, 0:P], odq[rows, h // 2, :], start=True, stop=True)
                pe.matmul(bank[:, T:S3], odk[rows, h // 2, P:T], odq[rows, h // 2, P:T], start=True, stop=True)\
                    .then_inc(st("sb_z"), 1)

            def minus_breaks(h):
                pe.wait_ge(st("sb_masked"), h + 1)
                bank, b = ps[:, 4 + h % 3, :], sb_brk(h)
                rows = slice(HD2 * (h % 2), HD2 * (h % 2) + HD2)
                pe.matmul(bank[:, 0:T], odk[rows, h // 2, 0:P], odq[rows, h // 2, :], start=True, stop=False)
                pe.matmul(bank[:, 0:T], neg_after, b[:, 0:T], start=False, stop=False)
                pe.matmul(bank[:, P:T], neg_ones, b[:, T:S3], start=False, stop=True)
                pe.matmul(bank[:, T:S3], odk[rows, h // 2, P:T], odq[rows, h // 2, P:T], start=True, stop=False)
                pe.matmul(bank[:, T:S3], neg_after, b[:, T:S3], start=False, stop=True).then_inc(st("sb_log"), 1)

            def weighted_values(h):
                pe.wait_ge(st("sb_sel"), h + 1)
                if h % 2 == 0 and h >= 4:
                    pe.wait_ge(st("sb_out"), h // 2 - 1)
                rows = slice(HD2 * (h % 2), HD2 * (h % 2) + HD2)
                bank, pr = ps[rows, (h // 2) % 2, :], sb_prob(h)
                vh = lambda s: odv[:, s, h * HD2:(h + 1) * HD2]
                pe.matmul(bank[:, 0:T], vh(0), pr[:, 0:T], start=True, stop=False)
                pe.matmul(bank[:, P:T], vh(1), pr[:, T:S3], start=False, stop=True).then_inc(st("sb_o"), 1)

            pe.wait_ge(unit_free["a"], before("a", unit[0] - 1))
            pe.wait_ge(unit_free["v"], before("v", unit[0] - 1))
            pe.wait_ge(x_done, 16)
            for i in range(HO + 3):
                if i < HO:
                    z_scores(i)
                if 1 <= i < HO + 1:
                    minus_breaks(i - 1)
                if i >= 3:
                    weighted_values(i - 3)
            out_project("od_out", 8, OUT2, lambda k: pe.wait_ge(st("sb_split"), k + 1))
            norm(5)
            feed_forward(1, 20, 24)

        @block.sync
        def _(sp):
            sp.dma_start(cst[:, :], const).then_inc(consts_in, 16)
            sp.dma_start(att_mask[:, :, :], mask.rearrange("p (t c) -> p t c", t=2)).then_inc(consts_in, 16)
            for n in range(len(PIECES)):
                if n >= NRAW:
                    sp.wait_ge(*raw_use[n - NRAW])
                dst, src = piece_dma(n)
                sp.dma_start(dst, src).then_inc(loaded[n % NRAW], 16)
            for t in range(NT):
                sp.wait_ge(x_done, 4 * 5 + 2 * (t + 1))
                sp.dma_start(out[0, t * P:(t + 1) * P, :], x[:, t, :]).then_inc(out_stored, 16)
            sp.wait_ge(out_stored, 16 * NT)

        @block.scalar
        def _(act):
            def link(ins):
                then("act", act, ins)

            split = [0]

            def advance(upto):
                while split[0] <= min(upto, len(HALVES) - 1):
                    s = split[0]
                    n = HALVES[s][0]
                    wait_loaded(act, n)
                    for r in (s, s + 1) if isinstance(HALVES[s][3], tuple) and HALVES[s][3][1] == 0 else (s,):
                        if previous_in(r) is not None:
                            act.wait_ge(*half_use[previous_in(r)])
                    act.activation(half_view(w_hi, s), HALVES[s][2], ACT.Copy).then_inc(hi_done, 1)
                    split[0] += 1

            def unit_of(stage, i):
                u = FIRST[stage] + i
                advance(unit_half[u] + NSPLIT - 1)
                act.wait_ge(unit_ready, u + 1)
                return unit_bank(u)

            def ln_exp_tables():
                act.preload_act_table_set("natural_log_exp_and_others")

            hs = [0]

            def norm(j, outs):
                ln_exp_tables()
                for t in range(NT):
                    if j == 0:
                        if t == 0:
                            act.wait_ge(x_in, 16)
                    else:
                        act.wait_ge(x_done, 4 * (j - 1) + 2 * (t + 1))
                    ins = act.activation(xn[:, t, :], x[:, t, :], ACT.Square, accum_out=ssum[:, t:t + 1])
                link(ins)
                link(act.activation(rstd, ssum, ACT.Ln, scale=1.0 / D, bias=eps_t))
                act.activation(rstd, rstd, ACT.Exp, scale=-0.5).then_inc(rstd_done, 1)
                for base, scale, shift in outs:
                    for u in range(4):
                        act.wait_ge(unit_ready, FIRST[f"norm{j}"] + u + 1)
                        bank = unit_bank(FIRST[f"norm{j}"] + u)
                        if base != outs[0][0]:
                            act.wait_ge(h_used, u + 1)
                        for kk in range(2):
                            k = 2 * u + kk
                            ins = act.activation(act_hi[:, base + k, :], bank[:, kk * T:(kk + 1) * T], ACT.Identity,
                                                 scale=scale[:, k:k + 1],
                                                 bias=0.0 if shift is None else shift[:, k:k + 1])
                        ins.then_inc(h_hi, 1)
                        hs[0] += 1

            act.wait_ge(cols_ready, 2)
            act.activation(silu_c, col["c"], ACT.Silu).then_inc(silu_c_ready, 1)
            link(act.activation(lb, lb_tmp, ACT.Sigmoid))
            act.activation(one_m_lb, lb_tmp, ACT.Sigmoid, scale=-1.0).then_inc(st("gate_sig_in"), 1)
            act.wait_ge(mod_read, 4)
            norm(0, [(SELF, scale0, shift0)])

            for u in range(8):
                bank = unit_of("a_f", u)
                sl = slice(2 * u, 2 * u + 2)
                act.activation(fz_b[:, sl, :], bank.rearrange("p (h t) -> p h t", h=2), ACT.Sigmoid)\
                    .then_inc(st("sig_ready"), 1)
                act.activation(k_in0[:, sl, :], bank.rearrange("p (h t) -> p h t", h=2), ACT.Sigmoid, scale=-1.0)\
                    .then_inc(unit_free["a"], 1)
            act.wait_ge(st("sig_ready"), 8)
            ln_exp_tables()
            advance(unit_half[FIRST["a_f"] + 7] + NSPLIT)
            for h in range(HA):
                act.activation(fz_b[:, h, :], fz_b[:, h, :], ACT.Ln, scale=one_m_lb[:, h:h + 1],
                               bias=lb[:, h:h + 1]).then_inc(st("ln_ready"), 1)

            def copy_v(u):
                bank = unit_of("a_i", u)
                act.activation(v_rows[:, u % 2, (u // 2) * HALF:(u // 2 + 1) * HALF], bank, ACT.Copy)\
                    .then_inc(unit_free["a"], 1)

            def exps(g):
                sl = slice(4 * g, 4 * g + 4)
                act.wait_ge(st("scan_ready"), g + 1)
                act.activation(q_dec[:, sl, :], fz_b[:, sl, :], ACT.Exp).then_inc(st("exp_ready"), 1)
                act.activation(k_in[:, sl, :], fz_b[:, sl, :], ACT.Exp, scale=-1.0).then_inc(st("exp_ready"), 1)
                act.wait_ge(st("spread_ready"), g + 1)
                act.activation(k_st[:, sl, :], k_st[:, sl, :], ACT.Exp).then_inc(st("spread_exp"), 1)

            e = unit_half[FIRST["a_f"] + 7] + NSPLIT
            for g in range(4):
                exps(g)
                advance(e + 2 * g)
            for u in range(8):
                bank = unit_of("a_g", u)
                if u == 0:
                    act.wait_ge(st("kin_ready"), 2 * HA)
                act.activation(silu_g[:, 2 * u:2 * u + 2, :], bank.rearrange("p (h t) -> p h t", h=2), ACT.Silu)\
                    .then_inc(unit_free["a"], 1)
            for u in range(8):
                copy_v(u)
            ln_exp_tables()
            advance(unit_half[FIRST["a_i"] + 7] + NSPLIT)

            def o_scale(h):
                act.wait_ge(st("ossq_ready"), h + 1)
                if h >= 2:
                    act.wait_ge(st("o_used"), h - 1)
                link(act.activation(o_r[:, h % 2, :], ps[:, 2 + h % 2, T:2 * T], ACT.Ln,
                                    scale=1.0 / P, bias=eps_t))
                act.activation(o_r[:, h % 2, :], o_r[:, h % 2, :], ACT.Exp, scale=-0.5).then_inc(st("orstd_ready"), 1)

            for i in range(HA + 4):
                if i < HA:
                    act.wait_ge(st("kst_turned"), i + 1)
                    if i >= 2:
                        act.wait_ge(st("state_ready"), i - 1)
                    act.activation(kst_sb[:, i % 2, :, :], ps[:, 6 + i % 2, 0:T].rearrange(
                        "p (t k) -> p t k", t=2), ACT.Copy).then_inc(st("kst_copied"), 1)
                if 2 <= i < HA + 2:
                    h = i - 2
                    act.wait_ge(st("o_ready"), h + 1)
                    if h >= 2:
                        act.wait_ge(st("ossq_ready"), h - 1)
                    act.activation(o_sq[:, h % 2, :], ps[:, 2 + h % 2, 0:T], ACT.Square).then_inc(st("osq_ready"), 1)
                if 3 <= i < HA + 3:
                    o_scale(i - 3)

            advance(first_half[AT[("kv", 0)]] + NSPLIT - 2)

            norm(1, [(KV, scale_kv, shift_kv), (SELF, scale1, shift1)])
            count = [0]

            normed_units = [("k", i) for i in range(8)] + [("q", i) for i in range(8)] + [
                ("ev_k", 0), ("ev_q", 0), ("ev_q", 1)]

            def square_unit(stage, i):
                n = count[0]
                bank = unit_of(stage, i)
                if n >= 2:
                    act.wait_ge(st("hssq_ready"), n - 1)
                act.activation(h_sq[:, n % 2, :], bank, ACT.Square).then_inc(st("hsq_ready"), 1)
                count[0] += 1

            def scale_unit(n, size):
                act.wait_ge(st("hssq_ready"), n + 1)
                if n >= 2:
                    wait_read(act, *normed_units[n - 2])
                link(act.activation(h_r[:, n % 2, :], ps[:, 4 + n % 2, :], ACT.Ln, scale=1.0 / size, bias=eps_t))
                act.activation(h_r[:, n % 2, :], h_r[:, n % 2, :], ACT.Exp, scale=-0.5).then_inc(st("hrstd_ready"), 1)

            for i in range(8):
                square_unit("k", i)
                if i >= 1:
                    scale_unit(i - 1, P)
            for u in range(8):
                bank = unit_of("v", u)
                act.activation(v2_rows[:, u % 2, (u // 2) * HALF:(u // 2 + 1) * HALF], bank, ACT.Copy)\
                    .then_inc(unit_free["a"], 1)
                if u == 1:
                    scale_unit(7, P)
            bank = unit_of("forget", 0)
            act.wait_ge(fb_in, 16)
            act.wait_ge(st("f_min"), 1)
            link(act.activation(f_a, bank[0:HA, 0:T], ACT.Abs, bias=forget_b))
            link(act.activation(f_a, f_a, ACT.Exp, scale=-1.0))
            act.activation(f_a, f_a, ACT.Ln, bias=1.0).then_inc(st("f_ln"), 1)
            for i in range(8):
                square_unit("q", i)
                if i >= 1:
                    scale_unit(8 + i - 1, P)
            scale_unit(15, P)
            for u in range(8):
                bank = unit_of("g", u)
                act.activation(silu_g2[:, 2 * u:2 * u + 2, :], bank.rearrange("p (h t) -> p h t", h=2), ACT.Silu)\
                    .then_inc(unit_free["a"], 1)

            def softmax_heads(pre, heads):
                for i in range(heads + 2):
                    if i < heads:
                        act.wait_ge(st(pre + "_max"), i + 1)
                        if i >= 3:
                            act.wait_ge(st(pre + "_turned"), i - 2)
                        for t, q in enumerate((Q0, Q1)):
                            c = 2 * (i % 2) + t
                            ins = act.activation(prob[:, i % 3, q], lg[:, i % 2, q], ACT.Exp,
                                                 bias=row_neg[:, c:c + 1], accum_out=row_sum[:, c:c + 1])
                            if t == 1:
                                ins.then_inc(st(pre + "_exp"), 1)
                    if i >= 2:
                        h = i - 2
                        act.wait_ge(st(pre + "_turned"), h + 1)
                        if h >= 2:
                            act.wait_ge(st(pre + "_o"), h - 1)
                        act.activation(probT[:, h % 2, :], ps[:, 6 + h % 2, 0:S3], ACT.Copy)\
                            .then_inc(st(pre + "_tcopied"), 1)

            ln_exp_tables()
            advance(unit_half[FIRST["g"] + 7] + NSPLIT)
            softmax_heads("fx", HA)
            advance(first_half[AT[("ev_qi", 0)]] + NSPLIT - 2)

            norm(2, [(SELF, col["norm_mix_g_2"][:, 0:8], None)])
            bank = unit_of("ev_i", 0)
            act.activation(evqi, bank.rearrange("p (c t) -> p c t", c=2), ACT.Copy).then_inc(unit_free["a"], 1)
            bank = unit_of("ev_i", 1)
            act.activation(evki, bank[:, 0:T], ACT.Copy)
            act.activation(w_idx, bank[:, T:T + 8], ACT.Copy, scale=float((HIDX * HD2) ** -0.5))\
                .then_inc(unit_free["a"], 1)
            for h in range(HIDX):
                act.wait_ge(st("ev_rel"), h + 1)
                if h >= 2:
                    act.wait_ge(st("ev_score_used"), h - 1)
                act.activation(relu_s[:, h % 2, :], ps[:, 4 + h, 0:S3], ACT.Relu).then_inc(st("ev_relu"), 1)
            square_unit("ev_k", 0)
            bank = unit_of("ev_v", 0)
            act.activation(evv, bank[:, 0:T].rearrange("p (t d) -> p t d", t=2), ACT.Copy).then_inc(unit_free["a"], 1)
            scale_unit(16, HD2)
            square_unit("ev_q", 0)
            square_unit("ev_q", 1)
            scale_unit(17, HD2)
            for u in range(2):
                bank = unit_of("ev_u", u)
                act.activation(u_pad[:, 2 * u:2 * u + 2, PAD:], bank.rearrange("p (g t) -> p g t", g=2), ACT.Copy)\
                    .then_inc(unit_free["a"], 1)
                if u == 0:
                    scale_unit(18, HD2)
            advance(unit_half[FIRST["ev_u"] + 1] + NSPLIT)
            softmax_heads("ds", HE)
            advance(first_half[AT[("w1", 0, 0)]] + NSPLIT - 2)

            def feed_forward(layer):
                for c in range(FC):
                    bank = unit_of(f"up{layer}", c)
                    if c >= 2:
                        wait_read(act, f"up{layer}", c - 2)
                    act.activation(silu_a[:, c % 2, :], bank[:, 0:T], ACT.Silu).then_inc(st("up_silu"), 1)

            norm(3, [(SELF, col["norm_ffn_g_2"][:, 0:8], None)])
            feed_forward(0)
            advance(first_half[AT[("od_in", 0)]] + NSPLIT - 2)

            norm(4, [(SELF, col["norm_mix_g_2"][:, 8:16], None)])
            for u in range(4):
                bank = unit_of("od_q", u)
                act.activation(odq[:, 2 * u:2 * u + 2, :], bank.rearrange("p (h t) -> p h t", h=2), ACT.Copy,
                               scale=float(HD2 ** -0.5)).then_inc(unit_free["a"], 1)
            for u in (0, 2):
                bank = unit_of("od_v", u)
                act.activation(odv[:, 0, (u // 2) * HALF:(u // 2 + 1) * HALF], bank, ACT.Copy)\
                    .then_inc(unit_free["a"], 1)
            advance(unit_half[FIRST["od_v"] + 3] + NSPLIT)
            for i in range(HO + 1):
                if i < HO:
                    act.wait_ge(st("sb_z"), i + 1)
                    if i >= 2:
                        act.wait_ge(st("sb_soft"), i - 1)
                    link(act.activation(sb_ln_t(i), ps[:, 4 + i % 3, 0:S3], ACT.Abs))
                    link(act.activation(sb_ln_t(i), sb_ln_t(i), ACT.Exp, scale=-1.0))
                    act.activation(sb_ln_t(i), sb_ln_t(i), ACT.Ln, bias=1.0).then_inc(st("sb_ln"), 1)
                if i >= 1:
                    h = i - 1
                    act.wait_ge(st("sb_log"), h + 1)
                    if h >= 3:
                        act.wait_ge(st("sb_o"), h - 2)
                    act.activation(sb_prob(h), ps[:, 4 + h % 3, 0:S3], ACT.Exp).then_inc(st("sb_exp"), 1)
            advance(first_half[AT[("w1", 1, 0)]] + NSPLIT - 2)
            norm(5, [(SELF, col["norm_ffn_g_2"][:, 8:16], None)])
            feed_forward(1)
            advance(len(HALVES))

        @block.vector
        def _(dve):
            def link(ins):
                then("dve", dve, ins)

            split, piece_at = [0], [8]

            def advance(upto):
                while split[0] <= min(upto, len(HALVES) - 1):
                    s = split[0]
                    while piece_at[0] < HALVES[s][0]:
                        piece = PIECES[piece_at[0]]
                        piece_at[0] += 1
                        if piece[0] == "mod":
                            mod_sum(piece[1], piece[2])
                            if piece[2] == 1 and piece[1] not in (4, 14):
                                mod_take(piece[1] - 1)
                    dve.wait_ge(hi_done, s + 1)
                    dve.tensor_tensor(half_view(w_lo, s), HALVES[s][2], half_view(w_hi, s).bitcast(F32),
                                      ALU.subtract).then_inc(lo_done, 1)
                    split[0] += 1

            def unit_of(stage, i):
                u = FIRST[stage] + i
                advance(unit_half[u] + NSPLIT - 1)
                dve.wait_ge(unit_ready, u + 1)
                return unit_bank(u)

            def norm(j, outs):
                dve.wait_ge(rstd_done, j + 1)
                for t in range(NT):
                    dve.tensor_scalar(xn[:, t, :], x[:, t, :], rstd[:, t:t + 1], None, ALU.mult).then_inc(xn_done, 1)
                for base, scale, shift in outs:
                    for u in range(4):
                        b = hs[0] % 2
                        dve.wait_ge(h_hi, hs[0] + 1)
                        bank = unit_bank(FIRST[f"norm{j}"] + u)
                        for kk in range(2):
                            k = 2 * u + kk
                            dst = h_full[:, b, kk * T:(kk + 1) * T]
                            if shift is None:
                                ins = dve.tensor_scalar(dst, bank[:, kk * T:(kk + 1) * T], scale[:, k:k + 1],
                                                        None, ALU.mult)
                            else:
                                ins = dve.tensor_scalar(dst, bank[:, kk * T:(kk + 1) * T], scale[:, k:k + 1],
                                                        shift[:, k:k + 1], ALU.mult, ALU.add)
                        if base == outs[-1][0]:
                            ins.then_inc(unit_free["v"], 1)
                            dve.wait_ge(unit_free["v"], before("v", FIRST[f"norm{j}"] + u))
                        else:
                            ins.then_inc(h_used, 1)
                            hu[0] += 1
                            dve.wait_ge(h_used, hu[0])
                        dve.tensor_tensor(act_lo[:, base + 2 * u:base + 2 * u + 2, :],
                                          h_full[:, b, :].rearrange("p (k t) -> p k t", k=2),
                                          act_hi[:, base + 2 * u:base + 2 * u + 2, :].bitcast(F32),
                                          ALU.subtract).then_inc(h_lo, 1)
                        hs[0] += 1
                        dve.wait_ge(h_lo, hs[0])

            hs, hu = [0], [0]

            def add_y(j, gated_):
                for t in range(NT):
                    for n in range(2):
                        sl = slice(n * HALF, (n + 1) * HALF)
                        dve.wait_ge(y_ready, 4 * j + 2 * t + n + 1)
                        src = y_bank(t, n)
                        if gated_:
                            link(dve.tensor_tensor(acc[:, n, :], src, gate[:, sl], ALU.mult))
                            src = acc[:, n, :]
                        dve.tensor_tensor(x[:, t, sl], x[:, t, sl], src, ALU.add).then_inc(x_done, 1)

            mb = col["mod_b"]
            dest = {0: (shift0, 0, mb, 0, None), 1: (shift0, 4, mb, 4, None),
                    2: (scale0, 0, mb, 8, col["norm_g"][:, 0:4]), 3: (scale0, 4, mb, 12, col["norm_g"][:, 4:8]),
                    6: (shift1, 0, mb, 24, None), 7: (shift1, 4, mb, 28, None),
                    8: (scale1, 0, mb, 32, col["norm_g"][:, 8:12]), 9: (scale1, 4, mb, 36, col["norm_g"][:, 12:16]),
                    10: (shift_kv, 0, col["kv_mod_b"], 0, None), 11: (shift_kv, 4, col["kv_mod_b"], 4, None),
                    12: (scale_kv, 0, col["kv_mod_b"], 8, col["kv_norm_g"][:, 0:4]),
                    13: (scale_kv, 4, col["kv_mod_b"], 12, col["kv_norm_g"][:, 4:8])}

            def mod_sum(m, q):
                n = AT[("mod", m, q)]
                wait_loaded(dve, n)
                if m >= 2:
                    dve.wait_ge(mod_cols, m - 1)
                w = by_k(slot(n), 4)
                for k in range(4):
                    c = silu_c[:, 4 * q + k:4 * q + k + 1]
                    if q == 0 and k == 0:
                        ins = dve.tensor_scalar(acc[:, m % 2, :], w[:, 0, :], c, None, ALU.mult)
                    else:
                        ins = dve.scalar_tensor_tensor(out=acc[:, m % 2, :], in0=w[:, k, :], scalar=c,
                                                       in1=acc[:, m % 2, :], op0=ALU.mult, op1=ALU.add)
                    if k < 3:
                        link(ins)
                ins.then_inc(mod_summed, 1)
                dve.wait_ge(mod_summed, 2 * m + q + 1)

            def mod_take(m):
                dve.wait_ge(mod_cols, m + 1)
                bank = ps[:, 6 + m % 2, :]
                if m in (4, 5, 14, 15):
                    dve.wait_ge(gate_b_in, 16 if m < 14 else 32)
                    sl = slice((m % 2) * HALF, (m % 2 + 1) * HALF)
                    dve.tensor_tensor(gate[:, sl], gate[:, sl], bank, ALU.add).then_inc(mod_read, 1)
                    return
                dst, c, bias, b, gain = dest[m]
                if gain is None:
                    dve.tensor_tensor(dst[:, c:c + 4], bank[:, 0:4], bias[:, b:b + 4], ALU.add).then_inc(mod_read, 1)
                else:
                    link(dve.scalar_tensor_tensor(out=mod_tmp, in0=bank[:, 0:4], scalar=1.0, in1=bias[:, b:b + 4],
                                                  op0=ALU.add, op1=ALU.add))
                    dve.tensor_tensor(dst[:, c:c + 4], mod_tmp, gain, ALU.mult).then_inc(mod_read, 1)
                dve.wait_ge(mod_read, m + 1)

            dve.memset(eps_t, EPS)
            dve.wait_ge(rows_turned, 1)
            dve.tensor_copy(cols[:, :], ps[:, 4, 0:256]).then_inc(cols_ready, 1)
            dve.wait_ge(cols_ready, 1)
            link(dve.tensor_tensor(lb_tmp, col["a_lb_logits"][:, 0:16], col["a_lb_logits"][:, 16:32], ALU.subtract))
            dve.tensor_scalar(q_gain, col["b_q_norm_g"], float(P ** -0.5), None, ALU.mult)
            dve.tensor_scalar(ev_q_gain, ev_gain[:, 0:1], float(HD2 ** -0.5), None, ALU.mult).then_inc(cols_ready, 1)
            dve.wait_ge(cols_ready, 2)
            dve.wait_ge(silu_c_ready, 1)
            for m in range(4):
                mod_sum(m, 0)
                mod_sum(m, 1)
                if m >= 1:
                    mod_take(m - 1)
            mod_take(3)
            norm(0, [(SELF, scale0, shift0)])
            dve.wait_ge(st("gate_sig_in"), 1)

            link(dve.memset(att_sb, 0.0))
            e = unit_half[FIRST["a_f"] + 7]
            advance(e + NSPLIT - 1)
            for g in range(4):
                sl = slice(4 * g, 4 * g + 4)
                for h in range(4 * g, 4 * g + 4):
                    dve.wait_ge(st("ln_ready"), h + 1)
                    ins = dve.tensor_tensor_scan(fz_b[:, h, :], chunk_go, fz_b[:, h, :], 0.0, ALU.mult, ALU.add)
                ins.then_inc(st("scan_ready"), 1)
                dve.wait_ge(st("scan_ready"), g + 1)
                part = fz_b[:, sl, :].rearrange("p h (n c) -> p (h n) c", c=CHUNK)
                dst = k_st[:, sl, :].rearrange("p h (n c) -> p (h n) c", c=CHUNK)
                dve.tensor_tensor(dst, part[:, :, CHUNK - 1:CHUNK].to_broadcast([P, 4 * NC, CHUNK]), part,
                                  ALU.subtract).then_inc(st("spread_ready"), 1)
                advance(e + NSPLIT + 2 * g)
                dve.wait_ge(st("exp_ready"), 2 * (g + 1))
                dve.tensor_copy(dl[:, sl, :], q_dec[:, sl, CHUNK - 1::CHUNK])
                for h in range(4 * g, 4 * g + 4):
                    dve.scalar_tensor_tensor(out=k_in[:, h, :], in0=k_in0[:, h, :], scalar=one_m_lb[:, h:h + 1],
                                             in1=k_in[:, h, :], op0=ALU.mult, op1=ALU.mult)\
                        .then_inc(st("kin_ready"), 1)
                    dve.wait_ge(st("spread_exp"), g + 1)
                    dve.scalar_tensor_tensor(out=k_st[:, h, :], in0=k_in0[:, h, :], scalar=one_m_lb[:, h:h + 1],
                                             in1=k_st[:, h, :], op0=ALU.mult, op1=ALU.mult)\
                        .then_inc(st("kin_ready"), 1)
            for u in range(8):
                bank = unit_of("a_q", u)
                sl = slice(2 * u, 2 * u + 2)
                dve.tensor_tensor(q_dec[:, sl, :], bank.rearrange("p (h t) -> p h t", h=2), q_dec[:, sl, :], ALU.mult)\
                    .then_inc(unit_free["v"], 1)
            advance(unit_half[FIRST["a_i"] + 7] + NSPLIT)
            mod_take(13)
            dve.wait_ge(unit_free["a"], before("a", FIRST["a_g"] + 7))

            def o_out(h):
                dve.wait_ge(st("orstd_ready"), h + 1)
                if h >= 1:
                    dve.wait_ge(st("ot_ready"), h)
                dve.scalar_tensor_tensor(out=o_tmp, in0=ps[:, 2 + h % 2, 0:T], scalar=col["a_onorm_g"][:, h:h + 1],
                                         in1=o_r[:, h % 2, :], op0=ALU.mult, op1=ALU.mult).then_inc(st("o_used"), 1)
                dve.wait_ge(st("o_used"), h + 1)
                if h >= 2:
                    dve.wait_ge(st("ot_split"), h - 1)
                dve.tensor_tensor(o_full[:, h % 2, :], o_tmp, silu_g[:, h, :], ALU.mult).then_inc(st("ot_ready"), 1)

            for i in range(HA + 4):
                if i >= 4:
                    o_out(i - 4)
                if i < HA:
                    dve.wait_ge(st("att_ready"), i + 1)
                    if i >= 2:
                        dve.wait_ge(st("o_ready"), i - 1)
                    dve.copy_predicated(att_sb[:, i % 2, :, :], att_mask[:, :, :],
                                        ps[:, 4 + i % 2, 0:T].rearrange("p (t c) -> p t c", t=2))\
                        .then_inc(st("att_masked"), 1)
                if 1 <= i < HA + 1:
                    h = i - 1
                    dve.wait_ge(st("state_ready"), h + 1)
                    if h >= 2:
                        dve.wait_ge(st("o_ready"), h - 1)
                    link(dve.tensor_copy(state[:, h % 2, 0, :], ps[:, 0, 0:P]))
                    for n in range(1, NC - 1):
                        ins = dve.scalar_tensor_tensor(out=state[:, h % 2, n, :], in0=state[:, h % 2, n - 1, :],
                                                       scalar=dl[:, h, n:n + 1], in1=ps[:, n % 2, n * P:(n + 1) * P],
                                                       op0=ALU.mult, op1=ALU.add)
                        if n < NC - 2:
                            link(ins)
                    ins.then_inc(st("state_saved"), 1)
            advance(first_half[AT[("kv", 0)]] + NSPLIT - 2)
            add_y(0, True)

            norm(1, [(KV, scale_kv, shift_kv), (SELF, scale1, shift1)])

            def normed(stage, i, n, dst, gain):
                bank = unit_of(stage, i)
                if n == 7:
                    advance(unit_half[FIRST["v"] + 1])
                dve.wait_ge(st("hrstd_ready"), n + 1)
                dve.scalar_tensor_tensor(out=dst, in0=bank.rearrange("p (h t) -> p h t", h=2), scalar=gain,
                                         in1=h_r[:, n % 2, :].rearrange("p (h t) -> p h t", h=2),
                                         op0=ALU.mult, op1=ALU.mult).then_inc(unit_free["v"], 1)

            for i in range(8):
                normed("k", i, i, kN[:, 2 * i:2 * i + 2, :], col["k_norm_g"])
            bank = unit_of("forget", 0)
            dve.wait_ge(fb_in, 16)
            dve.tensor_scalar(f_b, bank[0:HA, 0:T], forget_b, 0.0, ALU.add, ALU.min).then_inc(st("f_min"), 1)
            dve.wait_ge(st("f_ln"), 1)
            link(dve.tensor_tensor(f_b, f_a, f_b, ALU.subtract))
            dve.nop().then_inc(unit_free["v"], 1)
            dve.tensor_tensor_scan(neg_f, f_b, f_b, 0.0, ALU.add, ALU.max).then_inc(st("nf_ready"), 1)
            for i in range(8):
                normed("q", i, 8 + i, qN[:, 2 * i:2 * i + 2, :], q_gain)
            advance(unit_half[FIRST["g"] + 7] + NSPLIT)
            mod_take(15)
            dve.wait_ge(unit_free["a"], before("a", FIRST["g"] + 7))

            def softmax_heads(pre, heads, bias, output):
                for i in range(heads + 4):
                    if i < heads:
                        dve.wait_ge(st(pre + "_logits"), i + 1)
                        if i >= 2:
                            dve.wait_ge(st(pre + "_exp"), i - 1)
                        c = 2 * (i % 2)
                        for t, q in enumerate((Q0, Q1)):
                            ins = dve.tensor_tensor_reduce(out=lg[:, i % 2, q], in0=ps[:, 4 + i % 2, q], in1=bias[:, q],
                                                           scale=1.0, scalar=LOW, op0=ALU.add, op1=ALU.max,
                                                           accum_out=row_max[:, c + t:c + t + 1])
                        link(ins)
                        dve.tensor_scalar(row_neg[:, c:c + 2], row_max[:, c:c + 2], -1.0, None, ALU.mult)\
                            .then_inc(st(pre + "_max"), 1)
                    if 1 <= i < heads + 1:
                        h = i - 1
                        c = 2 * (h % 2)
                        dve.wait_ge(st(pre + "_exp"), h + 1)
                        link(dve.reciprocal(row_inv[:, c:c + 2], row_sum[:, c:c + 2]))
                        for t, q in enumerate((Q0, Q1)):
                            ins = dve.tensor_scalar(prob[:, h % 3, q], prob[:, h % 3, q], row_inv[:, c + t:c + t + 1],
                                                    None, ALU.mult)
                        ins.then_inc(st(pre + "_prob"), 1)
                    if i >= 4:
                        output(i - 4)

            def fox_out(h):
                dve.wait_ge(st("fx_o"), h + 1)
                if h >= 2:
                    dve.wait_ge(st("fx_split"), h - 1)
                dve.tensor_tensor(o_full[:, h % 2, :], ps[:, h % 2, 0:T], silu_g2[:, h, :], ALU.mult)\
                    .then_inc(st("fx_out"), 1)

            softmax_heads("fx", HA, causal, fox_out)
            advance(first_half[AT[("ev_qi", 0)]] + NSPLIT - 2)
            add_y(1, True)

            norm(2, [(SELF, col["norm_mix_g_2"][:, 0:8], None)])
            dve.memset(u_pad[:, :, 0:PAD], 0.0)
            dve.memset(run_a[:, 0:PAD], 0.0)
            dve.memset(run_b[:, 0:PAD], 0.0)
            e = unit_half[FIRST["ev_i"] + 1] + NSPLIT
            advance(e - 1)
            wait_read(dve, "ev_i", 1)
            for h in range(HIDX):
                dve.wait_ge(st("ev_relu"), h + 1)
                for t, q in enumerate((Q0, Q1)):
                    wcol = w_idx[:, 4 * t + h:4 * t + h + 1]
                    if h == 0:
                        ins = dve.tensor_scalar(score[:, q], relu_s[:, h % 2, q], wcol, None, ALU.mult)
                    else:
                        ins = dve.scalar_tensor_tensor(out=score[:, q], in0=relu_s[:, h % 2, q], scalar=wcol,
                                                       in1=score[:, q], op0=ALU.mult, op1=ALU.add)
                ins.then_inc(st("ev_score_used"), 1)
                dve.wait_ge(st("ev_score_used"), h + 1)
            link(dve.tensor_tensor(score, score, causal, ALU.add))

            def choose(q, n, ahead):
                src = score[:, q]
                for r in range(TOPK // 8):
                    if r % 4 == 2:
                        advance(ahead + r // 4)
                    link(dve.max(top8, src))
                    if r < TOPK // 8 - 1:
                        link(dve.match_replace(out=cut[:, 0:n], in_to_replace=top8, in_values=src, imm_value=LOW))
                        src = cut[:, 0:n]
                least = top8[:, 7:8]
                dve.tensor_scalar(sel_eq[:, 0:n], score[:, q], least, None, ALU.is_equal)
                link(dve.tensor_scalar(sel_gt[:, 0:n], score[:, q], least, None, ALU.is_gt, ALU.add, accum_out=cnt))
                link(dve.tensor_scalar(rest, cnt, -1.0, float(TOPK), ALU.mult, ALU.add))
                link(dve.tensor_tensor_scan(sel_pre[:, 0:n], sel_eq[:, 0:n], sel_eq[:, 0:n], 0.0, ALU.add, ALU.max))
                link(dve.scalar_tensor_tensor(out=sel_eq[:, 0:n], in0=sel_pre[:, 0:n], scalar=rest, in1=sel_eq[:, 0:n],
                                              op0=ALU.is_le, op1=ALU.mult))
                link(dve.tensor_tensor(sel_gt[:, 0:n], sel_gt[:, 0:n], sel_eq[:, 0:n], ALU.add))
                link(dve.tensor_scalar(sel_gt[:, 0:n], sel_gt[:, 0:n], -FAR, FAR, ALU.mult, ALU.add))
                link(dve.tensor_tensor(ev_bias_t[:, q], sel_gt[:, 0:n], causal[:, q], ALU.add))

            choose(Q1, T, e)
            normed("ev_k", 0, 16, evk, ev_gain[:, 1:2])
            normed("ev_q", 0, 17, evq[:, 0:2, :], ev_q_gain)
            normed("ev_q", 1, 18, evq[:, 2:4, :], ev_q_gain)
            choose(Q0, P, unit_half[FIRST["ev_q"] + 1] + NSPLIT)
            dve.wait_ge(unit_free["a"], before("a", FIRST["ev_u"] + 1))
            for g in range(4):
                u, window = u_pad[:, g, :], 2
                src, dst, spare = u, run_a, run_b
                step = 1
                for _ in range(g + 1):
                    link(dve.tensor_tensor(dst[:, PAD:], src[:, PAD:], src[:, PAD - step:PAD + T - step], ALU.add))
                    src, dst, spare = dst, spare, dst
                    step *= 2
                window = step
                dve.scalar_tensor_tensor(out=mixed[:, g, PAD:], in0=src[:, 2 * PAD:], scalar=1.0 / window,
                                         in1=u[:, 2 * PAD:], op0=ALU.mult, op1=ALU.subtract)
                link(dve.tensor_tensor(mixed[:, g, 0:PAD], src[:, PAD:2 * PAD], inv_count[:, g, :], ALU.mult))
                dve.tensor_tensor(mixed[:, g, 0:PAD], mixed[:, g, 0:PAD], u[:, PAD:2 * PAD], ALU.subtract)\
                    .then_inc(st("ev_mixed"), 1)
            for pair in range(2):
                bank = unit_of("ev_pool", pair)
                for j in range(2):
                    g = 2 * pair + j
                    link(dve.tensor_scalar(pooled[:, g, :], bank[:, j * T:(j + 1) * T],
                                           col["ev_pool_scale_2"][:, g:g + 1], None, ALU.mult))
                c = slice(OUT2 + 4 + 2 * pair, OUT2 + 6 + 2 * pair)
                full = pooled[:, 2 * pair:2 * pair + 2, :]
                link(dve.tensor_copy(act_hi[:, c, :], full))
                dve.tensor_tensor(act_lo[:, c, :], full, act_hi[:, c, :].bitcast(F32), ALU.subtract)\
                    .then_inc(unit_free["v"], 1)

            def ds_out(h):
                if h % 2 == 1:
                    dve.wait_ge(st("ds_o"), h + 1)
                    if h >= 4:
                        dve.wait_ge(st("ds_split"), h // 2 - 1)
                    dve.tensor_copy(o_full[:, (h // 2) % 2, :], ps[:, (h // 2) % 2, 0:T]).then_inc(st("ds_out"), 1)

            advance(unit_half[FIRST["ev_pool"] + 1] + NSPLIT)
            softmax_heads("ds", HE, ev_bias_t, ds_out)
            advance(first_half[AT[("w1", 0, 0)]] + NSPLIT - 2)
            add_y(2, False)

            def feed_forward(layer):
                for c in range(FC):
                    bank = unit_of(f"up{layer}", c)
                    dve.wait_ge(st("up_silu"), layer * FC + c + 1)
                    g = g_full[:, c % 2, :]
                    dve.tensor_tensor(g, bank[:, T:2 * T], silu_a[:, c % 2, :], ALU.mult).then_inc(st("g_full"), 1)
                    dve.wait_ge(st("g_full"), layer * FC + c + 1)
                    if c >= 8:
                        dve.wait_ge(*half_use[down_half[layer, c - 8]])
                    dve.tensor_copy(act_hi[:, 8 + c % 8, :], g).then_inc(st("g_hi"), 1)
                    dve.wait_ge(st("g_hi"), layer * FC + c + 1)
                    dve.tensor_tensor(act_lo[:, 8 + c % 8, :], g, act_hi[:, 8 + c % 8, :].bitcast(F32), ALU.subtract)\
                        .then_inc(unit_free["v"], 1)

            norm(3, [(SELF, col["norm_ffn_g_2"][:, 0:8], None)])
            feed_forward(0)
            advance(first_half[AT[("od_in", 0)]] + NSPLIT - 2)
            add_y(3, False)

            norm(4, [(SELF, col["norm_mix_g_2"][:, 8:16], None)])
            for u in range(4):
                bank = unit_of("od_k", u)
                dve.tensor_copy(odk[:, 2 * u:2 * u + 2, :], bank.rearrange("p (h t) -> p h t", h=2))\
                    .then_inc(unit_free["v"], 1)
            for u in (1, 3):
                bank = unit_of("od_v", u)
                dve.tensor_copy(odv[:, 1, (u // 2) * HALF:(u // 2 + 1) * HALF], bank).then_inc(unit_free["v"], 1)
            advance(unit_half[FIRST["od_v"] + 3] + NSPLIT)
            for i in range(HO + 4):
                if i < HO:
                    dve.wait_ge(st("sb_ln"), i + 1)
                    if i >= 3:
                        dve.wait_ge(st("sb_log"), i - 2)
                    dve.scalar_tensor_tensor(out=sb_brk(i), in0=ps[:, 4 + i % 3, 0:S3], scalar=0.0, in1=sb_ln_t(i),
                                             op0=ALU.max, op1=ALU.add).then_inc(st("sb_soft"), 1)
                if i >= 4 and i % 2 == 1:
                    h = i - 4
                    dve.wait_ge(st("sb_o"), h + 1)
                    if h >= 4:
                        dve.wait_ge(st("sb_split"), h // 2 - 1)
                    dve.tensor_copy(o_full[:, (h // 2) % 2, :], ps[:, (h // 2) % 2, 0:T]).then_inc(st("sb_out"), 1)
            advance(first_half[AT[("w1", 1, 0)]] + NSPLIT - 2)
            add_y(4, False)
            norm(5, [(SELF, col["norm_ffn_g_2"][:, 8:16], None)])
            feed_forward(1)
            advance(len(HALVES))
            add_y(5, False)


def shape_constants():
    p = np.arange(P)
    ident = np.eye(P)
    ones = np.ones((P, P))
    ones64 = (p[:, None] // HD2 == p[None, :] // HD2).astype(float)
    neg_after = -(p[:, None] >= p[None, :]).astype(float)
    t0 = np.where(p[None, :] <= p[:, None], 0.0, FAR)
    causal = np.concatenate([t0, np.zeros((P, P)), t0], axis=1)
    go = np.broadcast_to((np.arange(T) % CHUNK != 0).astype(float), (P, T))
    count = np.concatenate([1.0 / np.minimum(np.arange(1, 17), w) for w in (2, 4, 8, 16)])
    count = np.broadcast_to(count, (P, 64))
    const = np.concatenate([ident, ones, ones64, neg_after, -ones, causal, go, count], axis=1).astype(np.float32)
    m = ((p[:, None] // CHUNK == p[None, :] // CHUNK) & (p[:, None] <= p[None, :])).astype(np.int32)
    return np.ascontiguousarray(const), np.ascontiguousarray(np.concatenate([m, m], axis=1))


_INS = ["x", "c", "mod_w", "mod_b", "norm_g", "a_w_in", "a_lb_logits", "a_onorm_g", "a_w_out", "kv_mod_w", "kv_mod_b",
        "kv_norm_g", "kv_w", "kv_fb", "k_norm_g", "b_w_in", "b_q_norm_g", "b_w_out", "norm_mix_g_2", "norm_ffn_g_2",
        "ev_w_in_2", "ev_w_out_2", "ev_q_norm_g_2", "ev_k_norm_g_2", "ev_pool_w_2", "ev_pool_scale_2",
        "od_w_qkv_2", "od_w_out_2", "ffn_w1_2", "ffn_w3_2", "ffn_w2_2"]


def kernel(**inputs):
    import concourse.bacc as bacc
    from concourse.bass_utils import run_bass_kernel_spmd

    nc = bacc.Bacc("TRN2", target_bir_lowering=False, num_devices=1)
    arrays, views = {}, {}
    for name in _INS:
        v = np.ascontiguousarray(inputs[name])
        arrays[f"in_{name}"] = v
        views[name] = nc.dram_tensor(f"in_{name}", v.shape, mybir.dt.from_np(v.dtype), kind="ExternalInput").ap()
    const, mask = shape_constants()
    arrays["shape_constants"], arrays["shape_mask"] = const, mask
    c = nc.dram_tensor("shape_constants", const.shape, F32, kind="ExternalInput").ap()
    m = nc.dram_tensor("shape_mask", mask.shape, I32, kind="ExternalInput").ap()
    out = nc.dram_tensor("out", (1, T, D), F32, kind="ExternalOutput").ap()
    build(nc, views, c, m, out)
    r = run_bass_kernel_spmd(nc, [arrays], core_ids=[0])
    return r.results[0]["out"]
```

```python
from contextlib import ExitStack

import numpy as np

import concourse.bass as bass
from concourse import mybir
from concourse.alu_op_type import AluOpType as ALU

ACT = mybir.ActivationFunctionType
F32 = mybir.dt.float32
F32R = mybir.dt.float32r
I32 = mybir.dt.int32
X = mybir.AxisListType.X

P = 128
D = 1024
T = 256
NT = T // P
KD = D // P
W = 2048
HA = W // P
CHUNK = 64
NC = T // CHUNK
HALF = 512
FF = 2816
FC = FF // P
HD2 = 64
HE = 8
HIDX = 4
HO = 16
EV_COLS = 1604
TOPK = min(256, T // 4)
EPS = 1e-6
FAR = -1e30
LOW = -3e38
NRAW = 3
PIECE = 2048
NSPLIT = 4
PART = PIECE // 2
ARRAY = 4096
S3 = P + T
Q0, Q1 = slice(0, P), slice(P, S3)

VEC_A = [("norm_g", 16), ("mod_b", 48), ("kv_norm_g", 8), ("kv_mod_b", 16),
         ("norm_mix_g_2", 16), ("norm_ffn_g_2", 16)]
VEC_B = [("a_lb_logits", 32), ("a_onorm_g", 16), ("ev_pool_scale_2", 4), ("k_norm_g", 1), ("b_q_norm_g", 1)]


def weight_pieces():
    pieces = [("mod", m, q) for m in range(4) for q in range(2)]
    mods = [(m, q) for m in range(4, 14) for q in range(2)]
    for n in range(32):
        pieces.append(("a_in", n))
        if (1 <= n < 8 or n in (16, 18, 19, 21, 22, 23) or n >= 24) and mods:
            pieces.append(("mod", *mods.pop(0)))
    pieces += [("a_out", n) for n in range(8)]
    pieces += [("kv", n) for n in range(16)] + [("forget", 0)]
    mods = [(m, q) for m in (14, 15) for q in range(2)]
    for n in range(16):
        pieces.append(("b_in", n))
        if n % 3 and mods:
            pieces.append(("mod", *mods.pop(0)))
    pieces += [("b_out", n) for n in range(8)]
    pieces += [("ev_qi", 0), ("ev_small", 0), ("ev_kv", 0), ("ev_q", 0), ("ev_q", 1), ("ev_u", 0), ("ev_u", 1),
               ("pool_w", 0)]
    pieces += [("ev_out", n) for n in range(4)]

    def ffn(layer):
        order = []
        for i in range(FC // 2 + 2):
            if i < FC // 2:
                order += [("w1", layer, i), ("w3", layer, i)]
            if i >= 2:
                order.append(("w2", layer, i - 2))
        return order

    pieces += ffn(0)
    pieces += [("od_in", n) for n in range(12)] + [("od_out", n) for n in range(4)]
    pieces += ffn(1)
    return pieces


def units():
    out = []

    def add(stage, engines):
        out.extend((stage, e) for e in engines)

    add("norm0", "vvvv")
    add("a_f", "a" * 8)
    add("a_i", "a" * 8)
    add("a_q", "v" * 8)
    add("a_g", "a" * 8)
    add("norm1", "aaaa")
    add("k", "v" * 8)
    add("v", "a" * 8)
    add("forget", "v")
    add("q", "v" * 8)
    add("g", "a" * 8)
    add("norm2", "vvvv")
    add("ev_i", "aa")
    add("ev_k", "v")
    add("ev_v", "a")
    add("ev_q", "vv")
    add("ev_u", "aa")
    add("ev_pool", "vv")
    add("norm3", "vvvv")
    add("up0", "v" * FC)
    add("norm4", "vvvv")
    add("od_q", "aaaa")
    add("od_k", "vvvv")
    add("od_v", "avav")
    add("norm5", "vvvv")
    add("up1", "v" * FC)
    return out


def build(nc, a, const, mask, out):
    PIECES = weight_pieces()
    AT = {t: n for n, t in enumerate(PIECES)}
    UNITS = units()
    FIRST = {}
    for n, (s, _) in enumerate(UNITS):
        FIRST.setdefault(s, n)

    with ExitStack() as ctx:
        def sb(name, shape, dt=F32):
            return ctx.enter_context(nc.sbuf_tensor(name, shape, dt))

        def sem(name):
            return ctx.enter_context(nc.semaphore(name))

        raw = sb("raw_weights", [P, NRAW, PIECE])
        w_hi = sb("w_hi", [P, NSPLIT * PART], F32R)
        w_lo = sb("w_lo", [P, NSPLIT * PART], F32R)
        with nc.sbuf_tensor("act_f32", [P, 2, 16 * T], F32) as act_f32:
            pass
        act_hi = sb("act_hi", [P, 16, T], F32R)
        act_lo = sb("act_lo", [P, 16, T], F32R)
        big = sb("big", [P, 5, ARRAY])
        x = sb("x", [P, NT, D])
        gate = sb("gate", [P, D])
        acc = sb("acc", [P, 2, HALF])
        cst = sb("cst", [P, const.shape[1]])
        att_mask = sb("att_mask", [P, 2, P], I32)
        cols = sb("cols", [P, 256])
        small = sb("small", [P, 256])
        work = sb("work", [P, 3584])

        ident, ones, ones64 = cst[:, 0:128], cst[:, 128:256], cst[:, 256:384]
        neg_after, neg_ones = cst[:, 384:512], cst[:, 512:640]
        causal = cst[:, 640:1024]
        chunk_go = cst[:, 1024:1280]
        inv_count = cst[:, 1280:1344].rearrange("p (g t) -> p g t", g=4)

        def grid(n, heads=HA):
            return big[:, n, 0:heads * T].rearrange("p (h t) -> p h t", h=heads)

        xn = big[:, 4, 0:NT * D].rearrange("p (t n) -> p t n", t=NT)
        SELF, KV = 0, KD

        at = 0
        col = {}
        for vecs, base in ((VEC_A, 0), (VEC_B, 128)):
            at = base
            for name, n in vecs:
                col[name] = cols[:, at:at + n]
                at += n
        ev_gain = cols[:, at:at + 2]

        silu_c = small[:, 0:8]
        one_m_lb, lb = small[:, 8:24], small[:, 24:40]
        lb_tmp = small[:, 40:56]
        scale0, shift0 = small[:, 56:64], small[:, 64:72]
        scale1, shift1 = small[:, 72:80], small[:, 80:88]
        scale_kv, shift_kv = small[:, 88:96], small[:, 96:104]
        ssum, mean_eps, rstd = small[:, 104:106], small[:, 106:107], small[:, 216:218]
        q_gain = small[:, 108:109]
        ev_q_gain = small[:, 109:110]
        eps_t = small[:, 110:111]
        row_max, row_neg = small[:, 112:116], small[:, 116:120]
        row_sum, row_inv = small[:, 120:124], small[:, 124:128]
        dl = small[:, 128:192].rearrange("p (h n) -> p h n", h=HA)
        w_idx = small[:, 192:200]
        top8 = small[:, 200:208]
        cnt, rest = small[:, 208:209], small[:, 209:210]
        mod_tmp = small[:, 210:214]
        forget_b = small[0:HA, 214:215]

        ps = ctx.enter_context(nc.psum_tensor("ps", [P, 8, HALF], F32))

        def unit_bank(u):
            return ps[:, u % 4, :]

        def y_bank(t, n):
            return ps[:, 4 + 2 * t + n, :]

        loaded = [sem(f"raw{s}_loaded") for s in range(NRAW)]
        hi_done, lo_done = sem("half_hi_written"), sem("half_lo_written")
        pe_used = sem("half_used_by_pe")
        mod_summed = sem("mod_piece_summed")
        h_hi, h_lo, h_used = sem("h_hi_written"), sem("h_lo_written"), sem("keys_h_read")
        self_hi, self_lo = sem("self_h_hi_written"), sem("self_h_lo_written")
        c_in, ident_in, masks_in, rows_a_in, rows_b_in, x_in, gate_b_in, out_stored = (sem(n) for n in (
            "c_in", "ident_in", "masks_in", "rows_a_in", "rows_b_in", "x_in", "gate_bias_in", "out_stored"))
        fb_in = sem("forget_bias_in")
        c_turned, rows_turned, cols_ready = sem("c_turned"), sem("rows_turned"), sem("cols_ready")
        silu_c_ready = sem("silu_c_ready")
        unit_ready = sem("unit_ready")
        unit_free = {"a": sem("unit_read_by_act"), "v": sem("unit_read_by_dve")}
        mod_cols, mod_read = sem("mod_cols_ready"), sem("mod_cols_read")
        x_done, rstd_done, xn_done = sem("x_done"), sem("x_rstd_done"), sem("xn_done")
        y_ready = sem("y_ready")
        act_chain, dve_chain, pool_chain = sem("act_step"), sem("dve_step"), sem("pool_step")

        def before(engine, u):
            return sum(1 for _, e in UNITS[:u + 1] if e == engine)

        def wait_loaded(eng, n):
            eng.wait_ge(loaded[n % NRAW], 16 * (n // NRAW + 1))

        def slot(n):
            return raw[:, n % NRAW, :]

        def by_k(v, k=KD):
            return v.rearrange("p (k n) -> p k n", k=k)

        HALVES, first_half = [], {}

        def add_half(n, src, dst):
            HALVES.append((n, at_slot[0] % NSPLIT, src, dst))
            at_slot[0] += 1

        at_slot = [0]
        for n, piece in enumerate(PIECES):
            kind = piece[0]
            first_half[n] = len(HALVES)
            if kind in ("mod", "pool_w"):
                continue
            if kind in ("a_out", "b_out", "ev_out", "od_out", "w2"):
                for j in range(2):
                    add_half(n, by_k(slot(n), 2)[:, j, :], lambda v: v)
            elif kind == "forget":
                src = by_k(slot(n)[:, 0:KD * HA]).rearrange("p k (a n) -> p k a n", a=1)
                add_half(n, src.to_broadcast([P, KD, 8, HA]), lambda v: v.rearrange("p (k a n) -> p k a n", k=KD, a=8))
            elif kind == "ev_small":
                w = by_k(slot(n)[:, 0:KD * 68])
                src = w[:, :, 0:HD2].rearrange("p k (a n) -> p k a n", a=1)
                add_half(n, src.to_broadcast([P, KD, 2, HD2]), lambda v: v.rearrange("p (k a n) -> p k a n", k=KD, a=2))
                add_half(n, w[:, :, 64:68], lambda v: by_k(v[:, 0:KD * 4]))
            elif kind == "ev_kv":
                w = by_k(slot(n))
                for g in range(2):
                    src = w[:, :, g * HD2:(g + 1) * HD2].rearrange("p k (a n) -> p k a n", a=1)
                    add_half(n, src.to_broadcast([P, KD, 2, HD2]),
                             lambda v: v.rearrange("p (k a n) -> p k a n", k=KD, a=2))
                add_half(n, w[:, :, P:2 * P], by_k)
            elif kind == "a_in" and 8 <= piece[1] < 16 or kind == "kv" and piece[1] >= 8 or kind == "od_in" and piece[1] >= 8:
                at_slot[0] += at_slot[0] % 2
                for j in range(2):
                    add_half(n, by_k(slot(n))[:, :, j * P:(j + 1) * P], ("pair", j))
            else:
                for j in range(2):
                    add_half(n, by_k(slot(n))[:, :, j * P:(j + 1) * P], by_k)
        first_half[len(PIECES)] = len(HALVES)

        def half_view(tensor, s):
            place, dst = HALVES[s][1], HALVES[s][3]
            if isinstance(dst, tuple):
                pair = by_k(tensor[:, (place - dst[1]) * PART:(place - dst[1] + 2) * PART])
                return pair[:, :, dst[1] * P:(dst[1] + 1) * P]
            return dst(tensor[:, place * PART:(place + 1) * PART])

        def half_flat(tensor, s):
            place = HALVES[s][1]
            return tensor[:, place * PART:(place + 1) * PART]

        def previous_in(s):
            return next((r for r in range(s - 1, -1, -1) if HALVES[r][1] == HALVES[s][1]), None)

        def wait_read(eng, stage, i):
            u = FIRST[stage] + i
            eng.wait_ge(unit_free[UNITS[u][1]], before(UNITS[u][1], u))

        half_use = {}
        unit_half = {}
        raw_use = {}
        for n, piece in enumerate(PIECES):
            if piece[0] == "mod":
                raw_use[n] = (mod_summed, 2 * piece[1] + piece[2] + 1)
            elif piece[0] != "pool_w":
                raw_use[n] = (lo_done, first_half[n + 1])

        chain = {"act": 0, "dve": 0, "pool": 0}

        def then(eng_name, eng, ins):
            s = {"act": act_chain, "dve": dve_chain, "pool": pool_chain}[eng_name]
            chain[eng_name] += 1
            ins.then_inc(s, 1)
            eng.wait_ge(s, chain[eng_name])

        S = {}

        def st(name):
            if name not in S:
                S[name] = sem(name)
            return S[name]

        for name in ("sig_ready ln_ready scan_ready exp_ready spread_ready spread_exp kin_ready "
                     "out_hi ot_split fx_split ds_split sb_split kst_turned kst_copied att_ready att_masked even_states state_ready state_saved o_ready "
                     "osq_ready ossq_ready orstd_ready o_used ot_ready "
                     "hsq_ready hssq_ready hrstd_ready "
                     "f_min f_ln nf_ready "
                     "fx_logits fx_max fx_exp fx_prob fx_turned fx_tcopied fx_o fx_out "
                     "ev_rel ev_relu ev_score_used "
                     "ev_mixed "
                     "ds_logits ds_max ds_exp ds_prob ds_turned ds_tcopied ds_o ds_out "
                     "up_silu g_full g_hi sb_z sb_ln sb_soft sb_masked sb_log sb_exp sb_sel sb_o sb_out"
                     ).split():
            st(name)

        a_in_at = [2048, 4096, 0, 6144]

        def col_tile(w, c0, n):
            return w.rearrange("(k p) n -> p k n", p=P)[:, :, c0:c0 + n]

        def row_tile(w, k0, nk):
            return w[k0 * P:(k0 + nk) * P, :].rearrange("(k p) n -> p k n", p=P)

        def piece_dma(n):
            kind, i = PIECES[n][0], PIECES[n][-1]
            s = slot(n)
            wide, rows = by_k(s), by_k(s, 2)
            if kind == "mod":
                m = PIECES[n][1]
                w, j = (a["mod_w"][0], m) if m < 6 else (a["mod_w"][1], m - 6) if m < 10 else \
                       (a["kv_mod_w"], m - 10) if m < 14 else (a["mod_w"][1], m - 10)
                return by_k(s, 4), row_tile(w, 4 * i, 4)[:, :, HALF * j:HALF * (j + 1)]
            if kind == "a_in":
                return wide, col_tile(a["a_w_in"][0], a_in_at[i // 8] + T * (i % 8), T)
            if kind == "kv":
                return wide, col_tile(a["kv_w"], T * i, T)
            if kind == "forget":
                return by_k(s[:, 0:KD * HA]), col_tile(a["kv_w"], 2 * W, HA)
            if kind == "b_in":
                return wide, col_tile(a["b_w_in"][0], T * i, T)
            if kind == "ev_small":
                return by_k(s[:, 0:KD * 68]), col_tile(a["ev_w_in_2"][0], 1024, 68)
            if kind in ("ev_qi", "ev_kv", "ev_q", "ev_u"):
                c0 = {"ev_qi": 768, "ev_kv": 512, "ev_q": T * i, "ev_u": 1092 + T * i}[kind]
                return wide, col_tile(a["ev_w_in_2"][0], c0, T)
            if kind == "pool_w":
                return by_k(s[:, 0:4 * P], 4), a["ev_pool_w_2"][0].rearrange("g c d -> c g d")
            if kind == "od_in":
                return wide, col_tile(a["od_w_qkv_2"][0], T * i, T)
            if kind in ("a_out", "b_out", "ev_out", "od_out"):
                w = {"a_out": "a_w_out", "b_out": "b_w_out", "ev_out": "ev_w_out_2", "od_out": "od_w_out_2"}[kind]
                return rows, row_tile(a[w][0], 2 * i, 2)
            layer = PIECES[n][1]
            if kind in ("w1", "w3"):
                return wide, col_tile(a[f"ffn_{kind}_2"][layer], T * i, T)
            return rows, row_tile(a["ffn_w2_2"][layer], 2 * i, 2)

        fz_b, k_in0, q_dec, k_in, k_st = (grid(n) for n in range(5))
        silu_g = grid(0)
        v_rows = [act_f32[:, t, KD * T:] for t in range(NT)]
        kst_sb = work[:, 0:512].rearrange("p (b t k) -> p b t k", b=2, t=2)
        att_sb = work[:, 512:1024].rearrange("p (b t c) -> p b t c", b=2, t=2)
        state = work[:, 1024:1792].rearrange("p (b n v) -> p b n v", b=2, n=3)
        o_sq = work[:, 1792:2304].rearrange("p (b t) -> p b t", b=2)
        o_r = work[:, 2304:2816].rearrange("p (b t) -> p b t", b=2)
        o_tmp = work[:, 2816:3072]
        o_full = work[:, 3072:3584].rearrange("p (b t) -> p b t", b=2)
        h_full = work[:, 2560:3584].rearrange("p (b n) -> p b n", b=2)
        h_self = big[:, 4, NT * D:].rearrange("p (k t) -> p k t", k=KD)

        kN, v2_rows, qN, silu_g2 = grid(0), big[:, 1, :].rearrange("p (t n) -> p t n", t=NT), grid(2), grid(3)
        h_sq = work[:, 0:1024].rearrange("p (b n) -> p b n", b=2)
        h_r = work[:, 1024:2048].rearrange("p (b n) -> p b n", b=2)
        f_a, f_b = work[0:HA, 2048:2048 + T], work[0:HA, 2304:2304 + T]
        neg_f = work[0:HA, 2688:2688 + T]
        lg = work[:, 0:2 * S3].rearrange("p (b n) -> p b n", b=2)
        prob = work[:, 768:768 + 3 * S3].rearrange("p (b n) -> p b n", b=3)
        probT = work[:, 1920:1920 + 2 * S3].rearrange("p (b n) -> p b n", b=2)

        evq = big[:, 0, 0:1024].rearrange("p (c t) -> p c t", c=4)
        evk = big[:, 0, 1024:1536].rearrange("p (g t) -> p g t", g=2)
        evqi = big[:, 0, 1536:2048].rearrange("p (c t) -> p c t", c=2)
        evki = big[:, 0, 2048:2304]
        evv = big[:, 0, 2304:2560].rearrange("p (t d) -> p t d", t=2)
        PAD = 16
        u_pad = big[:, 1, 0:4 * (PAD + T)].rearrange("p (g t) -> p g t", g=4)
        run_a = big[:, 1, 1088:1088 + PAD + T]
        run_b = big[:, 1, 1360:1360 + PAD + T]
        mixed = big[:, 1, 1632:1632 + 4 * T].rearrange("p (g t) -> p g t", g=4)
        pooled = big[:, 1, 2656:2656 + 4 * T].rearrange("p (g t) -> p g t", g=4)
        score = big[:, 3, 0:S3]
        relu_s = big[:, 3, 384:384 + 2 * S3].rearrange("p (b n) -> p b n", b=2)
        cut = big[:, 3, 1152:1152 + T]
        sel_gt = big[:, 3, 1536:1536 + T]
        sel_eq = big[:, 3, 1792:1792 + T]
        sel_pre = big[:, 3, 2048:2048 + T]
        ev_bias_t = big[:, 3, 2304:2304 + S3]
        OUT2 = 8

        silu_a = work[:, 0:512].rearrange("p (b t) -> p b t", b=2)
        g_full = work[:, 512:1024].rearrange("p (b t) -> p b t", b=2)

        odq, odk = grid(0, 8), big[:, 0, 2048:4096].rearrange("p (h t) -> p h t", h=8)
        odv = big[:, 1, 0:2048].rearrange("p (t n) -> p t n", t=NT)

        def sb_ln_t(i):
            return work[:, (i % 2) * S3:(i % 2) * S3 + S3]

        def sb_brk(i):
            return work[:, (2 + i % 3) * S3:(2 + i % 3) * S3 + S3]

        def sb_prob(i):
            return work[:, (5 + i % 3) * S3:(5 + i % 3) * S3 + S3]

        block = ctx.enter_context(nc.Block())

        vec_rows = [work[:, 0:P], work[:, P:2 * P]]
        c_row = work[0:KD, 2 * P:3 * P]
        ROWS_A = sum(n for _, n in VEC_A)

        def vector_rows(eng, vecs, rows, sem_):
            r = 0
            for name, n in vecs:
                src = a[name]
                if len(src.shape) == 2:
                    src = src.rearrange("a b -> (a b)")
                eng.dma_start(rows[r:r + n, :], src.rearrange("(r c) -> r c", c=P)).then_inc(sem_, 16)
                r += n

        @block.gpsimd
        def _(pool):
            pool.memset(vec_rows[1], 0.0).then_inc(pool_chain, 1)
            pool.wait_ge(pool_chain, 1)
            pool.wait_ge(mod_summed, 8)
            vector_rows(pool, VEC_B, vec_rows[1], rows_b_in)
            r = sum(n for _, n in VEC_B)
            for i, name in enumerate(("ev_q_norm_g_2", "ev_k_norm_g_2")):
                for half in range(2):
                    pool.dma_start(vec_rows[1][r + i:r + i + 1, HD2 * half:HD2 * (half + 1)], a[name])\
                        .then_inc(rows_b_in, 16)
            pool.dma_start(gate[:, :], a["mod_b"][0:1, 2 * D:3 * D].to_broadcast([P, D])).then_inc(gate_b_in, 16)
            pool.dma_start(cst[:, 256:], const[:, 256:]).then_inc(masks_in, 16)
            pool.dma_start(att_mask[:, :, :], mask.rearrange("p (t c) -> p t c", t=2)).then_inc(masks_in, 16)
            pool.dma_start(forget_b, a["kv_fb"].rearrange("(h a) -> h a", a=1)).then_inc(fb_in, 16)
            def split_output(i, full, done, freed, chunk):
                pool.wait_ge(done, i + 1)
                pool.tensor_copy(act_hi[:, chunk, :], full).then_inc(st("out_hi"), 1)
                outs[0] += 1
                pool.wait_ge(st("out_hi"), outs[0])
                pool.tensor_tensor(act_lo[:, chunk, :], full, act_hi[:, chunk, :].bitcast(F32), ALU.subtract)\
                    .then_inc(freed, 1)

            outs = [0]
            for h in range(HA):
                split_output(h, o_full[:, h % 2, :], st("ot_ready"), st("ot_split"), h)
            pool.wait_ge(x_done, 4)
            pool.dma_start(gate[:, :], a["mod_b"][1:2, 2 * D:3 * D].to_broadcast([P, D])).then_inc(gate_b_in, 16)
            for u in range(4):
                pair = slice(2 * u, 2 * u + 2)
                wait_read(pool, "norm1", u)
                pool.tensor_copy(act_hi[:, pair, :], h_self[:, pair, :]).then_inc(self_hi, 1)
                pool.wait_ge(self_hi, u + 1)
                pool.tensor_tensor(act_lo[:, pair, :], h_self[:, pair, :], act_hi[:, pair, :].bitcast(F32),
                                   ALU.subtract).then_inc(self_lo, 1)
            for h in range(HA):
                split_output(h, o_full[:, h % 2, :], st("fx_out"), st("fx_split"), h)
            def link(ins):
                then("pool", pool, ins)

            chain["pool"] = 1
            pool.wait_ge(st("fx_out"), HA)
            pool.memset(u_pad[:, :, 0:PAD], 0.0)
            pool.memset(run_a[:, 0:PAD], 0.0)
            link(pool.memset(run_b[:, 0:PAD], 0.0))
            for g in range(4):
                wait_read(pool, "ev_u", g // 2)
                u = u_pad[:, g, :]
                src, dst, spare = u, run_a, run_b
                step = 1
                for _ in range(g + 1):
                    link(pool.tensor_tensor(dst[:, PAD:], src[:, PAD:], src[:, PAD - step:PAD + T - step], ALU.add))
                    src, dst, spare = dst, spare, dst
                    step *= 2
                pool.tensor_tensor(mixed[:, g, 0:PAD], src[:, PAD:2 * PAD], inv_count[:, g, :], ALU.mult)
                link(pool.tensor_scalar(mixed[:, g, PAD:], src[:, 2 * PAD:], 1.0 / step, None, ALU.mult))
                pool.tensor_tensor(mixed[:, g, :], mixed[:, g, :], u[:, PAD:], ALU.subtract).then_inc(st("ev_mixed"), 1)
            for c in range(HE // 2):
                split_output(c, o_full[:, c % 2, :], st("ds_out"), st("ds_split"), OUT2 + c)

            for i in range(HO + 6):
                if i >= 6 and i % 2 == 0:
                    c = (i - 6) // 2
                    split_output(c, o_full[:, c % 2, :], st("sb_out"), st("sb_split"), OUT2 + c)
                if i < HO:
                    pool.wait_ge(st("sb_soft"), i + 1)
                    part = sb_brk(i).rearrange("p (b t) -> p b t", b=3)[:, 0:3:2, :]
                    pool.affine_select(out=part, in_=part, compare_op=ALU.is_gt, fill=0.0, base=0,
                                       pattern=[[0, 2], [1, P]], channel_multiplier=-1).then_inc(st("sb_masked"), 1)
                if 2 <= i < HO + 2:
                    pool.wait_ge(st("sb_exp"), i - 1)
                    part = sb_prob(i - 2).rearrange("p (b t) -> p b t", b=3)[:, 0:3:2, :]
                    pool.affine_select(out=part, in_=part, compare_op=ALU.is_gt, fill=0.0, base=0,
                                       pattern=[[0, 2], [1, P]], channel_multiplier=-1).then_inc(st("sb_sel"), 1)

        down_half = {}

        @block.tensor
        def _(pe):
            unit = [0]

            def open_unit(stage):
                u = unit[0]
                assert UNITS[u][0] == stage, (u, UNITS[u], stage)
                if u >= 4:
                    pe.wait_ge(unit_free[UNITS[u - 4][1]], before(UNITS[u - 4][1], u - 4))
                unit[0] += 1
                return unit_bank(u)

            halves_used, y_count, half = [0], [0], [0]

            def used(s, ins=None):
                if ins is None:
                    half_use[s] = (unit_ready, unit[0])
                else:
                    halves_used[0] += 1
                    ins.then_inc(pe_used, 1)
                    half_use[s] = (pe_used, halves_used[0])

            def next_half(kind):
                s = half[0]
                assert PIECES[HALVES[s][0]][0] == kind, (PIECES[HALVES[s][0]], kind)
                half[0] += 1
                pe.wait_ge(hi_done, s + 1)
                return s

            def wait_lo(s):
                pe.wait_ge(lo_done, s + 1)

            def close_unit(ins, s):
                ins.then_inc(unit_ready, 1)
                unit_half[unit[0] - 1] = s

            def features(dst, s, base, fresh=None):
                wh, wl = by_k(half_flat(w_hi, s)), by_k(half_flat(w_lo, s))
                if fresh is not None:
                    if fresh < 2:
                        lo_sem, count = h_lo, 4 * fresh
                    else:
                        lo_sem, count = unit_free["v"], before("v", FIRST[f"norm{fresh}"]) - 1
                    for k in range(KD):
                        if k % 2 == 0:
                            pe.wait_ge(h_hi, 4 * fresh + k // 2 + 1)
                        pe.matmul(dst, wh[:, k, :], act_hi[:, base + k, :], start=(k == 0), stop=False)
                    wait_lo(s)
                    for k in range(KD):
                        pe.matmul(dst, wl[:, k, :], act_hi[:, base + k, :], start=False, stop=False)
                    for k in range(KD):
                        if k % 2 == 0:
                            pe.wait_ge(lo_sem, count + k // 2 + 1)
                        ins = pe.matmul(dst, wh[:, k, :], act_lo[:, base + k, :], start=False, stop=(k == KD - 1))
                    return ins
                for k in range(KD):
                    pe.matmul(dst, wh[:, k, :], act_hi[:, base + k, :], start=(k == 0), stop=False)
                    pe.matmul(dst, wh[:, k, :], act_lo[:, base + k, :], start=False, stop=False)
                wait_lo(s)
                for k in range(KD):
                    ins = pe.matmul(dst, wl[:, k, :], act_hi[:, base + k, :], start=False, stop=(k == KD - 1))
                return ins

            def project_features(stage, kind, base, fresh=None):
                bank = open_unit(stage)
                s = next_half(kind)
                used(s, features(bank[:, 0:T], s, base, fresh))
                s = next_half(kind)
                close_unit(features(bank[:, T:2 * T], s, base), s)
                used(s)

            def project_tokens(stage, kind, base):
                banks = [open_unit(stage) for _ in range(NT)]
                for piece in range(2):
                    s = next_half(kind)
                    s2 = next_half(kind)
                    assert HALVES[s][1] % 2 == 0
                    place = HALVES[s][1]
                    wh = by_k(w_hi[:, place * PART:(place + 2) * PART])
                    wl = by_k(w_lo[:, place * PART:(place + 2) * PART])
                    out_cols = slice(piece * T, (piece + 1) * T)
                    for t in range(NT):
                        dst, tok = banks[t][:, out_cols], slice(t * P, (t + 1) * P)
                        for k in range(KD):
                            pe.matmul(dst, act_hi[:, base + k, tok], wh[:, k, :], start=(k == 0), stop=False)
                            pe.matmul(dst, act_lo[:, base + k, tok], wh[:, k, :], start=False, stop=False)
                        if t == 0:
                            wait_lo(s2)
                        for k in range(KD):
                            ins = pe.matmul(dst, act_hi[:, base + k, tok], wl[:, k, :], start=False, stop=(k == KD - 1))
                        if piece == 1:
                            ins.then_inc(unit_ready, 1)
                            unit_half[unit[0] - 2 + t] = s2
                    if piece == 0:
                        used(s, ins)
                        half_use[s2] = half_use[s]
                    else:
                        used(s)
                        used(s2)

            def out_half(kind, chunk, first, last):
                s = next_half(kind)
                wh, wl = half_flat(w_hi, s), half_flat(w_lo, s)
                parts = [(y_bank(t, n), slice(t * P, (t + 1) * P), slice(n * HALF, (n + 1) * HALF))
                         for t in range(NT) for n in range(2)]
                if last:
                    wait_lo(s)
                for group in ([[p] for p in parts] if last else [parts]):
                    for dst, tok, cols_ in group:
                        pe.matmul(dst, act_hi[:, chunk, tok], wh[:, cols_], start=first, stop=False)
                        pe.matmul(dst, act_lo[:, chunk, tok], wh[:, cols_], start=False, stop=False)
                    if not last:
                        wait_lo(s)
                    for dst, tok, cols_ in group:
                        ins = pe.matmul(dst, act_hi[:, chunk, tok], wl[:, cols_], start=False, stop=last)
                        if last:
                            ins.then_inc(y_ready, 1)
                if last:
                    y_count[0] += 4
                    half_use[s] = (y_ready, y_count[0])
                else:
                    used(s, ins)
                return s

            def out_project(kind, chunks, base, ready=None):
                for k in range(chunks):
                    if ready is not None:
                        ready(k)
                    out_half(kind, base + k, k == 0, k == chunks - 1)

            def norm(j):
                first = unit[0]
                banks = [open_unit(f"norm{j}") for _ in range(4)]
                for t in range(NT):
                    for k in range(KD):
                        if k % 4 == 0:
                            pe.wait_ge(xn_done, 4 * j + 2 * t + k // 4 + 1)
                        at = (k % 2) * T + t * P
                        ins = pe.transpose(banks[k // 2][:, at:at + P], xn[:, t, k * P:(k + 1) * P], ident)
                        if t == NT - 1 and k % 2 == 1:
                            ins.then_inc(unit_ready, 1)
                            unit_half[first + k // 2] = half[0] - 1

            def mod_columns(m):
                if m >= 2:
                    pe.wait_ge(mod_read, m - 1)
                bank = ps[:, 6 + m % 2, :]
                pe.wait_ge(mod_summed, 2 * (m + 1))
                if m in (4, 5, 14, 15):
                    ins = pe.matmul(bank, ones, acc[:, m % 2, :], start=True, stop=True)
                else:
                    for c in range(4):
                        ins = pe.matmul(bank[:, c:c + 1], acc[:, m % 2, c * P:(c + 1) * P], ones[:, 0:1],
                                        start=True, stop=True)
                ins.then_inc(mod_cols, 1)

            pe.wait_ge(c_in, 16)
            pe.wait_ge(ident_in, 16)
            pe.transpose(ps[:, 5, 0:KD], c_row, ident[0:KD, 0:KD]).then_inc(c_turned, 1)
            pe.wait_ge(rows_a_in, 16 * len(VEC_A))
            pe.transpose(ps[:, 4, 0:ROWS_A], vec_rows[0][0:ROWS_A, :], ident[0:ROWS_A, 0:ROWS_A])\
                .then_inc(rows_turned, 1)
            mod_columns(0)
            mod_columns(1)
            mod_columns(2)
            mod_columns(3)
            norm(0)

            mod_end = {}
            for n, piece in enumerate(PIECES):
                if piece[0] == "mod" and piece[1] >= 4 and piece[2] == 1:
                    k = next(r for r in PIECES[n:] if r[0] in ("a_in", "b_in"))
                    mod_end.setdefault(k, []).append(piece[1])
            for n in range(32):
                if n // 8 != 1:
                    project_features(("a_f", "", "a_q", "a_g")[n // 8], "a_in", SELF, 0 if n == 0 else None)
                elif n % 2 == 1:
                    project_tokens("a_i", "a_in", SELF)
                for m in mod_end.get(("a_in", n), ()):
                    mod_columns(m)
                if n == 4:
                    pe.wait_ge(rows_b_in, 16 * (len(VEC_B) + 4))
                    pe.transpose(ps[:, 4, P:2 * P], vec_rows[1], ident).then_inc(rows_turned, 1)

            def keys_turned(h):
                pe.wait_ge(st("kin_ready"), 2 * (h + 1))
                if h >= 2:
                    pe.wait_ge(st("kst_copied"), h - 1)
                for t in range(NT):
                    ins = pe.transpose(ps[:, 6 + h % 2, t * P:(t + 1) * P],
                                       k_st[:, h, t * P:(t + 1) * P], ident)
                ins.then_inc(st("kst_turned"), 1)

            def scores(h):
                wait_read(pe, "a_q", h // 2)
                if h >= 2:
                    pe.wait_ge(st("att_masked"), h - 1)
                for t in range(NT):
                    sl = slice(t * P, (t + 1) * P)
                    ins = pe.matmul(ps[:, 4 + h % 2, sl], k_in[:, h, sl], q_dec[:, h, sl], start=True, stop=True)
                ins.then_inc(st("att_ready"), 1)

            def states(h, chunks):
                if chunks[0] == 0:
                    pe.wait_ge(st("kst_copied"), h + 1)
                    if h >= 2:
                        pe.wait_ge(st("state_saved"), h - 1)
                else:
                    pe.wait_ge(st("even_states"), h + 1)
                for n in chunks:
                    rows = slice(CHUNK * (n % 2), CHUNK * (n % 2) + CHUNK)
                    ins = pe.matmul(ps[:, h % 2, n * P:(n + 1) * P], kst_sb[rows, h % 2, n // 2, :],
                                    v_rows[n // 2][rows, h * P:(h + 1) * P], start=True, stop=True)
                ins.then_inc(st("even_states") if chunks[0] == 0 else st("state_ready"), 1)

            def outputs(h):
                pe.wait_ge(st("att_masked"), h + 1)
                pe.wait_ge(st("state_saved"), h + 1)
                if h >= 2:
                    pe.wait_ge(st("o_used"), h - 1)
                bank = ps[:, 2 + h % 2, :]
                for t in range(NT):
                    pe.matmul(bank[:, t * P:(t + 1) * P], v_rows[t][:, h * P:(h + 1) * P], att_sb[:, h % 2, t, :],
                              start=True, stop=False)
                    for n in range(max(1, 2 * t), 2 * t + 2):
                        sl = slice(n * CHUNK, (n + 1) * CHUNK)
                        ins = pe.matmul(bank[:, sl], state[:, h % 2, n - 1, :], q_dec[:, h, sl],
                                        start=False, stop=(n == 2 * t + 1))
                ins.then_inc(st("o_ready"), 1)

            def square_sums(h):
                pe.wait_ge(st("osq_ready"), h + 1)
                pe.matmul(ps[:, 2 + h % 2, T:2 * T], ones, o_sq[:, h % 2, :], start=True, stop=True)\
                    .then_inc(st("ossq_ready"), 1)

            pe.wait_ge(unit_free["a"], before("a", unit[0] - 1))
            pe.wait_ge(unit_free["v"], before("v", unit[0] - 1))
            pe.wait_ge(mod_read, 14)
            for i in range(HA + 3):
                if i < HA:
                    keys_turned(i)
                    scores(i)
                if 1 <= i <= HA:
                    states(i - 1, (0, 2))
                if 2 <= i <= HA + 1:
                    outputs(i - 2)
                if 1 <= i <= HA:
                    states(i - 1, (1,))
                if i >= 3:
                    square_sums(i - 3)
            pe.wait_ge(st("o_used"), HA)
            out_project("a_out", HA, 0, lambda k: pe.wait_ge(st("ot_split"), k + 1))

            norm(1)

            def head_square_sums(mat, count):
                pe.wait_ge(st("hsq_ready"), count + 1)
                if count >= 2:
                    pe.wait_ge(st("hrstd_ready"), count - 1)
                pe.matmul(ps[:, 4 + count % 2, :], mat, h_sq[:, count % 2, :], start=True, stop=True)\
                    .then_inc(st("hssq_ready"), 1)

            pe.wait_ge(x_done, 4)
            for n in range(8):
                project_features("k", "kv", KV, 1 if n == 0 else None)
                if n >= 1:
                    head_square_sums(ones, n - 1)
            for n in range(4):
                project_tokens("v", "kv", KV)
                if n == 0:
                    head_square_sums(ones, 7)
            bank = open_unit("forget")
            s = next_half("forget")
            close_unit(features(bank[:, 0:T], s, KV), s)
            used(s)
            pe.wait_ge(self_lo, 4)
            for n in range(16):
                project_features("q" if n < 8 else "g", "b_in", SELF)
                if 1 <= n <= 8:
                    head_square_sums(ones, 8 + n - 1)
                for m in mod_end.get(("b_in", n), ()):
                    mod_columns(m)

            def softmax_heads(pre, heads, logits, pv):
                for i in range(heads + 3):
                    if i < heads:
                        if i >= 2:
                            pe.wait_ge(st(pre + "_max"), i - 1)
                        logits(i, ps[:, 4 + i % 2, :]).then_inc(st(pre + "_logits"), 1)
                    if 2 <= i < heads + 2:
                        h = i - 2
                        pe.wait_ge(st(pre + "_prob"), h + 1)
                        if h >= 2:
                            pe.wait_ge(st(pre + "_tcopied"), h - 1)
                        for b in range(3):
                            ins = pe.transpose(ps[:, 6 + h % 2, b * P:(b + 1) * P], prob[:, h % 3, b * P:(b + 1) * P], ident)
                        ins.then_inc(st(pre + "_turned"), 1)
                    if i >= 3:
                        h = i - 3
                        pe.wait_ge(st(pre + "_tcopied"), h + 1)
                        pv(h)

            def fox_logits(h, bank):
                if h % 2 == 0:
                    wait_read(pe, "q", h // 2)
                if h == 0:
                    pe.wait_ge(st("nf_ready"), 1)
                one = ident[0:HA, h:h + 1].to_broadcast([HA, P])
                for t in range(NT):
                    o = bank[:, P * t:P * t + P * (t + 1)]
                    pe.matmul(o, qN[:, h, t * P:(t + 1) * P], kN[:, h, 0:P * (t + 1)], start=True, stop=False)
                    ins = pe.matmul(o, one, neg_f[:, 0:P * (t + 1)], start=False, stop=True)
                return ins

            def fox_pv(h):
                if h >= 2:
                    pe.wait_ge(st("fx_out"), h - 1)
                bank = ps[:, h % 2, :]
                vh = lambda s: v2_rows[:, s, h * P:(h + 1) * P]
                pe.matmul(bank[:, 0:P], vh(0), probT[:, h % 2, 0:P], start=True, stop=True)
                pe.matmul(bank[:, P:T], vh(0), probT[:, h % 2, P:2 * P], start=True, stop=False)
                pe.matmul(bank[:, P:T], vh(1), probT[:, h % 2, 2 * P:3 * P], start=False, stop=True)\
                    .then_inc(st("fx_o"), 1)

            pe.wait_ge(unit_free["a"], before("a", unit[0] - 1))
            pe.wait_ge(unit_free["v"], before("v", unit[0] - 1))
            pe.wait_ge(mod_read, 16)
            pe.wait_ge(st("hrstd_ready"), 16)
            softmax_heads("fx", HA, fox_logits, fox_pv)
            out_project("b_out", HA, 0, lambda k: pe.wait_ge(st("fx_split"), k + 1))

            norm(2)
            count = 16
            project_features("ev_i", "ev_qi", SELF, 2)
            bank = open_unit("ev_i")
            s = next_half("ev_small")
            used(s, features(bank[:, 0:T], s, SELF))
            s = next_half("ev_small")
            wh, wl = (by_k(half_flat(w, s)[:, 0:KD * 4]) for w in (w_hi, w_lo))
            wait_lo(s)
            for t in range(NT):
                dst, tok = bank[:, T + 4 * t:T + 4 * t + 4], slice(t * P, (t + 1) * P)
                for k in range(KD):
                    pe.matmul(dst, act_hi[:, k, tok], wh[:, k, :], start=(k == 0), stop=False)
                    pe.matmul(dst, act_lo[:, k, tok], wh[:, k, :], start=False, stop=False)
                    ins = pe.matmul(dst, act_hi[:, k, tok], wl[:, k, :], start=False, stop=(k == KD - 1))
            close_unit(ins, s)
            used(s)
            pe.wait_ge(x_done, 8)
            bank = open_unit("ev_k")
            s = next_half("ev_kv")
            used(s, features(bank[:, 0:T], s, SELF))
            wait_read(pe, "ev_i", 1)
            for h in range(HIDX):
                rows = slice(HD2 * (h % 2), HD2 * (h % 2) + HD2)
                for t in range(NT):
                    ins = pe.matmul(ps[:, 4 + h, P * t:P * t + P * (t + 1)], evqi[rows, h // 2, t * P:(t + 1) * P],
                                    evki[rows, 0:P * (t + 1)], start=True, stop=True)
                ins.then_inc(st("ev_rel"), 1)
            s = next_half("ev_kv")
            close_unit(features(bank[:, T:2 * T], s, SELF), s)
            used(s)
            bank = open_unit("ev_v")
            s = next_half("ev_kv")
            wh, wl = by_k(half_flat(w_hi, s)), by_k(half_flat(w_lo, s))
            wait_lo(s)
            for t in range(NT):
                dst, tok = bank[:, t * P:(t + 1) * P], slice(t * P, (t + 1) * P)
                for k in range(KD):
                    pe.matmul(dst, act_hi[:, k, tok], wh[:, k, :], start=(k == 0), stop=False)
                    pe.matmul(dst, act_lo[:, k, tok], wh[:, k, :], start=False, stop=False)
                    ins = pe.matmul(dst, act_hi[:, k, tok], wl[:, k, :], start=False, stop=(k == KD - 1))
            close_unit(ins, s)
            used(s)
            pe.wait_ge(st("ev_relu"), HIDX)
            head_square_sums(ones64, 16)
            project_features("ev_q", "ev_q", SELF)
            project_features("ev_q", "ev_q", SELF)
            head_square_sums(ones64, 17)
            project_features("ev_u", "ev_u", SELF)
            head_square_sums(ones64, 18)
            project_features("ev_u", "ev_u", SELF)

            def ds_logits(h, bank):
                if h == 0:
                    wait_read(pe, "ev_q", 1)
                rows = slice(HD2 * (h % 2), HD2 * (h % 2) + HD2)
                for t in range(NT):
                    ins = pe.matmul(bank[:, P * t:P * t + P * (t + 1)], evq[rows, h // 2, t * P:(t + 1) * P],
                                    evk[rows, h // 4, 0:P * (t + 1)], start=True, stop=True)
                return ins

            def ds_pv(h):
                if h % 2 == 0 and h >= 4:
                    pe.wait_ge(st("ds_out"), h // 2 - 1)
                rows = slice(HD2 * (h % 2), HD2 * (h % 2) + HD2)
                bank = ps[rows, (h // 2) % 2, :]
                vh = lambda s: evv[:, s, HD2 * (h // 4):HD2 * (h // 4) + HD2]
                pe.matmul(bank[:, 0:P], vh(0), probT[:, h % 2, 0:P], start=True, stop=True)
                pe.matmul(bank[:, P:T], vh(0), probT[:, h % 2, P:2 * P], start=True, stop=False)
                pe.matmul(bank[:, P:T], vh(1), probT[:, h % 2, 2 * P:3 * P], start=False, stop=True)\
                    .then_inc(st("ds_o"), 1)

            pe.wait_ge(unit_free["a"], before("a", unit[0] - 1))
            pe.wait_ge(unit_free["v"], before("v", unit[0] - 1))
            softmax_heads("ds", HE, ds_logits, ds_pv)
            pe.wait_ge(st("ds_out"), HE // 2)
            n = AT[("pool_w", 0)]
            wait_loaded(pe, n)
            wp = by_k(slot(n)[:, 0:4 * P], 4)
            for pair in range(2):
                bank = open_unit("ev_pool")
                for j in range(2):
                    g = 2 * pair + j
                    pe.wait_ge(st("ev_mixed"), g + 1)
                    ins = pe.matmul(bank[:, j * T:(j + 1) * T], wp[:, g, :], mixed[:, g, :], start=True, stop=True)
                close_unit(ins, half[0] - 1)
            raw_use[n] = (unit_ready, unit[0])
            out_project("ev_out", 8, OUT2, lambda k: pe.wait_ge(st("ds_split"), k + 1) if k < 4 else
                        wait_read(pe, "ev_pool", (k - 4) // 2))

            def feed_forward(layer, xs, fresh):
                def up(i):
                    banks = [open_unit(f"up{layer}") for _ in range(2)]
                    for j in range(2):
                        s = next_half("w1")
                        used(s, features(banks[j][:, 0:T], s, SELF, fresh if i == 0 and j == 0 else None))
                    for j in range(2):
                        s = next_half("w3")
                        features(banks[j][:, T:2 * T], s, SELF).then_inc(unit_ready, 1)
                        half_use[s] = (unit_ready, unit[0] - 1 + j)
                        unit_half[unit[0] - 2 + j] = s

                def down(i):
                    if i == 0:
                        pe.wait_ge(x_done, xs)
                    for c in (2 * i, 2 * i + 1):
                        wait_read(pe, f"up{layer}", c)
                        down_half[layer, c] = out_half("w2", 8 + c % 8, c == 0, c == FC - 1)

                for i in range(FC // 2 + 2):
                    if i < FC // 2:
                        up(i)
                    if i >= 2:
                        down(i - 2)

            norm(3)
            feed_forward(0, 12, 3)

            norm(4)
            for n in range(8):
                project_features("od_q" if n < 4 else "od_k", "od_in", SELF, 4 if n == 0 else None)
            for n in range(2):
                project_tokens("od_v", "od_in", SELF)

            def z_scores(h):
                if h >= 4:
                    pe.wait_ge(st("sb_exp"), h - 3)
                rows = slice(HD2 * (h % 2), HD2 * (h % 2) + HD2)
                bank = ps[:, 4 + h % 4, :]
                pe.matmul(bank[:, 0:T], odk[rows, h // 2, 0:P], odq[rows, h // 2, :], start=True, stop=True)
                pe.matmul(bank[:, T:S3], odk[rows, h // 2, P:T], odq[rows, h // 2, P:T], start=True, stop=True)\
                    .then_inc(st("sb_z"), 1)

            def minus_breaks(h):
                pe.wait_ge(st("sb_masked"), h + 1)
                bank, b = ps[:, 4 + h % 4, :], sb_brk(h)
                rows = slice(HD2 * (h % 2), HD2 * (h % 2) + HD2)
                pe.matmul(bank[:, 0:T], odk[rows, h // 2, 0:P], odq[rows, h // 2, :], start=True, stop=False)
                pe.matmul(bank[:, 0:T], neg_after, b[:, 0:T], start=False, stop=False)
                pe.matmul(bank[:, P:T], neg_ones, b[:, T:S3], start=False, stop=True)
                pe.matmul(bank[:, T:S3], odk[rows, h // 2, P:T], odq[rows, h // 2, P:T], start=True, stop=False)
                pe.matmul(bank[:, T:S3], neg_after, b[:, T:S3], start=False, stop=True).then_inc(st("sb_log"), 1)

            def weighted_values(h):
                pe.wait_ge(st("sb_sel"), h + 1)
                if h % 2 == 0 and h >= 4:
                    pe.wait_ge(st("sb_out"), h // 2 - 1)
                rows = slice(HD2 * (h % 2), HD2 * (h % 2) + HD2)
                bank, pr = ps[rows, (h // 2) % 2, :], sb_prob(h)
                vh = lambda s: odv[:, s, h * HD2:(h + 1) * HD2]
                pe.matmul(bank[:, 0:T], vh(0), pr[:, 0:T], start=True, stop=False)
                pe.matmul(bank[:, P:T], vh(1), pr[:, T:S3], start=False, stop=True).then_inc(st("sb_o"), 1)

            pe.wait_ge(unit_free["a"], before("a", unit[0] - 1))
            pe.wait_ge(unit_free["v"], before("v", unit[0] - 1))
            pe.wait_ge(x_done, 16)
            for i in range(HO + 4):
                if i < HO:
                    z_scores(i)
                if 2 <= i < HO + 2:
                    minus_breaks(i - 2)
                if i >= 4:
                    weighted_values(i - 4)
            out_project("od_out", 8, OUT2, lambda k: pe.wait_ge(st("sb_split"), k + 1))
            norm(5)
            feed_forward(1, 20, 5)

        @block.sync
        def _(sp):
            sp.dma_start(c_row, a["c"].rearrange("a (r c) -> (a r) c", c=P)).then_inc(c_in, 16)
            sp.dma_start(cst[:, 0:256], const[:, 0:256]).then_inc(ident_in, 16)
            for n in range(len(PIECES)):
                if n >= NRAW:
                    sp.wait_ge(*raw_use[n - NRAW])
                dst, src = piece_dma(n)
                sp.dma_start(dst, src).then_inc(loaded[n % NRAW], 16)
                if n == 2:
                    vector_rows(sp, VEC_A, vec_rows[0], rows_a_in)
                if n == 6:
                    sp.dma_start(x[:, :, :], a["x"][0].rearrange("(t p) n -> p t n", p=P)).then_inc(x_in, 16)
            for t in range(NT):
                sp.wait_ge(x_done, 4 * 5 + 2 * (t + 1))
                sp.dma_start(out[0, t * P:(t + 1) * P, :], x[:, t, :]).then_inc(out_stored, 16)
            sp.wait_ge(out_stored, 16 * NT)

        @block.scalar
        def _(act):
            def link(ins):
                then("act", act, ins)

            split = [0]

            def advance(upto):
                while split[0] <= min(upto, len(HALVES) - 1):
                    s = split[0]
                    n = HALVES[s][0]
                    wait_loaded(act, n)
                    for r in (s, s + 1) if isinstance(HALVES[s][3], tuple) and HALVES[s][3][1] == 0 else (s,):
                        if previous_in(r) is not None:
                            act.wait_ge(*half_use[previous_in(r)])
                    act.activation(half_view(w_hi, s), HALVES[s][2], ACT.Copy).then_inc(hi_done, 1)
                    split[0] += 1

            def unit_of(stage, i):
                u = FIRST[stage] + i
                advance(unit_half[u] + NSPLIT - 1)
                act.wait_ge(unit_ready, u + 1)
                return unit_bank(u)

            def ln_exp_tables():
                act.preload_act_table_set("natural_log_exp_and_others")

            def norm(j, base, scale, shift=None):
                ln_exp_tables()
                for t in range(NT):
                    for n in range(2):
                        if j == 0 and t + n == 0:
                            act.wait_ge(x_in, 16)
                        if j > 0:
                            act.wait_ge(x_done, 4 * (j - 1) + 2 * t + n + 1)
                        sl = slice(n * HALF, (n + 1) * HALF)
                        link(act.activation(xn[:, t, sl], x[:, t, sl], ACT.Square, accum_out=ssum[:, n:n + 1]))
                        if n == 0:
                            link(act.activation(mean_eps, ssum[:, 0:1], ACT.Identity, scale=1.0 / D, bias=eps_t))
                    link(act.activation(rstd[:, t:t + 1], ssum[:, 1:2], ACT.Ln, scale=1.0 / D, bias=mean_eps))
                    act.activation(rstd[:, t:t + 1], rstd[:, t:t + 1], ACT.Exp, scale=-0.5).then_inc(rstd_done, 1)
                if j == 0:
                    act.wait_ge(mod_read, 4)
                for u in range(4):
                    act.wait_ge(unit_ready, FIRST[f"norm{j}"] + u + 1)
                    for k in (2 * u, 2 * u + 1):
                        ins = scaled(act_hi[:, base + k, :], j, k, scale, shift)
                    ins.then_inc(h_hi, 1)

            def scaled(dst, j, k, scale, shift):
                bank = unit_bank(FIRST[f"norm{j}"] + k // 2)
                return act.activation(dst, bank[:, (k % 2) * T:(k % 2 + 1) * T], ACT.Identity, scale=scale[:, k:k + 1],
                                      bias=0.0 if shift is None else shift[:, k:k + 1])

            act.wait_ge(c_turned, 1)
            act.activation(silu_c, ps[:, 5, 0:KD], ACT.Silu).then_inc(silu_c_ready, 1)
            norm(0, SELF, scale0, shift0)
            for u in range(8):
                bank = unit_of("a_f", u)
                sl = slice(2 * u, 2 * u + 2)
                act.activation(fz_b[:, sl, :], bank.rearrange("p (h t) -> p h t", h=2), ACT.Sigmoid)\
                    .then_inc(st("sig_ready"), 1)
                act.activation(k_in0[:, sl, :], bank.rearrange("p (h t) -> p h t", h=2), ACT.Sigmoid, scale=-1.0)\
                    .then_inc(unit_free["a"], 1)
            act.wait_ge(cols_ready, 2)
            link(act.activation(lb, lb_tmp, ACT.Sigmoid))
            link(act.activation(one_m_lb, lb_tmp, ACT.Sigmoid, scale=-1.0))
            act.wait_ge(st("sig_ready"), 8)
            ln_exp_tables()

            def logs(g):
                for h in range(4 * g, 4 * g + 4):
                    act.activation(fz_b[:, h, :], fz_b[:, h, :], ACT.Ln, scale=one_m_lb[:, h:h + 1],
                                   bias=lb[:, h:h + 1]).then_inc(st("ln_ready"), 1)

            def exps(g):
                sl = slice(4 * g, 4 * g + 4)
                act.wait_ge(st("scan_ready"), g + 1)
                act.activation(q_dec[:, sl, :], fz_b[:, sl, :], ACT.Exp).then_inc(st("exp_ready"), 1)
                act.activation(k_in[:, sl, :], fz_b[:, sl, :], ACT.Exp, scale=-1.0).then_inc(st("exp_ready"), 1)
                act.wait_ge(st("spread_ready"), g + 1)
                act.activation(k_st[:, sl, :], k_st[:, sl, :], ACT.Exp).then_inc(st("spread_exp"), 1)

            logs(0)
            for g in range(4):
                e = unit_half[FIRST["a_i"] + 2 * g + 1]
                advance(e + 2)
                if g < 3:
                    logs(g + 1)
                advance(e + 4)
                for u in (2 * g, 2 * g + 1):
                    bank = unit_of("a_i", u)
                    act.activation(v_rows[u % 2][:, (u // 2) * HALF:(u // 2 + 1) * HALF], bank, ACT.Copy)\
                        .then_inc(unit_free["a"], 1)
                if g >= 1:
                    exps(g - 1)
            for u in range(8):
                advance(unit_half[FIRST["a_q"] + u] + NSPLIT - 1)
                if u == 1:
                    exps(3)
            for u in range(8):
                bank = unit_of("a_g", u)
                if u == 0:
                    act.wait_ge(st("kin_ready"), 2 * HA)
                act.activation(silu_g[:, 2 * u:2 * u + 2, :], bank.rearrange("p (h t) -> p h t", h=2), ACT.Silu)\
                    .then_inc(unit_free["a"], 1)
            ln_exp_tables()
            advance(unit_half[FIRST["a_g"] + 7] + NSPLIT)

            def o_scale(h):
                act.wait_ge(st("ossq_ready"), h + 1)
                if h >= 2:
                    act.wait_ge(st("o_used"), h - 1)
                link(act.activation(o_r[:, h % 2, :], ps[:, 2 + h % 2, T:2 * T], ACT.Ln,
                                    scale=1.0 / P, bias=eps_t))
                act.activation(o_r[:, h % 2, :], o_r[:, h % 2, :], ACT.Exp, scale=-0.5).then_inc(st("orstd_ready"), 1)

            for i in range(HA + 4):
                if i < HA:
                    act.wait_ge(st("kst_turned"), i + 1)
                    if i >= 2:
                        act.wait_ge(st("state_ready"), i - 1)
                    act.activation(kst_sb[:, i % 2, :, :], ps[:, 6 + i % 2, 0:T].rearrange(
                        "p (t k) -> p t k", t=2), ACT.Copy).then_inc(st("kst_copied"), 1)
                if 2 <= i < HA + 2:
                    h = i - 2
                    act.wait_ge(st("o_ready"), h + 1)
                    if h >= 2:
                        act.wait_ge(st("ossq_ready"), h - 1)
                    act.activation(o_sq[:, h % 2, :], ps[:, 2 + h % 2, 0:T], ACT.Square).then_inc(st("osq_ready"), 1)
                if 3 <= i < HA + 3:
                    o_scale(i - 3)

            advance(first_half[AT[("kv", 0)]] + 1)

            norm(1, KV, scale_kv, shift_kv)
            for u in range(4):
                act.wait_ge(h_used, u + 1)
                scaled(h_self[:, 2 * u, :], 1, 2 * u, scale1, shift1)
                scaled(h_self[:, 2 * u + 1, :], 1, 2 * u + 1, scale1, shift1).then_inc(unit_free["a"], 1)
            count = [0]

            normed_units = [("k", i) for i in range(8)] + [("q", i) for i in range(8)] + [
                ("ev_k", 0), ("ev_q", 0), ("ev_q", 1)]

            def square_unit(stage, i):
                n = count[0]
                bank = unit_of(stage, i)
                if n >= 2:
                    act.wait_ge(st("hssq_ready"), n - 1)
                act.activation(h_sq[:, n % 2, :], bank, ACT.Square).then_inc(st("hsq_ready"), 1)
                count[0] += 1

            def scale_unit(n, size):
                act.wait_ge(st("hssq_ready"), n + 1)
                if n >= 2:
                    wait_read(act, *normed_units[n - 2])
                link(act.activation(h_r[:, n % 2, :], ps[:, 4 + n % 2, :], ACT.Ln, scale=1.0 / size, bias=eps_t))
                act.activation(h_r[:, n % 2, :], h_r[:, n % 2, :], ACT.Exp, scale=-0.5).then_inc(st("hrstd_ready"), 1)

            for i in range(8):
                square_unit("k", i)
                if i >= 1:
                    scale_unit(i - 1, P)
            for u in range(8):
                bank = unit_of("v", u)
                act.activation(v2_rows[:, u % 2, (u // 2) * HALF:(u // 2 + 1) * HALF], bank, ACT.Copy)\
                    .then_inc(unit_free["a"], 1)
                if u == 1:
                    scale_unit(7, P)
            bank = unit_of("forget", 0)
            act.wait_ge(fb_in, 16)
            act.wait_ge(st("f_min"), 1)
            link(act.activation(f_a, bank[0:HA, 0:T], ACT.Abs, bias=forget_b))
            link(act.activation(f_a, f_a, ACT.Exp, scale=-1.0))
            act.activation(f_a, f_a, ACT.Ln, bias=1.0).then_inc(st("f_ln"), 1)
            for i in range(8):
                square_unit("q", i)
                if i >= 1:
                    scale_unit(8 + i - 1, P)
            scale_unit(15, P)
            for u in range(8):
                bank = unit_of("g", u)
                act.activation(silu_g2[:, 2 * u:2 * u + 2, :], bank.rearrange("p (h t) -> p h t", h=2), ACT.Silu)\
                    .then_inc(unit_free["a"], 1)

            def softmax_heads(pre, heads):
                for i in range(heads + 2):
                    if i < heads:
                        act.wait_ge(st(pre + "_max"), i + 1)
                        if i >= 3:
                            act.wait_ge(st(pre + "_turned"), i - 2)
                        for t, q in enumerate((Q0, Q1)):
                            c = 2 * (i % 2) + t
                            ins = act.activation(prob[:, i % 3, q], lg[:, i % 2, q], ACT.Exp,
                                                 bias=row_neg[:, c:c + 1], accum_out=row_sum[:, c:c + 1])
                            if t == 1:
                                ins.then_inc(st(pre + "_exp"), 1)
                    if i >= 2:
                        h = i - 2
                        act.wait_ge(st(pre + "_turned"), h + 1)
                        if h >= 2:
                            act.wait_ge(st(pre + "_o"), h - 1)
                        act.activation(probT[:, h % 2, :], ps[:, 6 + h % 2, 0:S3], ACT.Copy)\
                            .then_inc(st(pre + "_tcopied"), 1)

            ln_exp_tables()
            advance(unit_half[FIRST["g"] + 7] + NSPLIT)
            softmax_heads("fx", HA)
            advance(first_half[AT[("ev_qi", 0)]] + 1)

            norm(2, SELF, col["norm_mix_g_2"][:, 0:8])
            bank = unit_of("ev_i", 0)
            act.activation(evqi, bank.rearrange("p (c t) -> p c t", c=2), ACT.Copy).then_inc(unit_free["a"], 1)
            bank = unit_of("ev_i", 1)
            act.activation(evki, bank[:, 0:T], ACT.Copy)
            act.activation(w_idx, bank[:, T:T + 8], ACT.Copy, scale=float((HIDX * HD2) ** -0.5))\
                .then_inc(unit_free["a"], 1)
            for h in range(HIDX):
                act.wait_ge(st("ev_rel"), h + 1)
                if h >= 2:
                    act.wait_ge(st("ev_score_used"), h - 1)
                act.activation(relu_s[:, h % 2, :], ps[:, 4 + h, 0:S3], ACT.Relu).then_inc(st("ev_relu"), 1)
            square_unit("ev_k", 0)
            bank = unit_of("ev_v", 0)
            act.activation(evv, bank[:, 0:T].rearrange("p (t d) -> p t d", t=2), ACT.Copy).then_inc(unit_free["a"], 1)
            scale_unit(16, HD2)
            square_unit("ev_q", 0)
            square_unit("ev_q", 1)
            scale_unit(17, HD2)
            for u in range(2):
                bank = unit_of("ev_u", u)
                act.activation(u_pad[:, 2 * u:2 * u + 2, PAD:], bank.rearrange("p (g t) -> p g t", g=2), ACT.Copy)\
                    .then_inc(unit_free["a"], 1)
                if u == 0:
                    scale_unit(18, HD2)
            advance(unit_half[FIRST["ev_u"] + 1] + NSPLIT)
            softmax_heads("ds", HE)
            advance(first_half[AT[("w1", 0, 0)]] + 1)

            def feed_forward(layer):
                for c in range(FC):
                    bank = unit_of(f"up{layer}", c)
                    if c >= 2:
                        wait_read(act, f"up{layer}", c - 2)
                    act.activation(silu_a[:, c % 2, :], bank[:, 0:T], ACT.Silu).then_inc(st("up_silu"), 1)

            norm(3, SELF, col["norm_ffn_g_2"][:, 0:8])
            feed_forward(0)
            advance(first_half[AT[("od_in", 0)]] + 1)

            norm(4, SELF, col["norm_mix_g_2"][:, 8:16])
            for u in range(4):
                bank = unit_of("od_q", u)
                act.activation(odq[:, 2 * u:2 * u + 2, :], bank.rearrange("p (h t) -> p h t", h=2), ACT.Copy,
                               scale=float(HD2 ** -0.5)).then_inc(unit_free["a"], 1)
            for u in (0, 2):
                bank = unit_of("od_v", u)
                act.activation(odv[:, 0, (u // 2) * HALF:(u // 2 + 1) * HALF], bank, ACT.Copy)\
                    .then_inc(unit_free["a"], 1)
            advance(unit_half[FIRST["od_v"] + 3] + NSPLIT)
            for i in range(HO + 2):
                if i < HO:
                    act.wait_ge(st("sb_z"), i + 1)
                    if i >= 2:
                        act.wait_ge(st("sb_soft"), i - 1)
                    link(act.activation(sb_ln_t(i), ps[:, 4 + i % 4, 0:S3], ACT.Abs))
                    link(act.activation(sb_ln_t(i), sb_ln_t(i), ACT.Exp, scale=-1.0))
                    act.activation(sb_ln_t(i), sb_ln_t(i), ACT.Ln, bias=1.0).then_inc(st("sb_ln"), 1)
                if i >= 2:
                    h = i - 2
                    act.wait_ge(st("sb_log"), h + 1)
                    if h >= 3:
                        act.wait_ge(st("sb_o"), h - 2)
                    act.activation(sb_prob(h), ps[:, 4 + h % 4, 0:S3], ACT.Exp).then_inc(st("sb_exp"), 1)
            advance(first_half[AT[("w1", 1, 0)]] + 1)
            norm(5, SELF, col["norm_ffn_g_2"][:, 8:16])
            feed_forward(1)
            advance(len(HALVES))

        @block.vector
        def _(dve):
            def link(ins):
                then("dve", dve, ins)

            split, piece_at = [0], [8]

            def advance(upto):
                while split[0] <= min(upto, len(HALVES) - 1):
                    s = split[0]
                    while piece_at[0] < HALVES[s][0]:
                        piece = PIECES[piece_at[0]]
                        piece_at[0] += 1
                        if piece[0] == "mod":
                            mod_sum(piece[1], piece[2])
                            if piece[2] == 1 and piece[1] not in (4, 14):
                                mod_take(piece[1] - 1)
                    dve.wait_ge(hi_done, s + 1)
                    dve.tensor_tensor(half_view(w_lo, s), HALVES[s][2], half_view(w_hi, s).bitcast(F32),
                                      ALU.subtract).then_inc(lo_done, 1)
                    split[0] += 1

            def unit_of(stage, i):
                u = FIRST[stage] + i
                advance(unit_half[u] + NSPLIT - 1)
                dve.wait_ge(unit_ready, u + 1)
                return unit_bank(u)

            def normalize(j):
                for t in range(NT):
                    dve.wait_ge(rstd_done, 2 * j + t + 1)
                    for n in range(2):
                        sl = slice(n * HALF, (n + 1) * HALF)
                        dve.tensor_scalar(xn[:, t, sl], x[:, t, sl], rstd[:, t:t + 1], None, ALU.mult).then_inc(xn_done, 1)

            def norm(j, base, scale, shift):
                if j > 0:
                    normalize(j)
                for u in range(4):
                    b = u % 2
                    dve.wait_ge(h_hi, 4 * j + u + 1)
                    bank = unit_bank(FIRST[f"norm{j}"] + u)
                    lo_n = 4 * j + u + 1
                    if shift is None:
                        for kk in range(2):
                            k = 2 * u + kk
                            ins = dve.scalar_tensor_tensor(
                                out=act_lo[:, base + k, :], in0=bank[:, kk * T:(kk + 1) * T], scalar=scale[:, k:k + 1],
                                in1=act_hi[:, base + k, :].bitcast(F32), op0=ALU.mult, op1=ALU.subtract)
                        ins.then_inc(unit_free["v"], 1)
                        continue
                    for kk in range(2):
                        k = 2 * u + kk
                        ins = dve.tensor_scalar(h_full[:, b, kk * T:(kk + 1) * T], bank[:, kk * T:(kk + 1) * T],
                                                scale[:, k:k + 1], shift[:, k:k + 1], ALU.mult, ALU.add)
                    freed = unit_free["v"] if j == 0 else h_used
                    ins.then_inc(freed, 1)
                    dve.wait_ge(freed, u + 1)
                    dve.tensor_tensor(act_lo[:, base + 2 * u:base + 2 * u + 2, :],
                                      h_full[:, b, :].rearrange("p (k t) -> p k t", k=2),
                                      act_hi[:, base + 2 * u:base + 2 * u + 2, :].bitcast(F32),
                                      ALU.subtract).then_inc(h_lo, 1)
                    dve.wait_ge(h_lo, lo_n)

            def add_y(j, gated_):
                for t in range(NT):
                    for n in range(2):
                        sl = slice(n * HALF, (n + 1) * HALF)
                        dve.wait_ge(y_ready, 4 * j + 2 * t + n + 1)
                        src = y_bank(t, n)
                        if gated_:
                            link(dve.tensor_tensor(acc[:, n, :], src, gate[:, sl], ALU.mult))
                            src = acc[:, n, :]
                        dve.tensor_tensor(x[:, t, sl], x[:, t, sl], src, ALU.add).then_inc(x_done, 1)

            mb = col["mod_b"]
            dest = {0: (shift0, 0, mb, 0, None), 1: (shift0, 4, mb, 4, None),
                    2: (scale0, 0, mb, 8, col["norm_g"][:, 0:4]), 3: (scale0, 4, mb, 12, col["norm_g"][:, 4:8]),
                    6: (shift1, 0, mb, 24, None), 7: (shift1, 4, mb, 28, None),
                    8: (scale1, 0, mb, 32, col["norm_g"][:, 8:12]), 9: (scale1, 4, mb, 36, col["norm_g"][:, 12:16]),
                    10: (shift_kv, 0, col["kv_mod_b"], 0, None), 11: (shift_kv, 4, col["kv_mod_b"], 4, None),
                    12: (scale_kv, 0, col["kv_mod_b"], 8, col["kv_norm_g"][:, 0:4]),
                    13: (scale_kv, 4, col["kv_mod_b"], 12, col["kv_norm_g"][:, 4:8])}

            def mod_sum(m, q):
                n = AT[("mod", m, q)]
                wait_loaded(dve, n)
                if m >= 2 and q == 0:
                    dve.wait_ge(mod_cols, m - 1)
                w = by_k(slot(n), 4)
                for k in range(4):
                    c = silu_c[:, 4 * q + k:4 * q + k + 1]
                    if q == 0 and k == 0:
                        ins = dve.tensor_scalar(acc[:, m % 2, :], w[:, 0, :], c, None, ALU.mult)
                    else:
                        ins = dve.scalar_tensor_tensor(out=acc[:, m % 2, :], in0=w[:, k, :], scalar=c,
                                                       in1=acc[:, m % 2, :], op0=ALU.mult, op1=ALU.add)
                    if k < 3:
                        link(ins)
                ins.then_inc(mod_summed, 1)
                dve.wait_ge(mod_summed, 2 * m + q + 1)

            def mod_take(m):
                dve.wait_ge(mod_cols, m + 1)
                bank = ps[:, 6 + m % 2, :]
                if m in (4, 5, 14, 15):
                    dve.wait_ge(gate_b_in, 16 if m < 14 else 32)
                    sl = slice((m % 2) * HALF, (m % 2 + 1) * HALF)
                    dve.tensor_tensor(gate[:, sl], gate[:, sl], bank, ALU.add).then_inc(mod_read, 1)
                    return
                dst, c, bias, b, gain = dest[m]
                if gain is None:
                    dve.tensor_tensor(dst[:, c:c + 4], bank[:, 0:4], bias[:, b:b + 4], ALU.add).then_inc(mod_read, 1)
                else:
                    link(dve.scalar_tensor_tensor(out=mod_tmp, in0=bank[:, 0:4], scalar=1.0, in1=bias[:, b:b + 4],
                                                  op0=ALU.add, op1=ALU.add))
                    dve.tensor_tensor(dst[:, c:c + 4], mod_tmp, gain, ALU.mult).then_inc(mod_read, 1)
                dve.wait_ge(mod_read, m + 1)

            dve.memset(eps_t, EPS)
            dve.wait_ge(silu_c_ready, 1)
            mod_sum(0, 0)
            mod_sum(0, 1)
            dve.wait_ge(rows_turned, 1)
            dve.tensor_copy(cols[:, 0:ROWS_A], ps[:, 4, 0:ROWS_A]).then_inc(cols_ready, 1)
            dve.wait_ge(cols_ready, 1)
            for m in range(1, 4):
                mod_sum(m, 0)
                mod_sum(m, 1)
                if m == 3:
                    normalize(0)
                mod_take(m - 1)
            mod_take(3)
            norm(0, SELF, scale0, shift0)

            link(dve.memset(att_sb, 0.0))
            for u in range(8):
                advance(unit_half[FIRST["a_f"] + u] + NSPLIT - 1)
                if u == 5:
                    dve.wait_ge(rows_turned, 2)
                    link(dve.tensor_copy(cols[:, P:2 * P], ps[:, 4, P:2 * P]))
                    dve.tensor_tensor(lb_tmp, col["a_lb_logits"][:, 0:16], col["a_lb_logits"][:, 16:32], ALU.subtract)
                    dve.tensor_scalar(q_gain, col["b_q_norm_g"], float(P ** -0.5), None, ALU.mult)
                    dve.tensor_scalar(ev_q_gain, ev_gain[:, 0:1], float(HD2 ** -0.5), None, ALU.mult)\
                        .then_inc(cols_ready, 1)
            dve.wait_ge(masks_in, 32)

            def scans(g):
                sl = slice(4 * g, 4 * g + 4)
                for h in range(4 * g, 4 * g + 4):
                    dve.wait_ge(st("ln_ready"), h + 1)
                    ins = dve.tensor_tensor_scan(fz_b[:, h, :], chunk_go, fz_b[:, h, :], 0.0, ALU.mult, ALU.add)
                ins.then_inc(st("scan_ready"), 1)
                dve.wait_ge(st("scan_ready"), g + 1)
                part = fz_b[:, sl, :].rearrange("p h (n c) -> p (h n) c", c=CHUNK)
                dst = k_st[:, sl, :].rearrange("p h (n c) -> p (h n) c", c=CHUNK)
                dve.tensor_tensor(dst, part[:, :, CHUNK - 1:CHUNK].to_broadcast([P, 4 * NC, CHUNK]), part,
                                  ALU.subtract).then_inc(st("spread_ready"), 1)

            def decayed_keys(g):
                sl = slice(4 * g, 4 * g + 4)
                dve.wait_ge(st("exp_ready"), 2 * g + 2)
                dve.tensor_copy(dl[:, sl, :], q_dec[:, sl, CHUNK - 1::CHUNK])
                dve.wait_ge(st("spread_exp"), g + 1)
                for h in range(4 * g, 4 * g + 4):
                    for k in (k_in, k_st):
                        dve.scalar_tensor_tensor(out=k[:, h, :], in0=k_in0[:, h, :], scalar=one_m_lb[:, h:h + 1],
                                                 in1=k[:, h, :], op0=ALU.mult, op1=ALU.mult)\
                            .then_inc(st("kin_ready"), 1)

            scans(0)
            for g in range(4):
                e = unit_half[FIRST["a_i"] + 2 * g + 1]
                advance(e + 2)
                if g < 3:
                    scans(g + 1)
                advance(e + 4)
                if g >= 2:
                    decayed_keys(g - 2)
            for u in range(8):
                if u in (3, 5):
                    decayed_keys((u + 1) // 2)
                bank = unit_of("a_q", u)
                sl = slice(2 * u, 2 * u + 2)
                dve.tensor_tensor(q_dec[:, sl, :], bank.rearrange("p (h t) -> p h t", h=2), q_dec[:, sl, :], ALU.mult)\
                    .then_inc(unit_free["v"], 1)
            advance(unit_half[FIRST["a_g"] + 7] + NSPLIT - 1)
            mod_take(13)
            dve.wait_ge(unit_free["a"], before("a", FIRST["a_g"] + 7))

            def o_out(h):
                dve.wait_ge(st("orstd_ready"), h + 1)
                if h >= 1:
                    dve.wait_ge(st("ot_ready"), h)
                dve.scalar_tensor_tensor(out=o_tmp, in0=ps[:, 2 + h % 2, 0:T], scalar=col["a_onorm_g"][:, h:h + 1],
                                         in1=o_r[:, h % 2, :], op0=ALU.mult, op1=ALU.mult).then_inc(st("o_used"), 1)
                dve.wait_ge(st("o_used"), h + 1)
                if h >= 2:
                    dve.wait_ge(st("ot_split"), h - 1)
                dve.tensor_tensor(o_full[:, h % 2, :], o_tmp, silu_g[:, h, :], ALU.mult).then_inc(st("ot_ready"), 1)

            for i in range(HA + 4):
                if i >= 4:
                    o_out(i - 4)
                if i < HA:
                    dve.wait_ge(st("att_ready"), i + 1)
                    if i >= 2:
                        dve.wait_ge(st("o_ready"), i - 1)
                    dve.copy_predicated(att_sb[:, i % 2, :, :], att_mask[:, :, :],
                                        ps[:, 4 + i % 2, 0:T].rearrange("p (t c) -> p t c", t=2))\
                        .then_inc(st("att_masked"), 1)
                if 1 <= i < HA + 1:
                    h = i - 1
                    dve.wait_ge(st("state_ready"), h + 1)
                    if h >= 2:
                        dve.wait_ge(st("o_ready"), h - 1)
                    link(dve.tensor_copy(state[:, h % 2, 0, :], ps[:, h % 2, 0:P]))
                    for n in range(1, NC - 1):
                        ins = dve.scalar_tensor_tensor(out=state[:, h % 2, n, :], in0=state[:, h % 2, n - 1, :],
                                                       scalar=dl[:, h, n:n + 1], in1=ps[:, h % 2, n * P:(n + 1) * P],
                                                       op0=ALU.mult, op1=ALU.add)
                        if n < NC - 2:
                            link(ins)
                    ins.then_inc(st("state_saved"), 1)
            advance(first_half[AT[("kv", 0)]] + 1)
            add_y(0, True)

            norm(1, KV, scale_kv, shift_kv)

            def normed(stage, i, n, dst, gain):
                bank = unit_of(stage, i)
                if n < 7 or 8 <= n < 15:
                    advance(unit_half[FIRST[stage] + i] + NSPLIT + 1)
                if n == 7:
                    advance(unit_half[FIRST["v"] + 1])
                dve.wait_ge(st("hrstd_ready"), n + 1)
                dve.scalar_tensor_tensor(out=dst, in0=bank.rearrange("p (h t) -> p h t", h=2), scalar=gain,
                                         in1=h_r[:, n % 2, :].rearrange("p (h t) -> p h t", h=2),
                                         op0=ALU.mult, op1=ALU.mult).then_inc(unit_free["v"], 1)

            for i in range(8):
                normed("k", i, i, kN[:, 2 * i:2 * i + 2, :], col["k_norm_g"])
            bank = unit_of("forget", 0)
            dve.wait_ge(fb_in, 16)
            dve.tensor_scalar(f_b, bank[0:HA, 0:T], forget_b, 0.0, ALU.add, ALU.min).then_inc(st("f_min"), 1)
            dve.wait_ge(st("f_ln"), 1)
            link(dve.tensor_tensor(f_b, f_a, f_b, ALU.subtract))
            dve.nop().then_inc(unit_free["v"], 1)
            dve.tensor_tensor_scan(neg_f, f_b, f_b, 0.0, ALU.add, ALU.max).then_inc(st("nf_ready"), 1)
            for i in range(8):
                normed("q", i, 8 + i, qN[:, 2 * i:2 * i + 2, :], q_gain)
            advance(unit_half[FIRST["g"] + 7])
            mod_take(15)
            dve.wait_ge(unit_free["a"], before("a", FIRST["g"] + 7))

            def softmax_heads(pre, heads, bias, output):
                for i in range(heads + 4):
                    if i < heads:
                        dve.wait_ge(st(pre + "_logits"), i + 1)
                        if i >= 2:
                            dve.wait_ge(st(pre + "_exp"), i - 1)
                        c = 2 * (i % 2)
                        for t, q in enumerate((Q0, Q1)):
                            ins = dve.tensor_tensor_reduce(out=lg[:, i % 2, q], in0=ps[:, 4 + i % 2, q], in1=bias[:, q],
                                                           scale=1.0, scalar=LOW, op0=ALU.add, op1=ALU.max,
                                                           accum_out=row_max[:, c + t:c + t + 1])
                        link(ins)
                        dve.tensor_scalar(row_neg[:, c:c + 2], row_max[:, c:c + 2], -1.0, None, ALU.mult)\
                            .then_inc(st(pre + "_max"), 1)
                    if 1 <= i < heads + 1:
                        h = i - 1
                        c = 2 * (h % 2)
                        dve.wait_ge(st(pre + "_exp"), h + 1)
                        link(dve.reciprocal(row_inv[:, c:c + 2], row_sum[:, c:c + 2]))
                        for t, q in enumerate((Q0, Q1)):
                            ins = dve.tensor_scalar(prob[:, h % 3, q], prob[:, h % 3, q], row_inv[:, c + t:c + t + 1],
                                                    None, ALU.mult)
                        ins.then_inc(st(pre + "_prob"), 1)
                    if i >= 4:
                        output(i - 4)

            def fox_out(h):
                dve.wait_ge(st("fx_o"), h + 1)
                if h >= 2:
                    dve.wait_ge(st("fx_split"), h - 1)
                dve.tensor_tensor(o_full[:, h % 2, :], ps[:, h % 2, 0:T], silu_g2[:, h, :], ALU.mult)\
                    .then_inc(st("fx_out"), 1)

            softmax_heads("fx", HA, causal, fox_out)
            advance(first_half[AT[("ev_qi", 0)]] + 1)
            add_y(1, True)

            norm(2, SELF, col["norm_mix_g_2"][:, 0:8], None)
            e = unit_half[FIRST["ev_i"] + 1] + NSPLIT
            advance(e - 1)
            wait_read(dve, "ev_i", 1)
            for h in range(HIDX):
                dve.wait_ge(st("ev_relu"), h + 1)
                for t, q in enumerate((Q0, Q1)):
                    wcol = w_idx[:, 4 * t + h:4 * t + h + 1]
                    if h == 0:
                        ins = dve.tensor_scalar(score[:, q], relu_s[:, h % 2, q], wcol, None, ALU.mult)
                    else:
                        ins = dve.scalar_tensor_tensor(out=score[:, q], in0=relu_s[:, h % 2, q], scalar=wcol,
                                                       in1=score[:, q], op0=ALU.mult, op1=ALU.add)
                ins.then_inc(st("ev_score_used"), 1)
                dve.wait_ge(st("ev_score_used"), h + 1)
            link(dve.tensor_tensor(score, score, causal, ALU.add))

            def choose(q, n, ahead):
                src = score[:, q]
                for r in range(TOPK // 8):
                    if r % 4 == 2:
                        advance(ahead + r // 4)
                    link(dve.max(top8, src))
                    if r < TOPK // 8 - 1:
                        link(dve.match_replace(out=cut[:, 0:n], in_to_replace=top8, in_values=src, imm_value=LOW))
                        src = cut[:, 0:n]
                least = top8[:, 7:8]
                dve.tensor_scalar(sel_eq[:, 0:n], score[:, q], least, None, ALU.is_equal)
                link(dve.tensor_scalar(sel_gt[:, 0:n], score[:, q], least, None, ALU.is_gt, ALU.add, accum_out=cnt))
                link(dve.tensor_scalar(rest, cnt, -1.0, float(TOPK), ALU.mult, ALU.add))
                link(dve.tensor_tensor_scan(sel_pre[:, 0:n], sel_eq[:, 0:n], sel_eq[:, 0:n], 0.0, ALU.add, ALU.max))
                link(dve.scalar_tensor_tensor(out=sel_eq[:, 0:n], in0=sel_pre[:, 0:n], scalar=rest, in1=sel_eq[:, 0:n],
                                              op0=ALU.is_le, op1=ALU.mult))
                link(dve.tensor_tensor(sel_gt[:, 0:n], sel_gt[:, 0:n], sel_eq[:, 0:n], ALU.add))
                link(dve.tensor_scalar(sel_gt[:, 0:n], sel_gt[:, 0:n], -FAR, FAR, ALU.mult, ALU.add))
                link(dve.tensor_tensor(ev_bias_t[:, q], sel_gt[:, 0:n], causal[:, q], ALU.add))

            choose(Q1, T, e)
            normed("ev_k", 0, 16, evk, ev_gain[:, 1:2])
            normed("ev_q", 0, 17, evq[:, 0:2, :], ev_q_gain)
            normed("ev_q", 1, 18, evq[:, 2:4, :], ev_q_gain)
            choose(Q0, P, unit_half[FIRST["ev_q"] + 1] + NSPLIT)

            def ds_out(h):
                if h % 2 == 1:
                    dve.wait_ge(st("ds_o"), h + 1)
                    if h >= 4:
                        dve.wait_ge(st("ds_split"), h // 2 - 1)
                    dve.tensor_copy(o_full[:, (h // 2) % 2, :], ps[:, (h // 2) % 2, 0:T]).then_inc(st("ds_out"), 1)

            advance(unit_half[FIRST["ev_u"] + 1] + NSPLIT)
            softmax_heads("ds", HE, ev_bias_t, ds_out)
            for pair in range(2):
                bank = unit_of("ev_pool", pair)
                for j in range(2):
                    g = 2 * pair + j
                    link(dve.tensor_scalar(pooled[:, g, :], bank[:, j * T:(j + 1) * T],
                                           col["ev_pool_scale_2"][:, g:g + 1], None, ALU.mult))
                c = slice(OUT2 + 4 + 2 * pair, OUT2 + 6 + 2 * pair)
                full = pooled[:, 2 * pair:2 * pair + 2, :]
                link(dve.tensor_copy(act_hi[:, c, :], full))
                dve.tensor_tensor(act_lo[:, c, :], full, act_hi[:, c, :].bitcast(F32), ALU.subtract)\
                    .then_inc(unit_free["v"], 1)
            advance(first_half[AT[("w1", 0, 0)]] + 1)
            add_y(2, False)

            def feed_forward(layer):
                for c in range(FC):
                    bank = unit_of(f"up{layer}", c)
                    dve.wait_ge(st("up_silu"), layer * FC + c + 1)
                    g = g_full[:, c % 2, :]
                    dve.tensor_tensor(g, bank[:, T:2 * T], silu_a[:, c % 2, :], ALU.mult).then_inc(st("g_full"), 1)
                    dve.wait_ge(st("g_full"), layer * FC + c + 1)
                    if c >= 8:
                        dve.wait_ge(*half_use[down_half[layer, c - 8]])
                    dve.tensor_copy(act_hi[:, 8 + c % 8, :], g).then_inc(st("g_hi"), 1)
                    dve.wait_ge(st("g_hi"), layer * FC + c + 1)
                    dve.tensor_tensor(act_lo[:, 8 + c % 8, :], g, act_hi[:, 8 + c % 8, :].bitcast(F32), ALU.subtract)\
                        .then_inc(unit_free["v"], 1)

            norm(3, SELF, col["norm_ffn_g_2"][:, 0:8], None)
            feed_forward(0)
            advance(first_half[AT[("od_in", 0)]] + 1)
            add_y(3, False)

            norm(4, SELF, col["norm_mix_g_2"][:, 8:16], None)
            for u in range(4):
                bank = unit_of("od_k", u)
                dve.tensor_copy(odk[:, 2 * u:2 * u + 2, :], bank.rearrange("p (h t) -> p h t", h=2))\
                    .then_inc(unit_free["v"], 1)
            for u in (1, 3):
                bank = unit_of("od_v", u)
                dve.tensor_copy(odv[:, 1, (u // 2) * HALF:(u // 2 + 1) * HALF], bank).then_inc(unit_free["v"], 1)
            advance(unit_half[FIRST["od_v"] + 3] + NSPLIT)
            for i in range(HO + 5):
                if i < HO:
                    dve.wait_ge(st("sb_ln"), i + 1)
                    if i >= 3:
                        dve.wait_ge(st("sb_log"), i - 2)
                    dve.scalar_tensor_tensor(out=sb_brk(i), in0=ps[:, 4 + i % 4, 0:S3], scalar=0.0, in1=sb_ln_t(i),
                                             op0=ALU.max, op1=ALU.add).then_inc(st("sb_soft"), 1)
                if i >= 6 and i % 2 == 0:
                    h = i - 5
                    dve.wait_ge(st("sb_o"), h + 1)
                    if h >= 4:
                        dve.wait_ge(st("sb_split"), h // 2 - 1)
                    dve.tensor_copy(o_full[:, (h // 2) % 2, :], ps[:, (h // 2) % 2, 0:T]).then_inc(st("sb_out"), 1)
            advance(first_half[AT[("w1", 1, 0)]] + 1)
            add_y(4, False)
            norm(5, SELF, col["norm_ffn_g_2"][:, 8:16], None)
            feed_forward(1)
            advance(len(HALVES))
            add_y(5, False)


def shape_constants():
    p = np.arange(P)
    ident = np.eye(P)
    ones = np.ones((P, P))
    ones64 = (p[:, None] // HD2 == p[None, :] // HD2).astype(float)
    neg_after = -(p[:, None] >= p[None, :]).astype(float)
    t0 = np.where(p[None, :] <= p[:, None], 0.0, FAR)
    causal = np.concatenate([t0, np.zeros((P, P)), t0], axis=1)
    go = np.broadcast_to((np.arange(T) % CHUNK != 0).astype(float), (P, T))
    count = np.concatenate([1.0 / np.minimum(np.arange(1, 17), w) for w in (2, 4, 8, 16)])
    count = np.broadcast_to(count, (P, 64))
    const = np.concatenate([ident, ones, ones64, neg_after, -ones, causal, go, count], axis=1).astype(np.float32)
    m = ((p[:, None] // CHUNK == p[None, :] // CHUNK) & (p[:, None] <= p[None, :])).astype(np.int32)
    return np.ascontiguousarray(const), np.ascontiguousarray(np.concatenate([m, m], axis=1))


_INS = ["x", "c", "mod_w", "mod_b", "norm_g", "a_w_in", "a_lb_logits", "a_onorm_g", "a_w_out", "kv_mod_w", "kv_mod_b",
        "kv_norm_g", "kv_w", "kv_fb", "k_norm_g", "b_w_in", "b_q_norm_g", "b_w_out", "norm_mix_g_2", "norm_ffn_g_2",
        "ev_w_in_2", "ev_w_out_2", "ev_q_norm_g_2", "ev_k_norm_g_2", "ev_pool_w_2", "ev_pool_scale_2",
        "od_w_qkv_2", "od_w_out_2", "ffn_w1_2", "ffn_w3_2", "ffn_w2_2"]


def kernel(**inputs):
    import concourse.bacc as bacc
    from concourse.bass_utils import run_bass_kernel_spmd

    nc = bacc.Bacc("TRN2", target_bir_lowering=False, num_devices=1)
    arrays, views = {}, {}
    for name in _INS:
        v = np.ascontiguousarray(inputs[name])
        arrays[f"in_{name}"] = v
        views[name] = nc.dram_tensor(f"in_{name}", v.shape, mybir.dt.from_np(v.dtype), kind="ExternalInput").ap()
    const, mask = shape_constants()
    arrays["shape_constants"], arrays["shape_mask"] = const, mask
    c = nc.dram_tensor("shape_constants", const.shape, F32, kind="ExternalInput").ap()
    m = nc.dram_tensor("shape_mask", mask.shape, I32, kind="ExternalInput").ap()
    out = nc.dram_tensor("out", (1, T, D), F32, kind="ExternalOutput").ap()
    build(nc, views, c, m, out)
    r = run_bass_kernel_spmd(nc, [arrays], core_ids=[0])
    return r.results[0]["out"]
```
